# Optimizing a Trainium2 kernel written in Bass

```python
import jax, jax.numpy as jnp
from jax import lax
import numpy as np

D_MODEL = 1024
BATCH = 1
SEQ = 256
DEPTH = 2

N_EVEN = (DEPTH + 1) // 2
N_ODD = DEPTH // 2

CHUNK = 128
SGU_WIDTH = 2 * D_MODEL
SGU_GROUPS = 8
SGU_GROUP_DIM = SGU_WIDTH // SGU_GROUPS
RET_HEADS = 4
RET_DK = D_MODEL // RET_HEADS
RET_DV = 2 * RET_DK
RET_QK = RET_HEADS * RET_DK
RET_V = RET_HEADS * RET_DV
RET_IN = 2 * RET_QK + 2 * RET_V
ROPE_BASE = 10000.0
FFN_DIM = ((8 * D_MODEL // 3 + 127) // 128) * 128
N_EXPERTS = 8
TOP_K = 2
EPS = 1e-6

kernel_name = "hybrid_sgu_retention_moe_adaln"

def rmsnorm(x, g):
    xf = x.astype(jnp.float32)
    xf = xf * lax.rsqrt(jnp.mean(xf * xf, axis=-1, keepdims=True) + EPS)
    return (xf * g.astype(jnp.float32)).astype(x.dtype)

def layernorm(x, g, b):
    xf = x.astype(jnp.float32)
    mu = jnp.mean(xf, axis=-1, keepdims=True)
    var = jnp.mean(jnp.square(xf - mu), axis=-1, keepdims=True)
    y = (xf - mu) * lax.rsqrt(var + EPS) * g.astype(jnp.float32) + b.astype(jnp.float32)
    return y.astype(x.dtype)

def swiglu(h, w_gate_up, w_down):
    gu = h @ w_gate_up
    g, u = jnp.split(gu, 2, axis=-1)
    return (jax.nn.silu(g) * u) @ w_down

def chunked_sgu(h, w_in, ln_g, ln_b, w_s, b_s, w_out):
    bn, s, _ = h.shape
    nc = s // CHUNK
    z = jax.nn.gelu(h @ w_in)
    u, v = jnp.split(z, 2, axis=-1)
    v = layernorm(v, ln_g, ln_b)
    v = v.reshape(bn, nc, CHUNK, SGU_GROUPS, SGU_GROUP_DIM)
    mask = jnp.tril(jnp.ones((CHUNK, CHUNK), dtype=w_s.dtype))
    fv = jnp.einsum('gts,bnsgd->bntgd', w_s * mask, v) + b_s.T[:, :, None]
    y = u * fv.reshape(bn, s, SGU_WIDTH)
    return y @ w_out

def rope(t, positions):
    d = t.shape[-1]
    inv_freq = 1.0 / (ROPE_BASE ** (jnp.arange(0, d, 2, dtype=jnp.float32) / d))
    ang = positions.astype(jnp.float32)[..., None] * inv_freq
    cos = jnp.cos(ang)[:, :, None, :]
    sin = jnp.sin(ang)[:, :, None, :]
    tf = t.astype(jnp.float32)
    t1, t2 = jnp.split(tf, 2, axis=-1)
    return jnp.concatenate([t1 * cos - t2 * sin, t2 * cos + t1 * sin], axis=-1)

def retention(h, w_in, w_out, positions):
    bn, s, _ = h.shape
    nc = s // CHUNK
    proj = h @ w_in
    q, k, v, g = jnp.split(proj, [RET_QK, 2 * RET_QK, 2 * RET_QK + RET_V], axis=-1)
    q = rope(q.reshape(bn, s, RET_HEADS, RET_DK), positions)
    k = rope(k.reshape(bn, s, RET_HEADS, RET_DK), positions) * (RET_DK ** -0.5)
    v = v.reshape(bn, s, RET_HEADS, RET_DV).astype(jnp.float32)

    def to_chunks(t):
        return t.reshape(bn, nc, CHUNK, RET_HEADS, -1).transpose(1, 0, 3, 2, 4)

    qc, kc, vc = to_chunks(q), to_chunks(k), to_chunks(v)
    log_gamma = jnp.log1p(-jnp.exp2(-5.0 - jnp.arange(RET_HEADS, dtype=jnp.float32)))
    idx = jnp.arange(CHUNK, dtype=jnp.float32)
    rel = idx[:, None] - idx[None, :]
    intra = jnp.where(rel >= 0, jnp.exp(log_gamma[:, None, None] * jnp.maximum(rel, 0.0)), 0.0)
    xi = jnp.exp(log_gamma[:, None] * (idx + 1.0))[None, :, :, None]
    zeta = jnp.exp(log_gamma[:, None] * (CHUNK - 1.0 - idx))[None, :, :, None]
    chunk_decay = jnp.exp(log_gamma * CHUNK)[None, :, None, None]

    def step(state, qkv):
        qi, ki, vi = qkv
        scores = jnp.einsum('bhtd,bhsd->bhts', qi, ki) * intra
        o = (jnp.einsum('bhts,bhsv->bhtv', scores, vi)
             + jnp.einsum('bhtd,bhdv->bhtv', qi, state) * xi)
        state = state * chunk_decay + jnp.einsum('bhsd,bhsv->bhdv', ki, vi * zeta)
        return state, o

    state0 = jnp.zeros((bn, RET_HEADS, RET_DK, RET_DV), jnp.float32)
    _, o = lax.scan(step, state0, (qc, kc, vc))
    o = o.transpose(1, 0, 3, 2, 4).reshape(bn, s, RET_HEADS, RET_DV)
    o = o * lax.rsqrt(jnp.mean(o * o, axis=-1, keepdims=True) + EPS)
    o = o.reshape(bn, s, RET_V).astype(h.dtype) * jax.nn.silu(g)
    return o @ w_out

def moe_swiglu(h, w_router, b_router, w_gate_up, w_down):
    bn, s, dm = h.shape
    t = h.reshape(-1, dm)
    logits = (t @ w_router).astype(jnp.float32) + b_router.astype(jnp.float32)
    top_v, top_i = lax.top_k(logits, TOP_K)
    wts = jax.nn.softmax(top_v, axis=-1)
    gates = jnp.sum(jax.nn.one_hot(top_i, N_EXPERTS, dtype=jnp.float32) * wts[..., None], axis=1)
    gates = gates.astype(h.dtype)
    y = jnp.zeros_like(t)
    for e in range(N_EXPERTS):
        y = y + gates[:, e:e + 1] * swiglu(t, w_gate_up[e], w_down[e])
    return y.reshape(bn, s, dm)

def setup_inputs(seed: int = 0) -> dict:
    key = jax.random.key(seed)
    ks = jax.random.split(key, 24)

    def nrm(k, shape, std):
        return jax.random.normal(k, shape, jnp.float32) * std

    D = D_MODEL
    x = nrm(ks[0], (BATCH, SEQ, D), 1.0)
    c = nrm(ks[1], (BATCH, D), 1.0)
    offs = jax.random.randint(ks[2], (BATCH, 1), 0, 1024, dtype=jnp.int32)
    positions = jnp.arange(SEQ, dtype=jnp.int32)[None, :] + offs
    return {
        "x": x,
        "c": c,
        "positions": positions,
        "ada_w": nrm(ks[3], (DEPTH, D, 6 * D), 0.5 * D ** -0.5),
        "ada_b": nrm(ks[4], (DEPTH, 6 * D), 0.02),
        "mix_norm_g": 1.0 + nrm(ks[5], (DEPTH, D), 0.02),
        "ffn_norm_g": 1.0 + nrm(ks[6], (DEPTH, D), 0.02),
        "sgu_w_in": nrm(ks[7], (N_EVEN, D, 2 * SGU_WIDTH), D ** -0.5),
        "sgu_ln_g": 1.0 + nrm(ks[8], (N_EVEN, SGU_WIDTH), 0.02),
        "sgu_ln_b": nrm(ks[9], (N_EVEN, SGU_WIDTH), 0.02),
        "sgu_w_s": nrm(ks[10], (N_EVEN, SGU_GROUPS, CHUNK, CHUNK), 0.5 * CHUNK ** -0.5),
        "sgu_b_s": 1.0 + nrm(ks[11], (N_EVEN, SGU_GROUPS, CHUNK), 0.1),
        "sgu_w_out": nrm(ks[12], (N_EVEN, SGU_WIDTH, D), SGU_WIDTH ** -0.5),
        "ffn_w_gate_up": nrm(ks[13], (N_EVEN, D, 2 * FFN_DIM), D ** -0.5),
        "ffn_w_down": nrm(ks[14], (N_EVEN, FFN_DIM, D), FFN_DIM ** -0.5),
        "ret_w_in": nrm(ks[15], (N_ODD, D, RET_IN), D ** -0.5),
        "ret_w_out": nrm(ks[16], (N_ODD, RET_V, D), RET_V ** -0.5),
        "moe_w_router": nrm(ks[17], (N_ODD, D, N_EXPERTS), D ** -0.5),
        "moe_b_router": nrm(ks[18], (N_ODD, N_EXPERTS), 0.01),
        "moe_w_gate_up": nrm(ks[19], (N_ODD, N_EXPERTS, D, 2 * FFN_DIM), D ** -0.5),
        "moe_w_down": nrm(ks[20], (N_ODD, N_EXPERTS, FFN_DIM, D), FFN_DIM ** -0.5),
        "final_norm_g": 1.0 + nrm(ks[21], (D,), 0.02),
    }

def reference(x, c, positions, ada_w, ada_b, mix_norm_g, ffn_norm_g,
              sgu_w_in, sgu_ln_g, sgu_ln_b, sgu_w_s, sgu_b_s, sgu_w_out,
              ffn_w_gate_up, ffn_w_down, ret_w_in, ret_w_out,
              moe_w_router, moe_b_router, moe_w_gate_up, moe_w_down,
              final_norm_g):
    sc = jax.nn.silu(c)
    for i in range(DEPTH):
        j = i // 2
        mod = sc @ ada_w[i] + ada_b[i]
        sh1, s1, g1, sh2, s2, g2 = [m[:, None, :] for m in jnp.split(mod, 6, axis=-1)]
        h = rmsnorm(x, mix_norm_g[i]) * (1.0 + s1) + sh1
        if i % 2 == 0:
            y = chunked_sgu(h, sgu_w_in[j], sgu_ln_g[j], sgu_ln_b[j],
                            sgu_w_s[j], sgu_b_s[j], sgu_w_out[j])
        else:
            y = retention(h, ret_w_in[j], ret_w_out[j], positions)
        x = x + g1 * y
        h = rmsnorm(x, ffn_norm_g[i]) * (1.0 + s2) + sh2
        if i % 2 == 0:
            y = swiglu(h, ffn_w_gate_up[j], ffn_w_down[j])
        else:
            y = moe_swiglu(h, moe_w_router[j], moe_b_router[j],
                           moe_w_gate_up[j], moe_w_down[j])
        x = x + g2 * y
    return rmsnorm(x, final_norm_g)


_drawn_inputs = setup_inputs


def setup_inputs(seed=0):
    import zlib

    import numpy as np

    out = dict(_drawn_inputs(seed))
    spreads = {}
    factors = {'mix_norm_g': 4.195,
     'ffn_norm_g': 3.996,
     'sgu_ln_g': 8.0,
     'sgu_ln_b': 8.0,
     'moe_b_router': 5.045,
     'final_norm_g': 2.743}
    for name, (base, spread) in spreads.items():
        noise = np.random.default_rng([zlib.crc32(name.encode()), seed]).standard_normal(out[name].shape)
        drawn = base * np.exp(spread * noise) if base else spread * noise
        out[name] = __import__('jax').numpy.asarray(drawn.astype(out[name].dtype))
    for name, factor in factors.items():
        out[name] = (out[name] * factor).astype(out[name].dtype)
    return out
```

```python
import concourse.bass as bass
from concourse import mybir
from contextlib import ExitStack
import numpy as np

P = 128
D_MODEL = 1024
SEQ = 256
NCH = SEQ // P
KT = D_MODEL // P
SGU = 2 * D_MODEL
HEADS, DK, DV = 4, 256, 512
RET_IN = 2 * HEADS * DK + 2 * HEADS * DV
FFN = ((8 * D_MODEL // 3 + 127) // 128) * 128
NE = 8
EPS = 1e-6
UNIT = 2048
STEPS = FFN // 256
FU = 3 * STEPS
DENSE_RING, MOE_RING, SPLIT_RING = 9, 11, 3
MAGIC = 1.5 * 2.0 ** 23
TWO_PI_HI, TWO_PI_MID = 6.28125, 0.0019350051879882812
TWO_PI_LO = 2 * np.pi - TWO_PI_HI - TWO_PI_MID
SIN_MAX = 3.1415925


def ffn_unit(kind, s):
    if kind == "D":
        return 3 * s + 6 if s <= STEPS - 3 else FU - STEPS + s
    return 2 * s + max(0, s - 2) + (kind == "B")


FFN_ORDER = sorted([(ffn_unit(k, s), k, s) for k in "ABD" for s in range(STEPS)])

W_SGU_IN = 0
W_SGU_OUT = W_SGU_IN + 16
W_FFN = W_SGU_OUT + 8
W_RET_IN = W_FFN + FU
W_RET_OUT = W_RET_IN + 24
W_MOE = W_RET_OUT + 8


def dense_stream():
    out, a, w = [], 0, 0

    def ada(n):
        nonlocal a
        for _ in range(n):
            out.append(("A", a // 2, a % 2))
            a += 1

    def split(n):
        nonlocal w
        for _ in range(n):
            out.append(("W", w))
            w += 1
    ada(8)
    for _ in range(8):
        split(2)
        ada(1)
    for _ in range(8):
        split(1)
        ada(1)
    for u, k, s in FFN_ORDER:
        split(1)
        if k == "B" and s < 8:
            ada(1)
    for _ in range(12):
        split(2)
        ada(1)
    for j in range(8):
        split(1)
        if j < 4:
            ada(1)
    return out


STREAM = dense_stream()
N_DENSE = len(STREAM)
W_AT = {u[1]: n for n, u in enumerate(STREAM) if u[0] == "W"}
A_AT = {2 * u[1] + u[2]: n for n, u in enumerate(STREAM) if u[0] == "A"}
SLOT_ORDER = [(N_DENSE + i) % DENSE_RING for i in range(DENSE_RING)] + [9, 10]
BLOCK_BANKS = [(0, 1), (2, 4)]
ADA_BANK = 3


def trunk(nc, t, out):
    f32, f32r, i32, u32 = mybir.dt.float32, mybir.dt.float32r, mybir.dt.int32, mybir.dt.uint32
    ALU, ACT, AX = mybir.AluOpType, mybir.ActivationFunctionType, mybir.AxisListType
    ctx = ExitStack()
    with ctx:
        base = nc.sbuf_base if not callable(nc.sbuf_base) else nc.sbuf_base()
        base = (base + 63) // 64 * 64

        def at(name, shape, dt, off):
            return nc.alloc_sbuf_tensor_at(name, [P, *shape], dt, offset=base + off)

        def sem(name):
            return ctx.enter_context(nc.semaphore(name))

        KB = 1024
        RAW0, HI0, LO0 = 0, 88 * KB, 112 * KB
        X0, HTH0, HTL0, BIG0 = 136 * KB, 144 * KB, 152 * KB, 160 * KB
        ATH0, ATL0, F0 = 192 * KB, 196 * KB, 200 * KB
        E0 = RAW0 + 9 * 8 * KB
        raw = [at(f"raw{i}", [UNIT], f32, RAW0 + 8 * KB * i) for i in range(MOE_RING)]
        hi = [at(f"hi{i}", [UNIT], f32r, HI0 + 8 * KB * i) for i in range(SPLIT_RING)]
        lo = [at(f"lo{i}", [UNIT], f32r, LO0 + 8 * KB * i) for i in range(SPLIT_RING)]
        x_sb = at("x_sb", [NCH, D_MODEL], f32, X0)
        h_hi = at("h_hi", [KT, SEQ], f32r, HTH0)
        h_lo = at("h_lo", [KT, SEQ], f32r, HTL0)
        a_hi = at("a_hi", [2, 2, SEQ], f32r, ATH0)
        a_lo = at("a_lo", [2, 2, SEQ], f32r, ATL0)
        acc = at("acc", [2, 512], f32, E0)
        acc0 = at("acc0", [2, 512], f32, E0 + 4 * KB)
        gate1 = at("gate1", [D_MODEL], f32, E0 + 8 * KB)
        ws_t = at("ws_t", [8, P], f32, E0 + 12 * KB)
        trig = at("trig", [2, NCH, P], f32, E0 + 12 * KB)
        squares_o = at("squares_o", [512], f32, E0 + 12 * KB)
        sc_t = at("sc_t", [384], f32, E0 + 14 * KB)
        rope_tmp = at("rope_tmp", [2, P], f32, E0 + 14 * KB)
        xn = at("xn", [NCH, D_MODEL], f32, BIG0)
        u_sb = at("u_sb", [NCH, SGU], f32, BIG0)
        v_sb = at("v_sb", [NCH, SGU], f32, BIG0 + 16 * KB)
        bs_rows = at("bs_rows", [P], f32, BIG0 + 12 * KB)
        ws_raw = at("ws_raw", [8, P], f32, BIG0 + 8 * KB)
        fact = at("fact", [2, NCH, 256], f32, BIG0 + 8 * KB)
        rv = at("rv", [NCH, SGU], f32, BIG0)
        q_t = at("q_t", [8, SEQ], f32, BIG0 + 16 * KB)
        k_t = at("k_t", [8, SEQ], f32, BIG0 + 24 * KB)
        yacc = at("yacc", [NCH, D_MODEL], f32, BIG0 + 8 * KB)
        y_ev = at("y_ev", [D_MODEL], f32, BIG0 + 16 * KB)
        pick = at("pick", [NCH, P], f32, BIG0 + 20 * KB)
        pick_t = at("pick_t", [NCH, P], f32, BIG0 + 21 * KB)
        mact = at("mact", [2, NCH, 256], f32, BIG0 + 22 * KB)
        gval = at("gval", [KT, P], f32, BIG0 + 26 * KB)
        out_tmp = at("out_tmp", [4, 512], f32, ATH0)
        fin = at("fin", [D_MODEL], f32, HTH0)
        val_t = at("val_t", [KT, SEQ], f32, ATH0)
        ln_rows = at("ln_rows", [2, 2, 512], f32, ATH0)
        decay = at("decay", [HEADS, 256], f32, ATH0)
        rope = at("rope", [NCH, 512], f32, ATL0)
        silu_g = at("silu_g", [NCH, 512], f32, ATL0)
        gate2 = at("gate2", [D_MODEL], f32, F0)
        cst = at("cst", [4, P], f32, F0 + 4 * KB)
        small = [F0 + 6 * KB]

        def little(name, shape, dt=f32):
            n = int(np.prod(shape)) * 4
            small[0] += (-small[0]) % 32
            r = at(name, shape, dt, small[0])
            small[0] += n
            return r
        ident, ones, iota, utri = (cst[:, i, :] for i in range(4))
        vecs = little("vecs", [40])
        sc = little("sc", [KT])
        mods = little("mods", [2, 4, KT])
        mulv = little("mulv", [KT])
        ssq = little("ssq", [NCH])
        rstd = little("rstd", [NCH])
        bs_t = little("bs_t", [8])
        stats = little("stats", [NCH, 4, 6])
        mv = little("mv", [NCH, 2])
        oss = little("oss", [NCH])
        root = little("root", [NCH])
        step_t = little("step_t", [NCH])
        pos_i = little("pos_i", [NCH], i32)
        pos_f = little("pos_f", [NCH])
        wr = little("wr", [KT, NE])
        brow = little("brow", [NE])
        logit = at("logit", [NCH, NE], f32, BIG0 + 30 * KB)
        top = at("top", [NCH, 8], f32, BIG0 + 30 * KB + 64)
        topi = at("topi", [NCH, 8], u32, BIG0 + 30 * KB + 128)
        topf = at("topf", [NCH, 8], f32, BIG0 + 30 * KB + 192)
        oh = at("oh", [2, NCH, NE], f32, BIG0 + 30 * KB + 256)
        wts = at("wts", [NCH, 4], f32, BIG0 + 30 * KB + 384)
        m_sel = little("m_sel", [NCH, NE])
        gates = little("gates", [NCH, NE])
        slot = little("slot", [NCH, NE])
        most = little("most", [1])
        most_i = little("most_i", [1], i32)
        assert base + small[0] <= nc.sbuf_usable_end, (base, small[0], nc.sbuf_usable_end)

        bank = [ctx.enter_context(nc.psum_tensor(f"bank{i}", [P, 512], f32)) for i in range(8)]

        raw_full = [sem(f"raw_full{i}") for i in range(MOE_RING)]
        split_hi, units_dve, units_pe = sem("split_hi"), sem("units_dve"), sem("units_pe")
        acc0_full = [sem(f"acc0_full{i}") for i in range(2)]
        acc0_zero, acc0_used, acc_summed, mod_ready = (
            sem(n) for n in ("acc0_zero", "acc0_used", "acc_summed", "mod_ready"))
        s_cst, s_x, s_vec, s_ws, s_pos, s_invf, s_decay, s_wr, s_fing, s_out = (
            sem(n) for n in ("s_cst", "s_x", "s_vec", "s_ws", "s_pos", "s_invf", "s_decay", "s_wr", "s_fing", "s_out"))
        ln_full = [sem(f"ln_full{i}") for i in range(2)]
        sc_ready, var_ready, root_ready = sem("sc_ready"), sem("var_ready"), sem("root_ready")
        ws_masked, ws_tr, ws_ready = sem("ws_masked"), sem("ws_tr"), sem("ws_ready")
        x_ready, ss_ready, xn_ready, tr_ready, val_ready, h_hi_ready, h_ready = (
            sem(n) for n in ("x_ready", "ss_ready", "xn_ready", "tr_ready", "val_ready", "h_hi_ready", "h_ready"))
        gelu_done, v_norm, v_ready, fv_done, y_blk = (
            sem(n) for n in ("gelu_done", "v_norm", "v_ready", "fv_done", "y_blk"))
        t_done, at_hi, at_ready, silu_done, act_ready = (
            sem(n) for n in ("t_done", "at_hi", "at_ready", "silu_done", "act_ready"))
        ang_ready, trig_ready, rope_done, qk_tr, qk_ready, ret_act, scores_done, sct_ready, o_done, o_ss, og_done = (
            sem(n) for n in ("ang_ready", "trig_ready", "rope_done", "qk_tr", "qk_ready", "ret_act", "scores_done",
                             "sct_ready", "o_done", "o_ss", "og_done"))
        router_done, top_ready, exp_done, sel_ready, pos_done, slots_ready = (
            sem(n) for n in ("router_done", "top_ready", "exp_done", "sel_ready", "pos_done", "slots_ready"))
        pick_ready, pick_tr, pick_t_ready, gathered, gval_ready, g_hi_ready, g_ready, y_out, scattered, yacc_done = (
            sem(n) for n in ("pick_ready", "pick_tr", "pick_t_ready", "gathered", "gval_ready", "g_hi_ready",
                             "g_ready", "y_out", "scattered", "yacc_done"))
        dve_seq, fin_ready, yacc_zero, v_scaled = (
            sem(n) for n in ("dve_seq", "fin_ready", "yacc_zero", "v_scaled"))

        T_DENSE = 8 + STEPS + 8
        T_SGU, T_FFN, T_RET = 0, 8, 8 + STEPS

        def rhs(tile, kk, n0, n1, width):
            return tile[:, kk * width + n0:kk * width + n1]

        block = ctx.enter_context(nc.Block())

        @block.sync
        def _(sp):
            def ada_source(k, half):
                layer, b = divmod(k, 12)
                return columns(t["ada_w"][layer], b, half)

            def columns(w, b, half):
                return w.rearrange("(p k) n -> p k n", p=P)[:, 4 * half:4 * half + 4, 512 * b:512 * b + 512]

            def rows(w, j):
                return w[256 * j:256 * j + 256, :].rearrange("(k p) n -> p k n", p=P)

            def ffn_load(dst, gate_up, down, kind, s, full):
                if kind == "D":
                    sp.dma_start(dst[:].rearrange("p (k n) -> p k n", k=2), rows(down, s)).then_inc(full, 16)
                    return
                half = int(kind == "B")
                src = gate_up.rearrange("(p k) (g n) -> p (k g) n", p=P, g=2)
                sp.dma_start(dst[:].rearrange("p (k n) -> p k n", k=8),
                             src[:, 8 * half:8 * half + 8, 256 * s:256 * s + 256]).then_inc(full, 16)

            for k in range(4):
                g = t[("mix_norm_g", "ffn_norm_g")[k % 2]][k // 2]
                sp.dma_start(vecs[:, 8 * k:8 * k + 8], g.rearrange("(p k) -> p k", p=P)).then_inc(s_vec, 16)
            sp.dma_start(vecs[:, 32:40], t["c"].rearrange("a (p k) -> p (a k)", p=P)).then_inc(s_vec, 16)
            sp.dma_start(cst[:], t["consts"].rearrange("p (k n) -> p k n", k=4)).then_inc(s_cst, 16)
            for n, unit in enumerate(STREAM):
                slot_n, full = raw[n % DENSE_RING], raw_full[n % DENSE_RING]
                if n >= DENSE_RING:
                    sp.wait_ge(units_dve, n - DENSE_RING + 1)
                if unit[0] == "A":
                    _, k, half = unit
                    if half == 0:
                        if k < 2:
                            sp.wait_ge(acc0_zero, 1)
                        else:
                            sp.wait_ge(acc0_used, k - 1)
                        layer, b = divmod(k, 12)
                        sp.dma_start(acc0[0:1, k % 2, :], t["ada_b"][layer:layer + 1, 512 * b:512 * b + 512]) \
                            .then_inc(acc0_full[k % 2], 16)
                    sp.dma_start(slot_n[:].rearrange("p (k n) -> p k n", k=4), ada_source(k, half)).then_inc(full, 16)
                else:
                    w = unit[1]
                    if w < W_SGU_OUT:
                        b, half = divmod(w - W_SGU_IN, 2)
                        col = (b + 4) % 8
                        sp.dma_start(slot_n[:].rearrange("p (k n) -> p k n", k=4),
                                     columns(t["sgu_w_in"][0], col, half)).then_inc(full, 16)
                    elif w < W_FFN:
                        sp.dma_start(slot_n[:].rearrange("p (k n) -> p k n", k=2),
                                     rows(t["sgu_w_out"][0], w - W_SGU_OUT)).then_inc(full, 16)
                    elif w < W_RET_IN:
                        _, kind, s = FFN_ORDER[w - W_FFN]
                        ffn_load(slot_n, t["ffn_w_gate_up"][0], t["ffn_w_down"][0], kind, s, full)
                    elif w < W_RET_OUT:
                        b, half = divmod(w - W_RET_IN, 2)
                        sp.dma_start(slot_n[:].rearrange("p (k n) -> p k n", k=4),
                                     columns(t["ret_w_in"][0], b, half)).then_inc(full, 16)
                    else:
                        sp.dma_start(slot_n[:].rearrange("p (k n) -> p k n", k=2),
                                     rows(t["ret_w_out"][0], w - W_RET_OUT)).then_inc(full, 16)
                if n == 1:
                    sp.dma_start(x_sb[:], t["x"].rearrange("a (c p) n -> p (a c) n", p=P)).then_inc(s_x, 16)
                    sp.dma_start(bs_rows[0:8, :], t["sgu_b_s"][0]).then_inc(s_ws, 16)
                    sp.dma_start(ws_raw[:], t["sgu_w_s"][0].rearrange("g p s -> p g s")).then_inc(s_ws, 16)
                    sp.dma_start(pos_i[:], t["positions"].rearrange("a (c p) -> p (a c)", p=P),
                                 allow_slow_non_contiguous=True).then_inc(s_pos, 16)
                    sp.dma_start(wr[:], t["moe_w_router"][0].rearrange("(p k) n -> p k n", p=P)).then_inc(s_wr, 16)
                    sp.dma_start(brow[:], t["moe_b_router"][0:1, :].to_broadcast([P, NE])).then_inc(s_wr, 16)
                if unit == ("W", W_SGU_IN + 4):
                    sp.wait_ge(h_ready, 4)
                    for j in range(2):
                        for i, name in enumerate(("sgu_ln_g", "sgu_ln_b")):
                            sp.dma_start(ln_rows[:, j, i, :], t[name][0:1, 512 * j:512 * j + 512]
                                         .to_broadcast([P, 512])).then_inc(ln_full[j], 16)
                if unit in (("W", W_SGU_IN + 12), ("W", W_SGU_IN + 14)):
                    j = 2 + (unit[1] - W_SGU_IN - 12) // 2
                    sp.wait_ge(v_ready, j - 1)
                    for i, name in enumerate(("sgu_ln_g", "sgu_ln_b")):
                        sp.dma_start(ln_rows[:, j % 2, i, :], t[name][0:1, 512 * j:512 * j + 512]
                                     .to_broadcast([P, 512])).then_inc(ln_full[j % 2], 16)
                if unit == ("W", W_FFN + 4):
                    sp.wait_ge(y_blk, 4)
                    sp.dma_start(trig[:, 0, 0, :], t["inv_freq"].to_broadcast([P, P])).then_inc(s_invf, 16)
                if unit == ("W", W_RET_IN + 4):
                    sp.wait_ge(h_ready, 12)
                    sp.dma_start(decay[:], t["decay"].rearrange("p (h n) -> p h n", h=HEADS)).then_inc(s_decay, 16)

            def expert_load(e, u, kind, s):
                gu = t["moe_w_gate_up"][0][bass.ds(e, 1)].rearrange("a k n -> (a k) n")
                dn = t["moe_w_down"][0][bass.ds(e, 1)].rearrange("a k n -> (a k) n")
                k = SLOT_ORDER[u % MOE_RING]
                ffn_load(raw[k], gu, dn, kind, s, raw_full[k])

            for u, kind, s in FFN_ORDER[:MOE_RING]:
                if u < DENSE_RING:
                    sp.wait_ge(units_dve, N_DENSE + u - DENSE_RING + 1)
                elif u == DENSE_RING:
                    sp.wait_ge(mod_ready, 24)
                    sp.wait_ge(x_ready, 6)
                expert_load(0, u, kind, s)
            with sp.Fori(0, NE - 1) as e:
                for u, kind, s in FFN_ORDER[MOE_RING:]:
                    sp.wait_ge(units_dve, e * FU + (N_DENSE + u - MOE_RING + 1))
                    expert_load(e, u, kind, s)
                for u, kind, s in FFN_ORDER[:MOE_RING]:
                    sp.wait_ge(units_dve, e * FU + (N_DENSE + FU + u - MOE_RING + 1))
                    expert_load(e + 1, u, kind, s)
            for u, kind, s in FFN_ORDER[MOE_RING:]:
                sp.wait_ge(units_dve, (NE - 1) * FU + N_DENSE + u - MOE_RING + 1)
                expert_load(NE - 1, u, kind, s)
            sp.wait_ge(slots_ready, 1)
            n_most = sp.value_load(most_i[0:1, 0:1], min_val=0, max_val=SEQ)
            with sp.If(n_most > P):
                with sp.Fori(0, NE) as e:
                    for u, kind, s in FFN_ORDER:
                        sp.wait_ge(units_dve, e * FU + (NE * FU + N_DENSE + u - MOE_RING + 1))
                        expert_load(e, u, kind, s)
            sp.wait_ge(x_ready, 7)
            sp.dma_start(y_ev[:], t["final_norm_g"].rearrange("(a n) -> a n", a=1).to_broadcast([P, D_MODEL])) \
                .then_inc(s_fing, 16)
            for c in range(NCH):
                sp.wait_ge(fin_ready, c + 1)
                sp.dma_start(out[0, P * c:P * c + P, :], yacc[:, c, :]).then_inc(s_out, 16)
            sp.wait_ge(s_out, 16 * NCH)

        def raw_times(n):
            return 16 * (n // DENSE_RING + 1)

        def moe_raw_times(k, u, experts):
            before = sum(1 for n in range(N_DENSE) if n % DENSE_RING == k) if k < DENSE_RING else 0
            return experts * (16 * FU // MOE_RING) + 16 * (before + u // MOE_RING + 1)

        @block.scalar
        def _(act):
            copy = ACT.Copy
            roots = [0]

            def take_root(c0, c1):
                act.wait_ge(var_ready, roots[0] + 1)
                nc.scalar.activation(root[:, c0:c1], rstd[:, c0:c1], ACT.Sqrt).then_inc(root_ready, 1)
                roots[0] += 1

            def split(w):
                n = W_AT[w]
                act.wait_ge(raw_full[n % DENSE_RING], raw_times(n))
                if w >= SPLIT_RING:
                    act.wait_ge(units_pe, w - SPLIT_RING + 1)
                nc.scalar.activation(hi[w % SPLIT_RING][:], raw[n % DENSE_RING][:], copy).then_inc(split_hi, 1)

            def moe_split(u, e_units, experts):
                k, w = SLOT_ORDER[u % MOE_RING], W_MOE + u
                act.wait_ge(raw_full[k], moe_raw_times(k, u, experts))
                act.wait_ge(units_pe, e_units + (w - SPLIT_RING + 1))
                nc.scalar.activation(hi[w % SPLIT_RING][:], raw[k][:], copy).then_inc(split_hi, 1)

            def squares(k, c):
                if k == 0:
                    act.wait_ge(s_x, 16)
                else:
                    act.wait_ge(x_ready, 2 * (k - 1) + c + 1)
                nc.scalar.activation(val_t[:, 4 * c:4 * c + 4, :], x_sb[:, c, :].rearrange("p (k n) -> p k n", k=4),
                                     ACT.Square, accum_out=ssq[:, c:c + 1]).then_inc(ss_ready, 1)
                take_root(c, c + 1)

            def norm_hi(k):
                for j in range(4):
                    c, half = divmod(j, 2)
                    act.wait_ge(val_ready, 4 * k + j + 1)
                    nc.scalar.activation(h_hi[:, 4 * half:4 * half + 4, P * c:P * c + P],
                                         val_t[:, 4 * half:4 * half + 4, P * c:P * c + P], copy).then_inc(h_hi_ready, 1)

            def down_hi(i, psum, free):
                act.wait_ge(t_done, i + 1)
                if free is not None:
                    act.wait_ge(units_pe, free)
                nc.scalar.activation(a_hi[:, (i - T_SGU) % 2, :, :], psum[:].rearrange("p (k n) -> p k n", k=2),
                                     copy).then_inc(at_hi, 1)

            act.wait_ge(s_vec, 80)
            nc.scalar.activation(sc[:], vecs[:, 32:40], ACT.Silu).then_inc(sc_ready, 1)
            for c in range(NCH):
                squares(0, c)

            def gating_gelu(b):
                act.wait_ge(units_pe, W_SGU_IN + 2 * b + 2)
                for c in range(NCH):
                    dst = (v_sb if b < 4 else u_sb)[:, c, 512 * (b % 4):512 * (b % 4) + 512]
                    nc.scalar.activation(dst, bank[BLOCK_BANKS[b % 2][c]][:], ACT.Gelu_apprx_tanh).then_inc(gelu_done, 1)

            norm_hi(0)
            split(W_SGU_IN)
            split(W_SGU_IN + 1)
            for b in range(1, 8):
                split(W_SGU_IN + 2 * b)
                split(W_SGU_IN + 2 * b + 1)
                gating_gelu(b - 1)
                if b == 4:
                    take_root(0, NCH)
            split(W_SGU_OUT)
            split(W_SGU_OUT + 1)
            gating_gelu(7)

            def down_phase(w0, t0, wnext):
                down_hi(t0, bank[2], None)
                for j in range(1, 8):
                    if j + 1 < 8:
                        split(w0 + j + 1)
                    else:
                        split_next(wnext)
                    down_hi(t0 + j, bank[(2, 0)[j % 2]], w0 + j - 1 if j >= 2 else None)

            def split_next(w):
                if w is not None:
                    split(w)

            down_phase(W_SGU_OUT, T_SGU, W_FFN)
            split(W_FFN + 1)
            for c in range(NCH):
                squares(1, c)
            norm_hi(1)

            def ffn_silu(s, units, a0, tile, chunks, done):
                act.wait_ge(units_pe, units + (ffn_unit("B", s) + 1))
                if s >= 2:
                    act.wait_ge(t_done, a0 + (s - 1))
                for c in range(chunks):
                    b = c if chunks == 2 else s % 2
                    nc.scalar.activation(tile[:, s % 2, c, :], bank[b][:, 0:256], ACT.Silu).then_inc(silu_done, 1)

            def ffn_hi(s, units, t0, parity, chunks):
                act.wait_ge(t_done, t0 + (s + 1))
                act.wait_ge(units_pe, units + (ffn_unit("D", s - 2) + 1 if s >= 2 else 0))
                n = P * chunks
                nc.scalar.activation(a_hi[:, parity, :, 0:n], bank[2][:, 0:2 * n].rearrange("p (k n) -> p k n", k=2),
                                     copy).then_inc(at_hi, 1)

            for u, kind, s in FFN_ORDER:
                if u >= 2:
                    split(W_FFN + u)
                for s2 in range(STEPS):
                    if u == ffn_unit("B", s2) + 2:
                        ffn_silu(s2, W_FFN, T_FFN, fact, NCH, None)
                        if s2 >= 1:
                            ffn_hi(s2 - 1, W_FFN, T_FFN, (s2 - 1) % 2, NCH)
            ffn_hi(STEPS - 1, W_FFN, T_FFN, (STEPS - 1) % 2, NCH)

            split(W_RET_IN)
            split(W_RET_IN + 1)
            act.wait_ge(ang_ready, 1)
            nc.scalar.activation(trig[:, :, :, :], trig[:, :, :, :], ACT.Sin).then_inc(trig_ready, 1)
            for c in range(NCH):
                squares(2, c)
            norm_hi(2)

            def qk_copy(b):
                for c in range(NCH):
                    act.wait_ge(qk_tr, 2 * b + c + 1)
                    dst = (q_t if b < 2 else k_t)[:, 4 * (b % 2):4 * (b % 2) + 4, P * c:P * c + P]
                    nc.scalar.activation(dst, bank[5 + c][:].rearrange("p (k n) -> p k n", k=4),
                                         copy).then_inc(qk_ready, 1)

            def ret_v(b):
                act.wait_ge(units_pe, W_RET_IN + 2 * b + 2)
                for c in range(NCH):
                    nc.scalar.activation(rv[:, c, 512 * (b - 4):512 * (b - 4) + 512], bank[BLOCK_BANKS[b % 2][c]][:],
                                         copy).then_inc(ret_act, 1)

            def ret_gate(h):
                b = 8 + h
                act.wait_ge(units_pe, W_RET_IN + 2 * b + 2)
                if h >= 1:
                    act.wait_ge(og_done, h)
                for c in range(NCH):
                    nc.scalar.activation(silu_g[:, c, :], bank[BLOCK_BANKS[b % 2][c]][:], ACT.Silu).then_inc(ret_act, 1)
                act.wait_ge(o_done, h + 1)
                for c in range(NCH):
                    nc.scalar.activation(squares_o[:], bank[6 + c][:], ACT.Square, accum_out=oss[:, c:c + 1]) \
                        .then_inc(o_ss, 1)
                    act.wait_ge(o_ss, 2 * h + c + 1)
                take_root(0, NCH)

            for b in range(1, 12):
                split(W_RET_IN + 2 * b)
                split(W_RET_IN + 2 * b + 1)
                if b - 1 >= 4 and b - 1 < 8:
                    ret_v(b - 1)
                if 2 <= b < 6:
                    qk_copy(b - 2)
                if b - 1 >= 8:
                    ret_gate(b - 1 - 8)
            split(W_RET_OUT)
            split(W_RET_OUT + 1)
            ret_gate(3)
            down_phase(W_RET_OUT, T_RET, None)
            for c in range(NCH):
                squares(3, c)

            act.wait_ge(top_ready, 1)
            nc.scalar.activation(wts[:, :, 1], wts[:, :, 0], ACT.Exp).then_inc(exp_done, 1)

            def expert(e, units, experts, steps, one):
                moe_split(0, units, experts)
                moe_split(1, units, experts)
                act.wait_ge(pick_tr, one + 1)
                nc.scalar.activation(pick_t[:, :, :], bank[3][:, 0:SEQ].rearrange("p (c n) -> p c n", c=NCH),
                                     copy).then_inc(pick_t_ready, 1)
                act.wait_ge(gval_ready, one + 1)
                nc.scalar.activation(h_hi[:, :, 0:P], gval[:, :, :], copy).then_inc(g_hi_ready, 1)
                for u, kind, s in FFN_ORDER:
                    if u >= 2:
                        moe_split(u, units, experts)
                    for s2 in range(STEPS):
                        if u == ffn_unit("B", s2) + 2:
                            ffn_silu(s2, units + W_MOE, steps + T_DENSE, mact, 1, None)
                            if s2 >= 1:
                                ffn_hi(s2 - 1, units + W_MOE, steps + T_DENSE, (s2 - 1) % 2, 1)
                ffn_hi(STEPS - 1, units + W_MOE, steps + T_DENSE, (STEPS - 1) % 2, 1)
                act.wait_ge(units_pe, units + (W_MOE + FU))
                for half in range(2):
                    nc.scalar.activation(y_ev[:, 512 * half:512 * half + 512], bank[4 + half][:], copy).then_inc(y_out, 1)

            with act.Fori(0, NE) as e:
                expert(e, e * FU, e, e * STEPS, e)
            act.wait_ge(slots_ready, 1)
            n_most = act.value_load(most_i[0:1, 0:1], min_val=0, max_val=SEQ)
            with act.If(n_most > P):
                with act.Fori(0, NE) as e:
                    expert(e, e * FU + NE * FU, e + NE, e * STEPS + NE * STEPS, e + NE)
            act.wait_ge(x_ready, 7)
            nc.scalar.activation(fin[:], x_sb[:, 0, :], ACT.Square, accum_out=ssq[:, 0:1]).then_inc(ss_ready, 1)
            take_root(0, 1)
            act.wait_ge(x_ready, 8)
            nc.scalar.activation(gval[:, :, :], x_sb[:, 1, :].rearrange("p (k n) -> p k n", k=KT), ACT.Square,
                                 accum_out=ssq[:, 1:2]).then_inc(ss_ready, 1)
            take_root(1, 2)

        @block.gpsimd
        def _(pool):
            nc.gpsimd.memset(acc0[:, :, :], 0.0).then_inc(acc0_zero, 1)
            pool.wait_ge(s_ws, 32)
            nc.gpsimd.affine_select(out=ws_raw[:, :, :], in_=ws_raw[:, :, :], compare_op=ALU.is_ge, fill=0.0, base=0,
                                    pattern=[[0, 8], [-1, P]], channel_multiplier=1).then_inc(ws_masked, 1)
            for j in range(4):
                pool.wait_ge(v_norm, 2)
                pool.wait_ge(ln_full[j % 2], 32 * (j // 2 + 1))
                for c in range(NCH):
                    v = v_sb[:, c, 512 * j:512 * j + 512]
                    nc.gpsimd.tensor_tensor(v, v, ln_rows[:, j % 2, 0, :], ALU.mult).then_inc(v_scaled, 1)
                    pool.wait_ge(v_scaled, 2 * j + c + 1)
                    last = nc.gpsimd.tensor_tensor(v, v, ln_rows[:, j % 2, 1, :], ALU.add)
                last.then_inc(v_ready, 1)
            pool.wait_ge(x_ready, 6)
            nc.gpsimd.memset(yacc[:, :, :], 0.0).then_inc(yacc_zero, 1)

        @block.vector
        def _(dve):
            seq = [0]

            def link(ins):
                seq[0] += 1
                ins.then_inc(dve_seq, 1)
                dve.wait_ge(dve_seq, seq[0])

            V = nc.vector
            roots = [0]

            def rsqrt(src, c0, c1, scale):
                var, r, s = rstd[:, c0:c1], root[:, c0:c1], step_t[:, c0:c1]
                V.tensor_scalar(var, src, scale, EPS, ALU.mult, ALU.add).then_inc(var_ready, 1)
                roots[0] += 1
                dve.wait_ge(root_ready, roots[0])
                link(V.reciprocal(r, r))
                link(V.tensor_tensor(s, r, r, ALU.mult))
                link(V.tensor_tensor(s, s, var, ALU.mult))
                link(V.tensor_scalar(s, s, -0.5, 1.5, ALU.mult, ALU.add))
                link(V.tensor_tensor(var, r, s, ALU.mult))

            def split(w):
                n = W_AT[w]
                dve.wait_ge(split_hi, w + 1)
                if w >= SPLIT_RING:
                    dve.wait_ge(units_pe, w - SPLIT_RING + 1)
                V.tensor_tensor(lo[w % SPLIT_RING][:], raw[n % DENSE_RING][:], hi[w % SPLIT_RING][:].bitcast(f32),
                                ALU.subtract).then_inc(units_dve, 1)

            def ada(i):
                n = A_AT[i]
                k, half = divmod(i, 2)
                dve.wait_ge(raw_full[n % DENSE_RING], raw_times(n))
                if half == 0:
                    dve.wait_ge(acc0_full[k % 2], 16 * (k // 2 + 1))
                    if k >= 2:
                        dve.wait_ge(acc_summed, k - 1)
                for kk in range(4):
                    first, last = half == 0 and kk == 0, kk == 3
                    a = acc[:, k % 2, :]
                    ins = V.scalar_tensor_tensor(out=a, in0=raw[n % DENSE_RING][:, 512 * kk:512 * kk + 512],
                                                 scalar=sc[:, 4 * half + kk:4 * half + kk + 1],
                                                 in1=acc0[:, k % 2, :] if first else a, op0=ALU.mult, op1=ALU.add)
                    if first:
                        ins.then_inc(acc0_used, 1)
                        dve.wait_ge(acc0_used, k + 1)
                    elif not last:
                        link(ins)
                    else:
                        ins.then_inc(units_dve, 1)
                        dve.wait_ge(units_dve, n + 1)

            def mod(k):
                dve.wait_ge(acc_summed, k + 1)
                layer, b = divmod(k, 12)
                part, half = divmod(b, 2)
                if part in (2, 5):
                    dst, src = (gate1 if part == 2 else gate2)[:, 512 * half:512 * half + 512], bank[ADA_BANK][:]
                else:
                    i = {0: 0, 1: 1, 3: 2, 4: 3}[part]
                    rows = slice(64 * half, 64 * half + 64)
                    dst, src = mods[rows, layer, i, :], bank[ADA_BANK][rows, 0:KT]
                V.tensor_copy(dst, src).then_inc(mod_ready, 1)

            def normalize(k):
                for c in range(NCH):
                    dve.wait_ge(ss_ready, 2 * k + c + 1)
                    rsqrt(ssq[:, c:c + 1], c, c + 1, 1.0 / D_MODEL)
                    V.tensor_scalar(xn[:, c, :], x_sb[:, c, :], rstd[:, c:c + 1], None, ALU.mult).then_inc(xn_ready, 1)

            def norm_scale(k):
                layer, second = divmod(k, 2)
                dve.wait_ge(mod_ready, 12 * layer + (4 if not second else 10))
                dve.wait_ge(s_vec, 80)
                link(V.tensor_scalar(mulv[:], mods[:, layer, 2 * second + 1, :], 1.0, None, ALU.add))
                link(V.tensor_tensor(mulv[:], mulv[:], vecs[:, 8 * k:8 * k + 8], ALU.mult))

            def norm_values(k):
                layer, second = divmod(k, 2)
                norm_scale(k)
                for j in range(4):
                    c, half = divmod(j, 2)
                    dve.wait_ge(tr_ready, 4 * k + j + 1)
                    for q in range(4):
                        kt = 4 * half + q
                        last = V.tensor_scalar(val_t[:, kt, P * c:P * c + P], bank[4 + j][:, P * q:P * q + P],
                                               mulv[:, kt:kt + 1], mods[:, layer, 2 * second, kt:kt + 1],
                                               ALU.mult, ALU.add)
                    last.then_inc(val_ready, 1)
                if k < 3:
                    for j in range(4):
                        c, half = divmod(j, 2)
                        dve.wait_ge(h_hi_ready, 4 * k + j + 1)
                        at4 = (slice(None), slice(4 * half, 4 * half + 4), slice(P * c, P * c + P))
                        V.tensor_tensor(h_lo[at4], val_t[at4], h_hi[at4].bitcast(f32), ALU.subtract).then_inc(h_ready, 1)

            def down_lo(i, psum):
                dve.wait_ge(at_hi, i + 1)
                V.tensor_tensor(a_lo[:, i % 2, :, :], psum[:].rearrange("p (k n) -> p k n", k=2),
                                a_hi[:, i % 2, :, :].bitcast(f32), ALU.subtract).then_inc(at_ready, 1)

            def add_output(gate, units):
                dve.wait_ge(units_pe, units)
                for c in range(NCH):
                    for half in range(2):
                        cols = slice(512 * half, 512 * half + 512)
                        y = out_tmp[:, 2 * c + half, :]
                        link(V.tensor_tensor(y, bank[4 + 2 * c + half][:], gate[:, cols], ALU.mult))
                        last = V.tensor_tensor(x_sb[:, c, cols], x_sb[:, c, cols], y, ALU.add)
                    last.then_inc(x_ready, 1)

            normalize(0)
            dve.wait_ge(sc_ready, 1)
            for k in range(4):
                ada(2 * k)
                ada(2 * k + 1)
                if k:
                    mod(k - 1)
            mod(3)
            norm_values(0)

            split(W_SGU_IN)
            split(W_SGU_IN + 1)
            ada(8)
            dve.wait_ge(ws_tr, 1)
            V.tensor_copy(bs_t[:], bank[7][:, 0:8])
            V.tensor_copy(ws_t[:, 0:4, :], bank[5][:].rearrange("p (g n) -> p g n", g=4)).then_inc(ws_ready, 1)
            V.tensor_copy(ws_t[:, 4:8, :], bank[6][:].rearrange("p (g n) -> p g n", g=4)).then_inc(ws_ready, 1)

            def gating_out(j):
                dve.wait_ge(fv_done, j + 1)
                dve.wait_ge(gelu_done, 8 + 2 * (j + 1))
                for c in range(NCH):
                    for g in range(2):
                        u = u_sb[:, c, 512 * j + 256 * g:512 * j + 256 * g + 256]
                        last = V.scalar_tensor_tensor(out=u, in0=bank[5 + c][:, 256 * g:256 * g + 256],
                                                      scalar=bs_t[:, 2 * j + g:2 * j + g + 1], in1=u,
                                                      op0=ALU.add, op1=ALU.mult)
                last.then_inc(y_blk, 1)

            for b in range(1, 8):
                split(W_SGU_IN + 2 * b)
                split(W_SGU_IN + 2 * b + 1)
                ada(8 + b)
                if b % 2 and b > 1:
                    mod(4 + b // 2 - 1)
                if b - 1 < 4:
                    for c in range(NCH):
                        dve.wait_ge(gelu_done, 2 * (b - 1) + c + 1)
                        ins = V.bn_stats(stats[:, c, b - 1, :], v_sb[:, c, 512 * (b - 1):512 * b])
                        if b == 4:
                            link(ins)
                if b == 4:
                    for c in range(NCH):
                        link(V.bn_aggr(mv[:, c, :], stats[:, c, :, :]))
                    rsqrt(mv[:, :, 1], 0, NCH, 1.0)
                    for c in range(NCH):
                        V.tensor_scalar(v_sb[:, c, :], v_sb[:, c, :], mv[:, c, 0:1], rstd[:, c:c + 1],
                                        ALU.subtract, ALU.mult).then_inc(v_norm, 1)
            gating_out(0)

            split(W_SGU_OUT)
            ada(16)
            mod(7)
            split(W_SGU_OUT + 1)
            ada(17)
            for j in range(1, 4):
                gating_out(j)
            down_lo(T_SGU, bank[2])
            for j in range(1, 8):
                split(W_SGU_OUT + j + 1)
                if j < 7:
                    ada(17 + j)
                    if j % 2 == 1:
                        mod(8 + j // 2)
                down_lo(T_SGU + j, bank[(2, 0)[j % 2]])
            split(W_FFN + 1)
            mod(11)
            add_output(gate1, W_FFN)
            normalize(1)
            norm_values(1)

            def ffn_act(s, silu0, tile, chunks):
                for c in range(chunks):
                    dve.wait_ge(silu_done, silu0 + (chunks * s + c + 1))
                    b = c if chunks == 2 else s % 2
                    last = V.tensor_tensor(tile[:, s % 2, c, :], tile[:, s % 2, c, :], bank[b][:, 256:512], ALU.mult)
                last.then_inc(act_ready, 1)

            def ffn_lo(s, t0, parity, chunks):
                dve.wait_ge(at_hi, t0 + (s + 1))
                n = P * chunks
                V.tensor_tensor(a_lo[:, parity, :, 0:n], bank[2][:, 0:2 * n].rearrange("p (k n) -> p k n", k=2),
                                a_hi[:, parity, :, 0:n].bitcast(f32), ALU.subtract).then_inc(at_ready, 1)

            for u, kind, s in FFN_ORDER:
                if u >= 2:
                    split(W_FFN + u)
                if kind == "B" and s < 8:
                    ada(24 + s)
                if kind == "D" and s % 2 == 0 and s <= 6:
                    mod(12 + s // 2)
                for s2 in range(STEPS):
                    if u == ffn_unit("B", s2) + 2:
                        ffn_act(s2, 0, fact, NCH)
                        if s2 >= 1:
                            ffn_lo(s2 - 1, T_FFN, (s2 - 1) % 2, NCH)
            ffn_lo(STEPS - 1, T_FFN, (STEPS - 1) % 2, NCH)

            split(W_RET_IN)
            split(W_RET_IN + 1)
            ada(32)
            add_output(gate2, W_RET_IN)
            dve.wait_ge(s_invf, 16)
            dve.wait_ge(s_pos, 16)
            link(V.tensor_copy(pos_f[:], pos_i[:]))
            for c in range(NCH):
                link(V.tensor_scalar(trig[:, 1, c, :], trig[:, 0, 0, :], pos_f[:, c:c + 1], None, ALU.mult))
            for fn in range(2):
                a, turn, dst = trig[:, 1, :, :], rope_tmp[:, :, :], trig[:, fn, :, :]
                link(V.tensor_scalar(turn, a, 1.0 / (2 * np.pi), 0.25 if fn == 0 else 0.0, ALU.mult, ALU.add))
                link(V.tensor_scalar(turn, turn, MAGIC, MAGIC, ALU.add, ALU.subtract))
                link(V.scalar_tensor_tensor(out=dst, in0=turn, scalar=-TWO_PI_HI, in1=a, op0=ALU.mult, op1=ALU.add))
                link(V.scalar_tensor_tensor(out=dst, in0=turn, scalar=-TWO_PI_MID, in1=dst, op0=ALU.mult, op1=ALU.add))
                link(V.scalar_tensor_tensor(out=dst, in0=turn, scalar=-TWO_PI_LO, in1=dst, op0=ALU.mult, op1=ALU.add))
                if fn == 0:
                    link(V.tensor_scalar(dst, dst, np.pi / 2, None, ALU.add))
                last = V.tensor_scalar(dst, dst, SIN_MAX, -SIN_MAX, ALU.min, ALU.max)
                if fn == 0:
                    link(last)
            last.then_inc(ang_ready, 1)
            normalize(2)
            norm_values(2)

            def rotate(b):
                dve.wait_ge(units_pe, W_RET_IN + 2 * b + 2)
                for c in range(NCH):
                    if b:
                        dve.wait_ge(qk_tr, 2 * (b - 1) + c + 1)
                    ps = bank[BLOCK_BANKS[b % 2][c]][:].rearrange("p (h s f) -> p h s f", h=2, s=2)
                    r = rope[:, c, :].rearrange("p (h s f) -> p h s f", h=2, s=2)
                    t1, t2, r1, r2 = ps[:, :, 0, :], ps[:, :, 1, :], r[:, :, 0, :], r[:, :, 1, :]
                    cos, sin = (trig[:, i, c:c + 1, :].broadcast_to([P, 2, P]) for i in range(2))
                    link(V.tensor_tensor(rope_tmp[:, :, :], t2, sin, ALU.mult))
                    link(V.tensor_tensor(r1, t1, cos, ALU.mult))
                    link(V.tensor_tensor(r1, r1, rope_tmp[:, :, :], ALU.subtract))
                    link(V.tensor_tensor(rope_tmp[:, :, :], t1, sin, ALU.mult))
                    link(V.tensor_tensor(r2, t2, cos, ALU.mult))
                    V.tensor_tensor(r2, r2, rope_tmp[:, :, :], ALU.add).then_inc(rope_done, 1)
                    dve.wait_ge(rope_done, 2 * b + c + 1)

            def score(h):
                dve.wait_ge(scores_done, h + 1)
                dve.wait_ge(s_decay, 16)
                if h:
                    dve.wait_ge(o_done, h)
                V.tensor_tensor(sc_t[:, 0:256], bank[5][:, 0:256], decay[:, h, :], ALU.mult)
                V.tensor_tensor(sc_t[:, 256:384], bank[5][:, 256:384], decay[:, h, 0:P], ALU.mult) \
                    .then_inc(sct_ready, 1)

            def head_out(h):
                dve.wait_ge(o_ss, 2 * h + 2)
                rsqrt(oss[:, :], 0, NCH, 1.0 / DV)
                for c in range(NCH):
                    last = V.scalar_tensor_tensor(out=rv[:, c, 512 * h:512 * h + 512], in0=bank[6 + c][:],
                                                  scalar=rstd[:, c:c + 1], in1=silu_g[:, c, :],
                                                  op0=ALU.mult, op1=ALU.mult)
                last.then_inc(og_done, 1)

            for b in range(1, 12):
                split(W_RET_IN + 2 * b)
                if b >= 8:
                    score(b - 8)
                split(W_RET_IN + 2 * b + 1)
                ada(32 + b)
                if b % 2 and b > 1:
                    mod(16 + b // 2 - 1)
                if b - 1 < 4:
                    if b == 1:
                        dve.wait_ge(trig_ready, 1)
                    rotate(b - 1)
                if b - 1 >= 8:
                    head_out(b - 1 - 8)
            split(W_RET_OUT)
            ada(44)
            mod(21)
            split(W_RET_OUT + 1)
            ada(45)
            head_out(3)
            dve.wait_ge(og_done, 4)
            down_lo(T_RET, bank[2])
            for j in range(1, 8):
                if j < 7:
                    split(W_RET_OUT + j + 1)
                if j < 3:
                    ada(45 + j)
                if j == 1:
                    mod(22)
                if j == 4:
                    mod(23)
                down_lo(T_RET + j, bank[(2, 0)[j % 2]])
            add_output(gate1, W_MOE)
            normalize(3)
            norm_values(3)

            dve.wait_ge(router_done, 1)
            dve.wait_ge(s_wr, 32)
            for c in range(NCH):
                link(V.tensor_tensor(logit[:, c, :], bank[ADA_BANK][:, 8 * c:8 * c + 8], brow[:], ALU.add))
                link(V.max(top[:, c, :], logit[:, c, :]))
                link(V.max_index(topi[:, c, :], top[:, c, :], logit[:, c, :]))
            link(V.tensor_copy(topf[:, :, :], topi[:, :, :]))
            V.tensor_tensor(wts[:, :, 0], top[:, :, 1], top[:, :, 0], ALU.subtract).then_inc(top_ready, 1)
            for c in range(NCH):
                for i in range(2):
                    ins = V.tensor_scalar(oh[:, i, c, :], iota[:, 0:NE], topf[:, c, i:i + 1], None, ALU.is_equal)
            link(ins)
            V.tensor_tensor(m_sel[:, :, :], oh[:, 0, :, :], oh[:, 1, :, :], ALU.add).then_inc(sel_ready, 1)
            dve.wait_ge(exp_done, 1)
            link(V.tensor_scalar(wts[:, :, 2], wts[:, :, 1], 1.0, None, ALU.add))
            link(V.reciprocal(wts[:, :, 2], wts[:, :, 2]))
            link(V.tensor_tensor(wts[:, :, 3], wts[:, :, 1], wts[:, :, 2], ALU.mult))
            for c in range(NCH):
                link(V.tensor_scalar(gates[:, c, :], oh[:, 0, c, :], wts[:, c, 2:3], None, ALU.mult))
                link(V.scalar_tensor_tensor(out=gates[:, c, :], in0=oh[:, 1, c, :], scalar=wts[:, c, 3:4],
                                            in1=gates[:, c, :], op0=ALU.mult, op1=ALU.add))
            dve.wait_ge(pos_done, 1)
            for c in range(NCH):
                link(V.scalar_tensor_tensor(out=slot[:, c, :], in0=bank[ADA_BANK][:, 8 * c:8 * c + 8], scalar=1.0,
                                            in1=m_sel[:, c, :], op0=ALU.add, op1=ALU.mult))
                link(V.tensor_scalar(slot[:, c, :], slot[:, c, :], 1.0, None, ALU.subtract))
            link(V.reduce_max(most[:], bank[ADA_BANK][:, 16:24], AX.X))
            V.tensor_copy(most_i[:], most[:]).then_inc(slots_ready, 1)
            dve.wait_ge(yacc_zero, 1)

            def expert(e, units, experts, steps, one):
                def moe_split(u):
                    k, w = SLOT_ORDER[u % MOE_RING], W_MOE + u
                    dve.wait_ge(split_hi, units + (w + 1))
                    dve.wait_ge(units_pe, units + (w - SPLIT_RING + 1))
                    V.tensor_tensor(lo[w % SPLIT_RING][:], raw[k][:], hi[w % SPLIT_RING][:].bitcast(f32),
                                    ALU.subtract).then_inc(units_dve, 1)

                for c in range(NCH):
                    last = V.tensor_scalar(pick[:, c, :], iota, slot[:, c, bass.ds(e, 1)], None, ALU.is_equal)
                last.then_inc(pick_ready, 1)
                moe_split(0)
                moe_split(1)
                dve.wait_ge(gathered, one + 1)
                for kt in range(KT):
                    last = V.tensor_scalar(gval[:, kt, :], bank[6 + kt // 4][:, P * (kt % 4):P * (kt % 4) + P],
                                           mulv[:, kt:kt + 1], mods[:, 1, 2, kt:kt + 1], ALU.mult, ALU.add)
                last.then_inc(gval_ready, 1)
                dve.wait_ge(g_hi_ready, one + 1)
                V.tensor_tensor(h_lo[:, :, 0:P], gval[:, :, :], h_hi[:, :, 0:P].bitcast(f32),
                                ALU.subtract).then_inc(g_ready, 1)
                for u, kind, s in FFN_ORDER:
                    if u >= 2:
                        moe_split(u)
                    for s2 in range(STEPS):
                        if u == ffn_unit("B", s2) + 2:
                            ffn_act(s2, steps + NCH * STEPS, mact, 1)
                            if s2 >= 1:
                                ffn_lo(s2 - 1, steps + T_DENSE, (s2 - 1) % 2, 1)
                ffn_lo(STEPS - 1, steps + T_DENSE, (STEPS - 1) % 2, 1)
                for c in range(NCH):
                    dve.wait_ge(scattered, one * NCH + (c + 1))
                    for half in range(2):
                        cols = slice(512 * half, 512 * half + 512)
                        last = V.scalar_tensor_tensor(out=yacc[:, c, cols], in0=bank[(6, 4)[c] + half][:],
                                                      scalar=gates[:, c, bass.ds(e, 1)], in1=yacc[:, c, cols],
                                                      op0=ALU.mult, op1=ALU.add)
                last.then_inc(yacc_done, 1)
                dve.wait_ge(yacc_done, one + 1)

            with dve.Fori(0, NE) as e:
                expert(e, e * FU, e, e * STEPS, e)
            dve.wait_ge(slots_ready, 1)
            n_most = dve.value_load(most_i[0:1, 0:1], min_val=0, max_val=SEQ)
            with dve.If(n_most > P):
                V.tensor_scalar(slot[:, :, :], slot[:, :, :], float(P), None, ALU.subtract).then_inc(slots_ready, 1)
                dve.wait_ge(slots_ready, 2)
                with dve.Fori(0, NE) as e:
                    expert(e, e * FU + NE * FU, e + NE, e * STEPS + NE * STEPS, e + NE)

            for c in range(NCH):
                link(V.tensor_tensor(yacc[:, c, :], yacc[:, c, :], gate2[:], ALU.mult))
                V.tensor_tensor(x_sb[:, c, :], x_sb[:, c, :], yacc[:, c, :], ALU.add).then_inc(x_ready, 1)
            dve.wait_ge(s_fing, 16)
            for c in range(NCH):
                dve.wait_ge(ss_ready, 8 + c + 1)
                rsqrt(ssq[:, c:c + 1], c, c + 1, 1.0 / D_MODEL)
                V.scalar_tensor_tensor(out=yacc[:, c, :], in0=x_sb[:, c, :], scalar=rstd[:, c:c + 1], in1=y_ev[:],
                                       op0=ALU.mult, op1=ALU.mult).then_inc(fin_ready, 1)

        @block.tensor
        def _(pe):
            mm, tr = nc.tensor.matmul, nc.tensor.transpose

            def in_unit(w, half, banks, chunks):
                wh, wl = hi[w % SPLIT_RING], lo[w % SPLIT_RING]
                for c in range(chunks):
                    o = bank[banks[c]][:]
                    for kk in range(4):
                        kt = 4 * half + kk
                        ah, al = h_hi[:, kt, P * c:P * c + P], h_lo[:, kt, P * c:P * c + P]
                        cols = slice(512 * kk, 512 * kk + 512)
                        mm(o, ah, wh[:, cols], start=kt == 0, stop=False)
                        mm(o, ah, wl[:, cols], start=False, stop=False)
                        last = mm(o, al, wh[:, cols], start=False, stop=kt == KT - 1)
                last.then_inc(units_pe, 1)

            def down_unit(w, parity, first, final, chunks):
                wh, wl = hi[w % SPLIT_RING], lo[w % SPLIT_RING]
                for c in range(chunks):
                    for kk in range(2):
                        ah, al = (a[:, parity, kk, P * c:P * c + P] for a in (a_hi, a_lo))
                        for half in range(2):
                            o = bank[4 + 2 * c + half][:]
                            cols = slice(1024 * kk + 512 * half, 1024 * kk + 512 * half + 512)
                            mm(o, ah, wh[:, cols], start=first and kk == 0, stop=False)
                            mm(o, ah, wl[:, cols], start=False, stop=False)
                            last = mm(o, al, wh[:, cols], start=False, stop=final and kk == 1)
                last.then_inc(units_pe, 1)

            def unit_here(w):
                pe.wait_ge(units_dve, W_AT[w] + 1)

            def tile_of(a, c, kt):
                return a[:, c, :].rearrange("p (q k) -> p k q", k=KT)[:, kt, :]

            def norm_transposes(k):
                for j in range(4):
                    c, half = divmod(j, 2)
                    pe.wait_ge(xn_ready, 2 * k + c + 1)
                    for q in range(4):
                        kt = 4 * half + q
                        last = tr(bank[4 + j][:, P * q:P * q + P], tile_of(xn, c, kt), ident)
                    last.then_inc(tr_ready, 1)

            def ada_sum(k):
                pe.wait_ge(units_dve, A_AT[2 * k + 1] + 1)
                if k:
                    pe.wait_ge(mod_ready, k)
                a = acc[:, k % 2, :]
                if (k % 12) // 2 in (2, 5):
                    mm(bank[ADA_BANK][:], ones, a, start=True, stop=True).then_inc(acc_summed, 1)
                else:
                    rows = slice(64 * (k % 2), 64 * (k % 2) + 64)
                    cols = a.rearrange("p (q k) -> p k q", k=KT)
                    for kt in range(KT):
                        last = mm(bank[ADA_BANK][rows, kt:kt + 1], cols[:, kt, :], ones[:, 0:1], start=True, stop=True)
                    last.then_inc(acc_summed, 1)

            pe.wait_ge(s_cst, 16)
            norm_transposes(0)
            for k in range(4):
                ada_sum(k)

            def weights_transposed():
                pe.wait_ge(ws_masked, 1)
                pe.wait_ge(h_ready, 4)
                tr(bank[7][:, 0:8], bs_rows[0:8, :], ident[0:8, 0:8])
                for g in range(8):
                    last = tr(bank[5 + g // 4][:, P * (g % 4):P * (g % 4) + P], ws_raw[:, g, :], ident)
                last.then_inc(ws_tr, 1)

            def spatial(j):
                pe.wait_ge(v_ready, j + 1)
                pe.wait_ge(ws_ready, 2)
                if j:
                    pe.wait_ge(y_blk, j)
                for c in range(NCH):
                    for g in range(2):
                        last = mm(bank[5 + c][:, 256 * g:256 * g + 256], ws_t[:, 2 * j + g, :],
                                  v_sb[:, c, 512 * j + 256 * g:512 * j + 256 * g + 256], start=True, stop=True)
                last.then_inc(fv_done, 1)

            weights_transposed()
            for b in range(8):
                if b >= 2:
                    pe.wait_ge(gelu_done, 2 * (b - 1))
                for half in range(2):
                    w = W_SGU_IN + 2 * b + half
                    unit_here(w)
                    in_unit(w, half, BLOCK_BANKS[b % 2], NCH)
                    if half == 0 and b % 2 == 0 and b:
                        ada_sum(4 + b // 2 - 1)
                if b == 7:
                    ada_sum(7)
                if b >= 6:
                    spatial(b - 6)
            spatial(2)
            spatial(3)

            def down_transposes(j, src, b, t):
                for kk in range(2):
                    for c in range(NCH):
                        n = SEQ * kk + P * c
                        last = tr(bank[b][:, n:n + P], src[:, c, 256 * j + P * kk:256 * j + P * kk + P], ident)
                last.then_inc(t_done, 1)

            def down_phase(w0, t0, src, ready, sums):
                for j in range(8 + 1):
                    if j < 8:
                        if j % 2 == 0:
                            pe.wait_ge(ready, j // 2 + 1)
                        if j >= 2:
                            pe.wait_ge(at_ready, t0 + j - 1)
                        down_transposes(j, src, (2, 0)[j % 2], t0)
                    if j >= 1:
                        w, i = w0 + j - 1, t0 + j - 1
                        unit_here(w)
                        pe.wait_ge(at_ready, i + 1)
                        if j == 1:
                            pe.wait_ge(ready, 4)
                        down_unit(w, i % 2, j == 1, j == 8, NCH)
                        if j in sums:
                            ada_sum(sums[j])

            pe.wait_ge(gelu_done, 16)
            down_phase(W_SGU_OUT, T_SGU, u_sb, y_blk, {1: 8, 3: 9, 5: 10, 7: 11})

            norm_transposes(1)
            pe.wait_ge(h_ready, 8)

            def ffn_transposes(s, tile, chunks):
                for kk in range(2):
                    for c in range(chunks):
                        n = P * (chunks * kk + c)
                        last = tr(bank[2][:, n:n + P], tile[:, s % 2, c, P * kk:P * kk + P], ident)
                last.then_inc(t_done, 1)

            for u, kind, s in FFN_ORDER:
                w = W_FFN + u
                if kind == "A" and s:
                    pe.wait_ge(act_ready, s)
                if kind == "D":
                    if s == STEPS - 1:
                        pe.wait_ge(act_ready, STEPS)
                        pe.wait_ge(at_ready, T_FFN + s)
                        ffn_transposes(s, fact, NCH)
                    pe.wait_ge(at_ready, T_FFN + s + 1)
                unit_here(w)
                if kind == "D":
                    down_unit(w, s % 2, s == 0, s == STEPS - 1, NCH)
                else:
                    in_unit(w, int(kind == "B"), (0, 1), NCH)
                if kind == "B" and s:
                    pe.wait_ge(act_ready, s)
                    pe.wait_ge(at_ready, T_FFN + s - 1)
                    ffn_transposes(s - 1, fact, NCH)
                if kind == "A" and s >= 2 and s % 2 == 0 and s <= 8:
                    ada_sum(12 + s // 2 - 1)

            norm_transposes(2)
            pe.wait_ge(h_ready, 12)

            def qk_transposes(b):
                for c in range(NCH):
                    pe.wait_ge(rope_done, 2 * b + c + 1)
                    if b:
                        pe.wait_ge(qk_ready, 2 * (b - 1) + c + 1)
                    for i in range(4):
                        last = tr(bank[5 + c][:, P * i:P * i + P], rope[:, c, P * i:P * i + P], ident)
                    last.then_inc(qk_tr, 1)

            def scores(h):
                pe.wait_ge(qk_ready, 8)
                if h:
                    pe.wait_ge(sct_ready, h)
                for o, keys, queries in (((0, 256), (0, P), (0, SEQ)), ((256, 384), (P, SEQ), (P, SEQ))):
                    for kk in range(2):
                        last = mm(bank[5][:, o[0]:o[1]], k_t[:, 2 * h + kk, keys[0]:keys[1]],
                                  q_t[:, 2 * h + kk, queries[0]:queries[1]], start=kk == 0, stop=kk == 1)
                last.then_inc(scores_done, 1)

            def head_outputs(h):
                pe.wait_ge(sct_ready, h + 1)
                pe.wait_ge(ret_act, 8)
                if h:
                    pe.wait_ge(og_done, h)
                v0, v1 = (rv[:, c, 512 * h:512 * h + 512] for c in range(NCH))
                mm(bank[6][:], sc_t[:, 0:P], v0, start=True, stop=True)
                mm(bank[7][:], sc_t[:, P:256], v0, start=True, stop=False)
                mm(bank[7][:], sc_t[:, 256:384], v1, start=False, stop=True).then_inc(o_done, 1)

            for b in range(12):
                if 2 <= b < 6:
                    pe.wait_ge(rope_done, 2 * (b - 1))
                elif b >= 6:
                    pe.wait_ge(ret_act, 2 * (b - 5))
                if b >= 8:
                    scores(b - 8)
                for half in range(2):
                    w = W_RET_IN + 2 * b + half
                    unit_here(w)
                    in_unit(w, half, BLOCK_BANKS[b % 2], NCH)
                    if half == 0 and b % 2 == 0 and b:
                        ada_sum(16 + b // 2 - 1)
                if 1 <= b <= 4:
                    qk_transposes(b - 1)
                if b >= 8:
                    head_outputs(b - 8)
            ada_sum(21)
            pe.wait_ge(ret_act, 16)
            down_phase(W_RET_OUT, T_RET, rv, og_done, {1: 22, 3: 23})

            norm_transposes(3)
            pe.wait_ge(val_ready, 16)
            pe.wait_ge(s_wr, 32)
            pe.wait_ge(mod_ready, 24)
            for c in range(NCH):
                for kt in range(KT):
                    last = mm(bank[ADA_BANK][:, 8 * c:8 * c + 8], val_t[:, kt, P * c:P * c + P], wr[:, kt, :],
                              start=kt == 0, stop=kt == KT - 1)
            last.then_inc(router_done, 1)
            pe.wait_ge(sel_ready, 1)
            b3 = bank[ADA_BANK]
            mm(b3[:, 0:8], utri, m_sel[:, 0, :], start=True, stop=True)
            mm(b3[:, 8:16], utri, m_sel[:, 1, :], start=True, stop=False)
            mm(b3[:, 8:16], ones, m_sel[:, 0, :], start=False, stop=True)
            mm(b3[:, 16:24], ones, m_sel[:, 0, :], start=True, stop=False)
            mm(b3[:, 16:24], ones, m_sel[:, 1, :], start=False, stop=True).then_inc(pos_done, 1)
            pe.wait_ge(slots_ready, 1)

            def expert(e, units, steps, one):
                pe.wait_ge(pick_ready, one + 1)
                for kt in range(KT):
                    for c in range(NCH):
                        last = mm(bank[6 + kt // 4][:, P * (kt % 4):P * (kt % 4) + P], tile_of(xn, c, kt),
                                  pick[:, c, :], start=c == 0, stop=c == NCH - 1)
                last.then_inc(gathered, 1)
                for c in range(NCH):
                    last = tr(bank[3][:, P * c:P * c + P], pick[:, c, :], ident)
                last.then_inc(pick_tr, 1)
                pe.wait_ge(g_ready, one + 1)
                for u, kind, s in FFN_ORDER:
                    w = W_MOE + u
                    if kind == "A":
                        pe.wait_ge(act_ready, steps + (STEPS + max(0, s - 1)))
                    if kind == "D":
                        if s == STEPS - 1:
                            pe.wait_ge(act_ready, steps + (STEPS + STEPS))
                            pe.wait_ge(at_ready, steps + (T_DENSE + s))
                            ffn_transposes(s, mact, 1)
                        pe.wait_ge(at_ready, steps + (T_DENSE + s + 1))
                    pe.wait_ge(units_dve, units + (N_DENSE + u + 1))
                    if kind == "D":
                        down_unit(w, s % 2, s == 0, s == STEPS - 1, 1)
                    else:
                        in_unit(w, int(kind == "B"), (s % 2,), 1)
                    if kind == "B" and s:
                        pe.wait_ge(act_ready, steps + (STEPS + s))
                        pe.wait_ge(at_ready, steps + (T_DENSE + s - 1))
                        ffn_transposes(s - 1, mact, 1)
                pe.wait_ge(y_out, one * 2 + 2)
                pe.wait_ge(pick_t_ready, one + 1)
                for c in range(NCH):
                    for half in range(2):
                        last = mm(bank[(6, 4)[c] + half][:], pick_t[:, c, :], y_ev[:, 512 * half:512 * half + 512],
                                  start=True, stop=True)
                    last.then_inc(scattered, 1)

            with pe.Fori(0, NE) as e:
                expert(e, e * FU, e * STEPS, e)
            n_most = pe.value_load(most_i[0:1, 0:1], min_val=0, max_val=SEQ)
            with pe.If(n_most > P):
                with pe.Fori(0, NE) as e:
                    expert(e, e * FU + NE * FU, e * STEPS + NE * STEPS, e + NE)


def constants():
    i = np.arange(P)
    cst = np.stack([np.eye(P), np.ones((P, P)), np.tile(i, (P, 1)), i[:, None] < i[None, :]], axis=1)
    log_gamma = np.log1p(-np.exp2(-5.0 - np.arange(HEADS)))
    rel = (i[None, :] - i[:, None])[:, None, :]
    lg = log_gamma[None, :, None]
    intra = np.where(rel >= 0, np.exp(lg * np.maximum(rel, 0)), 0.0)
    cross = np.exp(lg * (P + rel))
    decay = np.concatenate([intra, cross], axis=2) * DK ** -0.5
    inv_freq = 1.0 / (np.float32(10000.0) ** (np.arange(0, DK, 2, dtype=np.float32) / np.float32(DK)))
    return {"consts": cst.reshape(P, 4 * P).astype(np.float32), "decay": decay.reshape(P, -1).astype(np.float32),
            "inv_freq": inv_freq.reshape(1, P).astype(np.float32)}


_INS = ["x", "c", "positions", "ada_w", "ada_b", "mix_norm_g", "ffn_norm_g", "sgu_w_in", "sgu_ln_g", "sgu_ln_b",
        "sgu_w_s", "sgu_b_s", "sgu_w_out", "ffn_w_gate_up", "ffn_w_down", "ret_w_in", "ret_w_out", "moe_w_router",
        "moe_b_router", "moe_w_gate_up", "moe_w_down", "final_norm_g"]


def kernel(**inputs):
    import concourse.bacc as _bacc
    from concourse.bass_utils import run_bass_kernel_spmd as _run

    nc = _bacc.Bacc("TRN2", target_bir_lowering=False, num_devices=1)
    arrays, t = {}, {}
    for name, a in [*((n, inputs[n]) for n in _INS), *constants().items()]:
        a = np.ascontiguousarray(a)
        arrays[f"in_{name}"] = a
        t[name] = nc.dram_tensor(f"in_{name}", a.shape, mybir.dt.from_np(a.dtype), kind="ExternalInput").ap()
    out = nc.dram_tensor("out", (1, SEQ, D_MODEL), mybir.dt.float32, kind="ExternalOutput").ap()
    trunk(nc, t, out)
    return _run(nc, [arrays], core_ids=[0]).results[0]["out"]
```

```python
import concourse.bass as bass
from concourse import mybir
from contextlib import ExitStack
import numpy as np

P = 128
D_MODEL = 1024
SEQ = 256
NCH = SEQ // P
KT = D_MODEL // P
SGU = 2 * D_MODEL
HEADS, DK, DV = 4, 256, 512
RET_IN = 2 * HEADS * DK + 2 * HEADS * DV
FFN = ((8 * D_MODEL // 3 + 127) // 128) * 128
NE = 8
EPS = 1e-6
UNIT = 2048
STEPS = FFN // 256
FU = 3 * STEPS
DENSE_RING, MOE_RING, SPLIT_RING = 9, 11, 3
MAGIC = 1.5 * 2.0 ** 23
TWO_PI_HI, TWO_PI_MID = 6.28125, 0.0019350051879882812
TWO_PI_LO = 2 * np.pi - TWO_PI_HI - TWO_PI_MID
SIN_MAX = 3.1415925


def ffn_unit(kind, s):
    if kind == "D":
        return 3 * s + 6 if s <= STEPS - 3 else FU - STEPS + s
    return 2 * s + max(0, s - 2) + (kind == "B")


FFN_ORDER = sorted([(ffn_unit(k, s), k, s) for k in "ABD" for s in range(STEPS)])

W_SGU_IN = 0
W_SGU_OUT = W_SGU_IN + 16
W_FFN = W_SGU_OUT + 8
W_RET_IN = W_FFN + FU
W_RET_OUT = W_RET_IN + 24
W_MOE = W_RET_OUT + 8


def dense_stream():
    out, a, w = [], 0, 0

    def ada(n):
        nonlocal a
        for _ in range(n):
            out.append(("A", a // 2, a % 2))
            a += 1

    def split(n):
        nonlocal w
        for _ in range(n):
            out.append(("W", w))
            w += 1
    ada(8)
    for _ in range(8):
        split(2)
        ada(1)
    for _ in range(8):
        split(1)
        ada(1)
    for u, k, s in FFN_ORDER:
        split(1)
        if k == "B" and s < 8:
            ada(1)
    for _ in range(12):
        split(2)
        ada(1)
    for j in range(8):
        split(1)
        if j < 4:
            ada(1)
    return out


STREAM = dense_stream()
N_DENSE = len(STREAM)
W_AT = {u[1]: n for n, u in enumerate(STREAM) if u[0] == "W"}
A_AT = {2 * u[1] + u[2]: n for n, u in enumerate(STREAM) if u[0] == "A"}
SLOT_ORDER = [(N_DENSE + i) % DENSE_RING for i in range(DENSE_RING)] + [9, 10]
BLOCK_BANKS = [(0, 1), (2, 4)]
ADA_BANK = 3


def trunk(nc, t, out):
    f32, f32r, i32, u32 = mybir.dt.float32, mybir.dt.float32r, mybir.dt.int32, mybir.dt.uint32
    ALU, ACT, AX = mybir.AluOpType, mybir.ActivationFunctionType, mybir.AxisListType
    ctx = ExitStack()
    with ctx:
        base = nc.sbuf_base if not callable(nc.sbuf_base) else nc.sbuf_base()
        base = (base + 63) // 64 * 64

        def at(name, shape, dt, off):
            return nc.alloc_sbuf_tensor_at(name, [P, *shape], dt, offset=base + off)

        def sem(name):
            return ctx.enter_context(nc.semaphore(name))

        KB = 1024
        RAW0, HI0, LO0 = 0, 88 * KB, 112 * KB
        X0, HTH0, HTL0, BIG0 = 136 * KB, 144 * KB, 152 * KB, 160 * KB
        ATH0, ATL0, F0 = 192 * KB, 196 * KB, 200 * KB
        E0 = RAW0 + 9 * 8 * KB
        raw = [at(f"raw{i}", [UNIT], f32, RAW0 + 8 * KB * i) for i in range(MOE_RING)]
        hi = [at(f"hi{i}", [UNIT], f32r, HI0 + 8 * KB * i) for i in range(SPLIT_RING)]
        lo = [at(f"lo{i}", [UNIT], f32r, LO0 + 8 * KB * i) for i in range(SPLIT_RING)]
        x_sb = at("x_sb", [NCH, D_MODEL], f32, X0)
        h_hi = at("h_hi", [KT, SEQ], f32r, HTH0)
        h_lo = at("h_lo", [KT, SEQ], f32r, HTL0)
        a_hi = at("a_hi", [2, 2, SEQ], f32r, ATH0)
        a_lo = at("a_lo", [2, 2, SEQ], f32r, ATL0)
        acc = at("acc", [2, 512], f32, E0)
        acc0 = at("acc0", [2, 512], f32, E0 + 4 * KB)
        gate1 = at("gate1", [D_MODEL], f32, E0 + 8 * KB)
        ws_t = at("ws_t", [8, P], f32, E0 + 12 * KB)
        trig = at("trig", [2, NCH, P], f32, E0 + 12 * KB)
        squares_o = at("squares_o", [512], f32, E0 + 12 * KB)
        sc_t = at("sc_t", [384], f32, E0 + 14 * KB)
        rope_tmp = at("rope_tmp", [2, P], f32, E0 + 14 * KB)
        xn = at("xn", [NCH, D_MODEL], f32, BIG0)
        u_sb = at("u_sb", [NCH, SGU], f32, BIG0)
        v_sb = at("v_sb", [NCH, SGU], f32, BIG0 + 16 * KB)
        bs_rows = at("bs_rows", [P], f32, BIG0 + 12 * KB)
        ws_raw = at("ws_raw", [8, P], f32, BIG0 + 8 * KB)
        fact = at("fact", [2, NCH, 256], f32, BIG0 + 8 * KB)
        rv = at("rv", [NCH, SGU], f32, BIG0)
        q_t = at("q_t", [8, SEQ], f32, BIG0 + 16 * KB)
        k_t = at("k_t", [8, SEQ], f32, BIG0 + 24 * KB)
        yacc = at("yacc", [NCH, D_MODEL], f32, BIG0 + 8 * KB)
        y_ev = at("y_ev", [D_MODEL], f32, BIG0 + 16 * KB)
        pick = at("pick", [NCH, P], f32, BIG0 + 20 * KB)
        pick_t = at("pick_t", [NCH, P], f32, BIG0 + 21 * KB)
        mact = at("mact", [2, NCH, 256], f32, BIG0 + 22 * KB)
        gval = at("gval", [KT, P], f32, BIG0 + 26 * KB)
        out_tmp = at("out_tmp", [4, 512], f32, BIG0 + 16 * KB)
        fin = at("fin", [D_MODEL], f32, HTH0)
        val_t = at("val_t", [KT, SEQ], f32, ATH0)
        ln_rows = at("ln_rows", [2, 2, 512], f32, ATH0)
        decay = at("decay", [HEADS, 256], f32, ATH0)
        rope = at("rope", [NCH, 512], f32, ATL0)
        silu_g = at("silu_g", [NCH, 512], f32, ATL0)
        gate2 = at("gate2", [D_MODEL], f32, F0)
        cst = at("cst", [4, P], f32, F0 + 4 * KB)
        small = [F0 + 6 * KB]

        def little(name, shape, dt=f32):
            n = int(np.prod(shape)) * 4
            small[0] += (-small[0]) % 32
            r = at(name, shape, dt, small[0])
            small[0] += n
            return r
        ident, ones, iota, utri = (cst[:, i, :] for i in range(4))
        vecs = little("vecs", [40])
        sc = little("sc", [KT])
        mods = little("mods", [2, 4, KT])
        mulv = little("mulv", [KT])
        ssq = little("ssq", [NCH])
        rstd = little("rstd", [NCH])
        bs_t = little("bs_t", [8])
        stats = little("stats", [NCH, 4, 6])
        mv = little("mv", [NCH, 2])
        oss = little("oss", [NCH])
        root = little("root", [NCH])
        step_t = little("step_t", [NCH])
        warm = little("warm", [1])
        pos_i = little("pos_i", [NCH], i32)
        pos_f = little("pos_f", [NCH])
        wr = little("wr", [KT, NE])
        brow = little("brow", [NE])
        logit = at("logit", [NCH, NE], f32, BIG0 + 30 * KB)
        top = at("top", [NCH, 8], f32, BIG0 + 30 * KB + 64)
        topi = at("topi", [NCH, 8], u32, BIG0 + 30 * KB + 128)
        topf = at("topf", [NCH, 8], f32, BIG0 + 30 * KB + 192)
        oh = at("oh", [2, NCH, NE], f32, BIG0 + 30 * KB + 256)
        wts = at("wts", [NCH, 4], f32, BIG0 + 30 * KB + 384)
        m_sel = little("m_sel", [NCH, NE])
        gates = little("gates", [NCH, NE + 1])
        slot = little("slot", [NCH, NE + 1])
        most = little("most", [1])
        most_i = little("most_i", [1], i32)
        assert base + small[0] <= nc.sbuf_usable_end, (base, small[0], nc.sbuf_usable_end)

        bank = [ctx.enter_context(nc.psum_tensor(f"bank{i}", [P, 512], f32)) for i in range(8)]

        raw_full = [sem(f"raw_full{i}") for i in range(MOE_RING)]
        split_hi, units_dve, units_pe, first_chunk = (
            sem(n) for n in ("split_hi", "units_dve", "units_pe", "first_chunk"))
        acc0_full = [sem(f"acc0_full{i}") for i in range(2)]
        acc0_zero, acc0_used, acc_summed, mod_ready = (
            sem(n) for n in ("acc0_zero", "acc0_used", "acc_summed", "mod_ready"))
        s_cst, s_x, s_vec, s_ws, s_pos, s_invf, s_decay, s_wr, s_fing, s_out = (
            sem(n) for n in ("s_cst", "s_x", "s_vec", "s_ws", "s_pos", "s_invf", "s_decay", "s_wr", "s_fing", "s_out"))
        ln_full = [sem(f"ln_full{i}") for i in range(2)]
        sc_ready, var_ready, root_ready = sem("sc_ready"), sem("var_ready"), sem("root_ready")
        ws_masked, ws_tr, ws_ready = sem("ws_masked"), sem("ws_tr"), sem("ws_ready")
        x_ready, ss_ready, xn_ready, tr_ready, val_ready, h_hi_ready, h_ready = (
            sem(n) for n in ("x_ready", "ss_ready", "xn_ready", "tr_ready", "val_ready", "h_hi_ready", "h_ready"))
        gelu_done, v_norm, v_ready, fv_done, y_blk = (
            sem(n) for n in ("gelu_done", "v_norm", "v_ready", "fv_done", "y_blk"))
        t_done, at_hi, at_ready, silu_done, act_ready = (
            sem(n) for n in ("t_done", "at_hi", "at_ready", "silu_done", "act_ready"))
        ang_ready, trig_ready, rope_done, qk_tr, qk_ready, ret_act, scores_done, sct_ready, o_done, o_ss, og_done = (
            sem(n) for n in ("ang_ready", "trig_ready", "rope_done", "qk_tr", "qk_ready", "ret_act", "scores_done",
                             "sct_ready", "o_done", "o_ss", "og_done"))
        router_done, top_ready, exp_done, sel_ready, pos_done, slots_ready = (
            sem(n) for n in ("router_done", "top_ready", "exp_done", "sel_ready", "pos_done", "slots_ready"))
        pick_ready, pick_tr, pick_t_ready, gathered, gval_ready, g_hi_ready, g_ready, y_out, scattered, yacc_done = (
            sem(n) for n in ("pick_ready", "pick_tr", "pick_t_ready", "gathered", "gval_ready", "g_hi_ready",
                             "g_ready", "y_out", "scattered", "yacc_done"))
        dve_seq, fin_ready, yacc_zero, v_scaled = (
            sem(n) for n in ("dve_seq", "fin_ready", "yacc_zero", "v_scaled"))

        T_DENSE = 8 + STEPS + 8
        T_SGU, T_FFN, T_RET = 0, 8, 8 + STEPS

        def rhs(tile, kk, n0, n1, width):
            return tile[:, kk * width + n0:kk * width + n1]

        block = ctx.enter_context(nc.Block())

        @block.sync
        def _(sp):
            def ada_source(k, half):
                layer, b = divmod(k, 12)
                return columns(t["ada_w"][layer], b, half)

            def columns(w, b, half):
                return w.rearrange("(p k) n -> p k n", p=P)[:, 4 * half:4 * half + 4, 512 * b:512 * b + 512]

            def rows(w, j):
                return w[256 * j:256 * j + 256, :].rearrange("(k p) n -> p k n", p=P)

            def ffn_load(dst, gate_up, down, kind, s, full):
                if kind == "D":
                    sp.dma_start(dst[:].rearrange("p (k n) -> p k n", k=2), rows(down, s)).then_inc(full, 16)
                    return
                half = int(kind == "B")
                src = gate_up.rearrange("(p k) (g n) -> p (k g) n", p=P, g=2)
                sp.dma_start(dst[:].rearrange("p (k n) -> p k n", k=8),
                             src[:, 8 * half:8 * half + 8, 256 * s:256 * s + 256]).then_inc(full, 16)

            for k in range(4):
                g = t[("mix_norm_g", "ffn_norm_g")[k % 2]][k // 2]
                sp.dma_start(vecs[:, 8 * k:8 * k + 8], g.rearrange("(p k) -> p k", p=P)).then_inc(s_vec, 16)
            sp.dma_start(vecs[:, 32:40], t["c"].rearrange("a (p k) -> p (a k)", p=P)).then_inc(s_vec, 16)
            sp.dma_start(cst[:], t["consts"].rearrange("p (k n) -> p k n", k=4)).then_inc(s_cst, 16)
            for n, unit in enumerate(STREAM):
                slot_n, full = raw[n % DENSE_RING], raw_full[n % DENSE_RING]
                if n >= DENSE_RING:
                    sp.wait_ge(units_dve, n - DENSE_RING + 1)
                if unit[0] == "A":
                    _, k, half = unit
                    if half == 0:
                        if k < 2:
                            sp.wait_ge(acc0_zero, 1)
                        else:
                            sp.wait_ge(acc0_used, k - 1)
                        layer, b = divmod(k, 12)
                        sp.dma_start(acc0[0:1, k % 2, :], t["ada_b"][layer:layer + 1, 512 * b:512 * b + 512]) \
                            .then_inc(acc0_full[k % 2], 16)
                    sp.dma_start(slot_n[:].rearrange("p (k n) -> p k n", k=4), ada_source(k, half)).then_inc(full, 16)
                else:
                    w = unit[1]
                    if w < W_SGU_OUT:
                        b, half = divmod(w - W_SGU_IN, 2)
                        col = (b + 4) % 8
                        sp.dma_start(slot_n[:].rearrange("p (k n) -> p k n", k=4),
                                     columns(t["sgu_w_in"][0], col, half)).then_inc(full, 16)
                    elif w < W_FFN:
                        sp.dma_start(slot_n[:].rearrange("p (k n) -> p k n", k=2),
                                     rows(t["sgu_w_out"][0], w - W_SGU_OUT)).then_inc(full, 16)
                    elif w < W_RET_IN:
                        _, kind, s = FFN_ORDER[w - W_FFN]
                        ffn_load(slot_n, t["ffn_w_gate_up"][0], t["ffn_w_down"][0], kind, s, full)
                    elif w < W_RET_OUT:
                        b, half = divmod(w - W_RET_IN, 2)
                        sp.dma_start(slot_n[:].rearrange("p (k n) -> p k n", k=4),
                                     columns(t["ret_w_in"][0], b, half)).then_inc(full, 16)
                    else:
                        sp.dma_start(slot_n[:].rearrange("p (k n) -> p k n", k=2),
                                     rows(t["ret_w_out"][0], w - W_RET_OUT)).then_inc(full, 16)
                if n == 1:
                    sp.dma_start(x_sb[:], t["x"].rearrange("a (c p) n -> p (a c) n", p=P)).then_inc(s_x, 16)
                    sp.dma_start(bs_rows[0:8, :], t["sgu_b_s"][0]).then_inc(s_ws, 16)
                    sp.dma_start(ws_raw[:], t["sgu_w_s"][0].rearrange("g p s -> p g s")).then_inc(s_ws, 16)
                    sp.dma_start(pos_i[:], t["positions"].rearrange("a (c p) -> p (a c)", p=P),
                                 allow_slow_non_contiguous=True).then_inc(s_pos, 16)
                    sp.dma_start(wr[:], t["moe_w_router"][0].rearrange("(p k) n -> p k n", p=P)).then_inc(s_wr, 16)
                    sp.dma_start(brow[:], t["moe_b_router"][0:1, :].to_broadcast([P, NE])).then_inc(s_wr, 16)
                if unit == ("W", W_SGU_IN + 4):
                    sp.wait_ge(h_ready, 4)
                    for j in range(2):
                        for i, name in enumerate(("sgu_ln_g", "sgu_ln_b")):
                            sp.dma_start(ln_rows[:, j, i, :], t[name][0:1, 512 * j:512 * j + 512]
                                         .to_broadcast([P, 512])).then_inc(ln_full[j], 16)
                if unit in (("W", W_SGU_IN + 12), ("W", W_SGU_IN + 14)):
                    j = 2 + (unit[1] - W_SGU_IN - 12) // 2
                    sp.wait_ge(v_ready, j - 1)
                    for i, name in enumerate(("sgu_ln_g", "sgu_ln_b")):
                        sp.dma_start(ln_rows[:, j % 2, i, :], t[name][0:1, 512 * j:512 * j + 512]
                                     .to_broadcast([P, 512])).then_inc(ln_full[j % 2], 16)
                if unit == ("W", W_FFN + 4):
                    sp.wait_ge(y_blk, 4)
                    sp.dma_start(trig[:, 0, 0, :], t["inv_freq"].to_broadcast([P, P])).then_inc(s_invf, 16)
                if unit == ("W", W_RET_IN + 4):
                    sp.wait_ge(h_ready, 12)
                    sp.dma_start(decay[:], t["decay"].rearrange("p (h n) -> p h n", h=HEADS)).then_inc(s_decay, 16)

            def expert_load(e, u, kind, s):
                gu = t["moe_w_gate_up"][0][bass.ds(e, 1)].rearrange("a k n -> (a k) n")
                dn = t["moe_w_down"][0][bass.ds(e, 1)].rearrange("a k n -> (a k) n")
                k = SLOT_ORDER[u % MOE_RING]
                ffn_load(raw[k], gu, dn, kind, s, raw_full[k])

            for u, kind, s in FFN_ORDER[:MOE_RING]:
                if u < DENSE_RING:
                    sp.wait_ge(units_dve, N_DENSE + u - DENSE_RING + 1)
                elif u == DENSE_RING:
                    sp.wait_ge(mod_ready, 24)
                    sp.wait_ge(x_ready, 6)
                expert_load(0, u, kind, s)
            with sp.Fori(0, NE - 1) as e:
                for u, kind, s in FFN_ORDER[MOE_RING:]:
                    sp.wait_ge(units_dve, e * FU + (N_DENSE + u - MOE_RING + 1))
                    expert_load(e, u, kind, s)
                for u, kind, s in FFN_ORDER[:MOE_RING]:
                    sp.wait_ge(units_dve, e * FU + (N_DENSE + FU + u - MOE_RING + 1))
                    expert_load(e + 1, u, kind, s)
            for u, kind, s in FFN_ORDER[MOE_RING:]:
                sp.wait_ge(units_dve, (NE - 1) * FU + N_DENSE + u - MOE_RING + 1)
                expert_load(NE - 1, u, kind, s)
            sp.wait_ge(slots_ready, 1)
            n_most = sp.value_load(most_i[0:1, 0:1], min_val=0, max_val=SEQ)
            with sp.If(n_most > P):
                with sp.Fori(0, NE) as e:
                    for u, kind, s in FFN_ORDER:
                        sp.wait_ge(units_dve, e * FU + (NE * FU + N_DENSE + u - MOE_RING + 1))
                        expert_load(e, u, kind, s)
            sp.wait_ge(x_ready, 7)
            sp.dma_start(y_ev[:], t["final_norm_g"].rearrange("(a n) -> a n", a=1).to_broadcast([P, D_MODEL])) \
                .then_inc(s_fing, 16)
            for c in range(NCH):
                sp.wait_ge(fin_ready, c + 1)
                sp.dma_start(out[0, P * c:P * c + P, :], yacc[:, c, :]).then_inc(s_out, 16)
            sp.wait_ge(s_out, 16 * NCH)

        def raw_times(n):
            return 16 * (n // DENSE_RING + 1)

        def moe_raw_times(k, u, experts):
            before = sum(1 for n in range(N_DENSE) if n % DENSE_RING == k) if k < DENSE_RING else 0
            return experts * (16 * FU // MOE_RING) + 16 * (before + u // MOE_RING + 1)

        @block.scalar
        def _(act):
            copy = ACT.Copy
            roots = [0]

            def take_root(c0, c1):
                act.wait_ge(var_ready, roots[0] + 1)
                nc.scalar.activation(root[:, c0:c1], rstd[:, c0:c1], ACT.Sqrt).then_inc(root_ready, 1)
                roots[0] += 1

            def split(w):
                n = W_AT[w]
                act.wait_ge(raw_full[n % DENSE_RING], raw_times(n))
                if w >= SPLIT_RING:
                    act.wait_ge(units_pe, w - SPLIT_RING + 1)
                nc.scalar.activation(hi[w % SPLIT_RING][:], raw[n % DENSE_RING][:], copy).then_inc(split_hi, 1)

            def moe_split(u, e_units, experts):
                k, w = SLOT_ORDER[u % MOE_RING], W_MOE + u
                act.wait_ge(raw_full[k], moe_raw_times(k, u, experts))
                act.wait_ge(units_pe, e_units + (w - SPLIT_RING + 1))
                nc.scalar.activation(hi[w % SPLIT_RING][:], raw[k][:], copy).then_inc(split_hi, 1)

            def squares(k, c):
                if k == 0:
                    act.wait_ge(s_x, 16)
                else:
                    act.wait_ge(x_ready, 2 * (k - 1) + c + 1)
                nc.scalar.activation(xn[:, c, :], x_sb[:, c, :], ACT.Square, accum_out=ssq[:, c:c + 1]) \
                    .then_inc(ss_ready, 1)

            def norm_hi(k, c):
                for half in range(2):
                    act.wait_ge(val_ready, 4 * k + 2 * c + half + 1)
                    nc.scalar.activation(h_hi[:, 4 * half:4 * half + 4, P * c:P * c + P],
                                         val_t[:, 4 * half:4 * half + 4, P * c:P * c + P], copy).then_inc(h_hi_ready, 1)

            def root_table():
                nc.scalar.activation(warm[:], ones[:, 0:1], ACT.Sqrt)

            def norm(k, w):
                root_table()
                squares(k, 0)
                take_root(0, 1)
                squares(k, 1)
                norm_hi(k, 0)
                split(w)
                take_root(1, 2)
                norm_hi(k, 1)

            def down_hi(i, psum, free):
                act.wait_ge(t_done, i + 1)
                if free is not None:
                    act.wait_ge(units_pe, free)
                nc.scalar.activation(a_hi[:, (i - T_SGU) % 2, :, :], psum[:].rearrange("p (k n) -> p k n", k=2),
                                     copy).then_inc(at_hi, 1)

            act.wait_ge(s_vec, 80)
            nc.scalar.activation(sc[:], vecs[:, 32:40], ACT.Silu).then_inc(sc_ready, 1)
            act.wait_ge(s_cst, 16)
            root_table()
            for c in range(NCH):
                squares(0, c)
                take_root(c, c + 1)

            def gating_gelu(b):
                act.wait_ge(units_pe, W_SGU_IN + 2 * b + 2)
                for c in range(NCH):
                    dst = (v_sb if b < 4 else u_sb)[:, c, 512 * (b % 4):512 * (b % 4) + 512]
                    nc.scalar.activation(dst, bank[BLOCK_BANKS[b % 2][c]][:], ACT.Gelu_apprx_tanh).then_inc(gelu_done, 1)

            norm_hi(0, 0)
            split(W_SGU_IN)
            split(W_SGU_IN + 1)
            norm_hi(0, 1)
            for b in range(1, 8):
                split(W_SGU_IN + 2 * b)
                split(W_SGU_IN + 2 * b + 1)
                gating_gelu(b - 1)
                if b == 4:
                    take_root(0, NCH)
            split(W_SGU_OUT)
            split(W_SGU_OUT + 1)
            gating_gelu(7)

            def down_phase(w0, t0, wnext):
                down_hi(t0, bank[2], None)
                for j in range(1, 8):
                    if j + 1 < 8:
                        split(w0 + j + 1)
                    down_hi(t0 + j, bank[(2, 0)[j % 2]], w0 + j - 1 if j >= 2 else None)
                if wnext is not None:
                    split(wnext)

            down_phase(W_SGU_OUT, T_SGU, W_FFN)
            norm(1, W_FFN + 1)

            def ffn_silu(s, units, a0, tile, chunks, done):
                act.wait_ge(units_pe, units + (ffn_unit("B", s) + 1))
                if s >= 2:
                    act.wait_ge(t_done, a0 + (s - 1))
                for c in range(chunks):
                    b = c if chunks == 2 else s % 2
                    nc.scalar.activation(tile[:, s % 2, c, :], bank[b][:, 0:256], ACT.Silu).then_inc(silu_done, 1)

            def ffn_hi(s, units, t0, parity, chunks):
                act.wait_ge(t_done, t0 + (s + 1))
                act.wait_ge(units_pe, units + (ffn_unit("D", s - 2) + 1 if s >= 2 else 0))
                n = P * chunks
                nc.scalar.activation(a_hi[:, parity, :, 0:n], bank[2][:, 0:2 * n].rearrange("p (k n) -> p k n", k=2),
                                     copy).then_inc(at_hi, 1)

            for u, kind, s in FFN_ORDER:
                if u >= 2:
                    split(W_FFN + u)
                for s2 in range(STEPS):
                    if u == ffn_unit("B", s2) + 2:
                        ffn_silu(s2, W_FFN, T_FFN, fact, NCH, None)
                        if s2 >= 1:
                            ffn_hi(s2 - 1, W_FFN, T_FFN, (s2 - 1) % 2, NCH)
            ffn_hi(STEPS - 1, W_FFN, T_FFN, (STEPS - 1) % 2, NCH)

            split(W_RET_IN)
            act.wait_ge(ang_ready, 1)
            nc.scalar.activation(trig[:, :, :, :], trig[:, :, :, :], ACT.Sin).then_inc(trig_ready, 1)
            norm(2, W_RET_IN + 1)

            def qk_copy(b):
                for c in range(NCH):
                    act.wait_ge(qk_tr, 2 * b + c + 1)
                    dst = (q_t if b < 2 else k_t)[:, 4 * (b % 2):4 * (b % 2) + 4, P * c:P * c + P]
                    nc.scalar.activation(dst, bank[5 + c][:].rearrange("p (k n) -> p k n", k=4),
                                         copy).then_inc(qk_ready, 1)

            def ret_v(b):
                act.wait_ge(units_pe, W_RET_IN + 2 * b + 2)
                for c in range(NCH):
                    nc.scalar.activation(rv[:, c, 512 * (b - 4):512 * (b - 4) + 512], bank[BLOCK_BANKS[b % 2][c]][:],
                                         copy).then_inc(ret_act, 1)

            def ret_gate(h):
                b = 8 + h
                act.wait_ge(units_pe, W_RET_IN + 2 * b + 2)
                if h >= 1:
                    act.wait_ge(og_done, h)
                for c in range(NCH):
                    nc.scalar.activation(silu_g[:, c, :], bank[BLOCK_BANKS[b % 2][c]][:], ACT.Silu).then_inc(ret_act, 1)
                act.wait_ge(o_done, h + 1)
                for c in range(NCH):
                    nc.scalar.activation(squares_o[:], bank[6 + c][:], ACT.Square, accum_out=oss[:, c:c + 1]) \
                        .then_inc(o_ss, 1)
                    act.wait_ge(o_ss, 2 * h + c + 1)
                take_root(0, NCH)

            for b in range(1, 12):
                split(W_RET_IN + 2 * b)
                split(W_RET_IN + 2 * b + 1)
                if b - 1 >= 4 and b - 1 < 8:
                    ret_v(b - 1)
                if 2 <= b < 6:
                    qk_copy(b - 2)
                if b - 1 >= 8:
                    ret_gate(b - 1 - 8)
            split(W_RET_OUT)
            split(W_RET_OUT + 1)
            ret_gate(3)
            down_phase(W_RET_OUT, T_RET, None)
            root_table()
            for c in range(NCH):
                squares(3, c)
                take_root(c, c + 1)

            act.wait_ge(top_ready, 1)
            nc.scalar.activation(wts[:, :, 1], wts[:, :, 0], ACT.Exp).then_inc(exp_done, 1)

            def gathered_hi(n):
                act.wait_ge(gval_ready, n)
                nc.scalar.activation(h_hi[:, :, 0:P], gval[:, :, :], copy).then_inc(g_hi_ready, 1)

            def take_output(units):
                act.wait_ge(units_pe, units + W_MOE)
                for half in range(2):
                    nc.scalar.activation(y_ev[:, 512 * half:512 * half + 512], bank[4 + half][:], copy).then_inc(y_out, 1)

            def expert(units, experts, steps, one, turn):
                for u, kind, s in FFN_ORDER:
                    moe_split(u, units, experts)
                    if u == 1:
                        take_output(units)
                    if u == 7:
                        act.wait_ge(pick_tr, one + 1)
                        nc.scalar.activation(pick_t[:, :, :], bank[3][:, 0:SEQ].rearrange("p (c n) -> p c n", c=NCH),
                                             copy).then_inc(pick_t_ready, 1)
                    for s2 in range(STEPS):
                        if u == ffn_unit("B", s2) + 2:
                            ffn_silu(s2, units + W_MOE, steps + T_DENSE, mact, 1, None)
                            if s2 >= 1:
                                ffn_hi(s2 - 1, units + W_MOE, steps + T_DENSE, (s2 - 1) % 2, 1)
                    if u == ffn_unit("B", STEPS - 1) + 2:
                        gathered_hi(turn + 2)
                ffn_hi(STEPS - 1, units + W_MOE, steps + T_DENSE, (STEPS - 1) % 2, 1)

            gathered_hi(1)
            with act.Fori(0, NE) as e:
                expert(e * FU, e, e * STEPS, e, e)
            take_output(NE * FU)
            act.wait_ge(slots_ready, 1)
            n_most = act.value_load(most_i[0:1, 0:1], min_val=0, max_val=SEQ)
            with act.If(n_most > P):
                gathered_hi(NE + 2)
                with act.Fori(0, NE) as e:
                    expert(e * FU + NE * FU, e + NE, e * STEPS + NE * STEPS, e + NE, e + NE + 1)
                take_output(2 * NE * FU)
            root_table()
            act.wait_ge(x_ready, 7)
            nc.scalar.activation(fin[:], x_sb[:, 0, :], ACT.Square, accum_out=ssq[:, 0:1]).then_inc(ss_ready, 1)
            take_root(0, 1)
            act.wait_ge(x_ready, 8)
            nc.scalar.activation(gval[:, :, :], x_sb[:, 1, :].rearrange("p (k n) -> p k n", k=KT), ACT.Square,
                                 accum_out=ssq[:, 1:2]).then_inc(ss_ready, 1)
            take_root(1, 2)

        @block.gpsimd
        def _(pool):
            nc.gpsimd.memset(acc0[:, :, :], 0.0).then_inc(acc0_zero, 1)
            pool.wait_ge(s_ws, 32)
            nc.gpsimd.affine_select(out=ws_raw[:, :, :], in_=ws_raw[:, :, :], compare_op=ALU.is_ge, fill=0.0, base=0,
                                    pattern=[[0, 8], [-1, P]], channel_multiplier=1).then_inc(ws_masked, 1)
            for j in range(4):
                pool.wait_ge(v_norm, 2)
                pool.wait_ge(ln_full[j % 2], 32 * (j // 2 + 1))
                for c in range(NCH):
                    v = v_sb[:, c, 512 * j:512 * j + 512]
                    nc.gpsimd.tensor_tensor(v, v, ln_rows[:, j % 2, 0, :], ALU.mult).then_inc(v_scaled, 1)
                    pool.wait_ge(v_scaled, 2 * j + c + 1)
                    last = nc.gpsimd.tensor_tensor(v, v, ln_rows[:, j % 2, 1, :], ALU.add)
                last.then_inc(v_ready, 1)
            pool.wait_ge(x_ready, 6)
            nc.gpsimd.memset(yacc[:, :, :], 0.0).then_inc(yacc_zero, 1)
            nc.gpsimd.memset(pick_t[:, :, :], 0.0).then_inc(pick_t_ready, 1)

        @block.vector
        def _(dve):
            seq = [0]

            def link(ins):
                seq[0] += 1
                ins.then_inc(dve_seq, 1)
                dve.wait_ge(dve_seq, seq[0])

            V = nc.vector
            roots = [0]

            def rsqrt(src, c0, c1, scale):
                var, r, s = rstd[:, c0:c1], root[:, c0:c1], step_t[:, c0:c1]
                V.tensor_scalar(var, src, scale, EPS, ALU.mult, ALU.add).then_inc(var_ready, 1)
                roots[0] += 1
                dve.wait_ge(root_ready, roots[0])
                link(V.reciprocal(r, r))
                link(V.tensor_tensor(s, r, r, ALU.mult))
                link(V.tensor_tensor(s, s, var, ALU.mult))
                link(V.tensor_scalar(s, s, -0.5, 1.5, ALU.mult, ALU.add))
                link(V.tensor_tensor(var, r, s, ALU.mult))

            def split(w):
                n = W_AT[w]
                dve.wait_ge(split_hi, w + 1)
                if w >= SPLIT_RING:
                    dve.wait_ge(units_pe, w - SPLIT_RING + 1)
                V.tensor_tensor(lo[w % SPLIT_RING][:], raw[n % DENSE_RING][:], hi[w % SPLIT_RING][:].bitcast(f32),
                                ALU.subtract).then_inc(units_dve, 1)

            def ada(i):
                n = A_AT[i]
                k, half = divmod(i, 2)
                dve.wait_ge(raw_full[n % DENSE_RING], raw_times(n))
                if half == 0:
                    dve.wait_ge(acc0_full[k % 2], 16 * (k // 2 + 1))
                    if k >= 2:
                        dve.wait_ge(acc_summed, k - 1)
                for kk in range(4):
                    first, last = half == 0 and kk == 0, kk == 3
                    a = acc[:, k % 2, :]
                    ins = V.scalar_tensor_tensor(out=a, in0=raw[n % DENSE_RING][:, 512 * kk:512 * kk + 512],
                                                 scalar=sc[:, 4 * half + kk:4 * half + kk + 1],
                                                 in1=acc0[:, k % 2, :] if first else a, op0=ALU.mult, op1=ALU.add)
                    if first:
                        ins.then_inc(acc0_used, 1)
                        dve.wait_ge(acc0_used, k + 1)
                    elif not last:
                        link(ins)
                    else:
                        ins.then_inc(units_dve, 1)
                        dve.wait_ge(units_dve, n + 1)

            def mod(k):
                dve.wait_ge(acc_summed, k + 1)
                layer, b = divmod(k, 12)
                part, half = divmod(b, 2)
                if part in (2, 5):
                    dst, src = (gate1 if part == 2 else gate2)[:, 512 * half:512 * half + 512], bank[ADA_BANK][:]
                else:
                    i = {0: 0, 1: 1, 3: 2, 4: 3}[part]
                    rows = slice(64 * half, 64 * half + 64)
                    dst, src = mods[rows, layer, i, :], bank[ADA_BANK][rows, 0:KT]
                V.tensor_copy(dst, src).then_inc(mod_ready, 1)

            def normalize(k, c):
                dve.wait_ge(ss_ready, 2 * k + c + 1)
                rsqrt(ssq[:, c:c + 1], c, c + 1, 1.0 / D_MODEL)
                V.tensor_scalar(xn[:, c, :], x_sb[:, c, :], rstd[:, c:c + 1], None, ALU.mult).then_inc(xn_ready, 1)

            def norm_scale(k):
                layer, second = divmod(k, 2)
                dve.wait_ge(mod_ready, 12 * layer + (4 if not second else 10))
                dve.wait_ge(s_vec, 80)
                link(V.tensor_scalar(mulv[:], mods[:, layer, 2 * second + 1, :], 1.0, None, ALU.add))
                link(V.tensor_tensor(mulv[:], mulv[:], vecs[:, 8 * k:8 * k + 8], ALU.mult))

            def norm_values(k, c):
                layer, second = divmod(k, 2)
                for half in range(2):
                    j = 2 * c + half
                    dve.wait_ge(tr_ready, 4 * k + j + 1)
                    for q in range(4):
                        kt = 4 * half + q
                        last = V.tensor_scalar(val_t[:, kt, P * c:P * c + P], bank[4 + j][:, P * q:P * q + P],
                                               mulv[:, kt:kt + 1], mods[:, layer, 2 * second, kt:kt + 1],
                                               ALU.mult, ALU.add)
                    last.then_inc(val_ready, 1)
                if k < 3:
                    for half in range(2):
                        dve.wait_ge(h_hi_ready, 4 * k + 2 * c + half + 1)
                        at4 = (slice(None), slice(4 * half, 4 * half + 4), slice(P * c, P * c + P))
                        V.tensor_tensor(h_lo[at4], val_t[at4], h_hi[at4].bitcast(f32), ALU.subtract).then_inc(h_ready, 1)

            def residual_norm(k, gate, units, w):
                norm_scale(k)
                dve.wait_ge(first_chunk, k)
                add_output(gate, 0)
                normalize(k, 0)
                dve.wait_ge(units_pe, units)
                add_output(gate, 1)
                norm_values(k, 0)
                if w is not None:
                    split(w)
                normalize(k, 1)
                norm_values(k, 1)

            def down_lo(i, psum):
                dve.wait_ge(at_hi, i + 1)
                V.tensor_tensor(a_lo[:, i % 2, :, :], psum[:].rearrange("p (k n) -> p k n", k=2),
                                a_hi[:, i % 2, :, :].bitcast(f32), ALU.subtract).then_inc(at_ready, 1)

            def add_output(gate, c):
                for half in range(2):
                    cols = slice(512 * half, 512 * half + 512)
                    y = out_tmp[:, 2 * c + half, :]
                    link(V.tensor_tensor(y, bank[4 + 2 * c + half][:], gate[:, cols], ALU.mult))
                    last = V.tensor_tensor(x_sb[:, c, cols], x_sb[:, c, cols], y, ALU.add)
                last.then_inc(x_ready, 1)

            normalize(0, 0)
            normalize(0, 1)
            dve.wait_ge(sc_ready, 1)
            for k in range(4):
                ada(2 * k)
                ada(2 * k + 1)
                if k:
                    mod(k - 1)
            mod(3)
            norm_scale(0)
            norm_values(0, 0)
            split(W_SGU_IN)
            split(W_SGU_IN + 1)
            norm_values(0, 1)

            ada(8)
            dve.wait_ge(ws_tr, 1)
            V.tensor_copy(bs_t[:], bank[7][:, 0:8])
            V.tensor_copy(ws_t[:, 0:4, :], bank[5][:].rearrange("p (g n) -> p g n", g=4)).then_inc(ws_ready, 1)
            V.tensor_copy(ws_t[:, 4:8, :], bank[6][:].rearrange("p (g n) -> p g n", g=4)).then_inc(ws_ready, 1)

            def gating_out(j):
                dve.wait_ge(fv_done, j + 1)
                dve.wait_ge(gelu_done, 8 + 2 * (j + 1))
                for c in range(NCH):
                    for g in range(2):
                        u = u_sb[:, c, 512 * j + 256 * g:512 * j + 256 * g + 256]
                        last = V.scalar_tensor_tensor(out=u, in0=bank[5 + c][:, 256 * g:256 * g + 256],
                                                      scalar=bs_t[:, 2 * j + g:2 * j + g + 1], in1=u,
                                                      op0=ALU.add, op1=ALU.mult)
                last.then_inc(y_blk, 1)

            for b in range(1, 8):
                split(W_SGU_IN + 2 * b)
                split(W_SGU_IN + 2 * b + 1)
                ada(8 + b)
                if b % 2 and b > 1:
                    mod(4 + b // 2 - 1)
                if b - 1 < 4:
                    for c in range(NCH):
                        dve.wait_ge(gelu_done, 2 * (b - 1) + c + 1)
                        ins = V.bn_stats(stats[:, c, b - 1, :], v_sb[:, c, 512 * (b - 1):512 * b])
                        if b == 4:
                            link(ins)
                if b == 4:
                    for c in range(NCH):
                        link(V.bn_aggr(mv[:, c, :], stats[:, c, :, :]))
                    rsqrt(mv[:, :, 1], 0, NCH, 1.0)
                    for c in range(NCH):
                        V.tensor_scalar(v_sb[:, c, :], v_sb[:, c, :], mv[:, c, 0:1], rstd[:, c:c + 1],
                                        ALU.subtract, ALU.mult).then_inc(v_norm, 1)
            gating_out(0)

            split(W_SGU_OUT)
            ada(16)
            mod(7)
            split(W_SGU_OUT + 1)
            ada(17)
            for j in range(1, 4):
                gating_out(j)
            down_lo(T_SGU, bank[2])
            for j in range(1, 8):
                if j < 7:
                    split(W_SGU_OUT + j + 1)
                    ada(17 + j)
                    if j % 2 == 1:
                        mod(8 + j // 2)
                down_lo(T_SGU + j, bank[(2, 0)[j % 2]])
            mod(11)
            split(W_FFN)
            residual_norm(1, gate1, W_FFN, W_FFN + 1)

            def ffn_act(s, silu0, tile, chunks):
                for c in range(chunks):
                    dve.wait_ge(silu_done, silu0 + (chunks * s + c + 1))
                    b = c if chunks == 2 else s % 2
                    last = V.tensor_tensor(tile[:, s % 2, c, :], tile[:, s % 2, c, :], bank[b][:, 256:512], ALU.mult)
                last.then_inc(act_ready, 1)

            def ffn_lo(s, t0, parity, chunks):
                dve.wait_ge(at_hi, t0 + (s + 1))
                n = P * chunks
                V.tensor_tensor(a_lo[:, parity, :, 0:n], bank[2][:, 0:2 * n].rearrange("p (k n) -> p k n", k=2),
                                a_hi[:, parity, :, 0:n].bitcast(f32), ALU.subtract).then_inc(at_ready, 1)

            for u, kind, s in FFN_ORDER:
                if u >= 2:
                    split(W_FFN + u)
                if kind == "B" and s < 8:
                    ada(24 + s)
                if kind == "D" and s % 2 == 0 and s <= 6:
                    mod(12 + s // 2)
                for s2 in range(STEPS):
                    if u == ffn_unit("B", s2) + 2:
                        ffn_act(s2, 0, fact, NCH)
                        if s2 >= 1:
                            ffn_lo(s2 - 1, T_FFN, (s2 - 1) % 2, NCH)
            ffn_lo(STEPS - 1, T_FFN, (STEPS - 1) % 2, NCH)

            split(W_RET_IN)
            dve.wait_ge(s_invf, 16)
            dve.wait_ge(s_pos, 16)
            link(V.tensor_copy(pos_f[:], pos_i[:]))
            for c in range(NCH):
                link(V.tensor_scalar(trig[:, 1, c, :], trig[:, 0, 0, :], pos_f[:, c:c + 1], None, ALU.mult))
            for fn in range(2):
                a, turn, dst = trig[:, 1, :, :], rope_tmp[:, :, :], trig[:, fn, :, :]
                link(V.tensor_scalar(turn, a, 1.0 / (2 * np.pi), 0.25 if fn == 0 else 0.0, ALU.mult, ALU.add))
                link(V.tensor_scalar(turn, turn, MAGIC, MAGIC, ALU.add, ALU.subtract))
                link(V.scalar_tensor_tensor(out=dst, in0=turn, scalar=-TWO_PI_HI, in1=a, op0=ALU.mult, op1=ALU.add))
                link(V.scalar_tensor_tensor(out=dst, in0=turn, scalar=-TWO_PI_MID, in1=dst, op0=ALU.mult, op1=ALU.add))
                link(V.scalar_tensor_tensor(out=dst, in0=turn, scalar=-TWO_PI_LO, in1=dst, op0=ALU.mult, op1=ALU.add))
                if fn == 0:
                    link(V.tensor_scalar(dst, dst, np.pi / 2, None, ALU.add))
                last = V.tensor_scalar(dst, dst, SIN_MAX, -SIN_MAX, ALU.min, ALU.max)
                if fn == 0:
                    link(last)
            last.then_inc(ang_ready, 1)
            residual_norm(2, gate2, W_RET_IN, W_RET_IN + 1)
            ada(32)

            def rotate(b):
                dve.wait_ge(units_pe, W_RET_IN + 2 * b + 2)
                for c in range(NCH):
                    if b:
                        dve.wait_ge(qk_tr, 2 * (b - 1) + c + 1)
                    ps = bank[BLOCK_BANKS[b % 2][c]][:].rearrange("p (h s f) -> p h s f", h=2, s=2)
                    r = rope[:, c, :].rearrange("p (h s f) -> p h s f", h=2, s=2)
                    t1, t2, r1, r2 = ps[:, :, 0, :], ps[:, :, 1, :], r[:, :, 0, :], r[:, :, 1, :]
                    cos, sin = (trig[:, i, c:c + 1, :].broadcast_to([P, 2, P]) for i in range(2))
                    link(V.tensor_tensor(rope_tmp[:, :, :], t2, sin, ALU.mult))
                    link(V.tensor_tensor(r1, t1, cos, ALU.mult))
                    link(V.tensor_tensor(r1, r1, rope_tmp[:, :, :], ALU.subtract))
                    link(V.tensor_tensor(rope_tmp[:, :, :], t1, sin, ALU.mult))
                    link(V.tensor_tensor(r2, t2, cos, ALU.mult))
                    V.tensor_tensor(r2, r2, rope_tmp[:, :, :], ALU.add).then_inc(rope_done, 1)
                    dve.wait_ge(rope_done, 2 * b + c + 1)

            def score(h):
                dve.wait_ge(scores_done, h + 1)
                dve.wait_ge(s_decay, 16)
                if h:
                    dve.wait_ge(o_done, h)
                V.tensor_tensor(sc_t[:, 0:256], bank[5][:, 0:256], decay[:, h, :], ALU.mult)
                V.tensor_tensor(sc_t[:, 256:384], bank[5][:, 256:384], decay[:, h, 0:P], ALU.mult) \
                    .then_inc(sct_ready, 1)

            def head_out(h):
                dve.wait_ge(o_ss, 2 * h + 2)
                rsqrt(oss[:, :], 0, NCH, 1.0 / DV)
                for c in range(NCH):
                    last = V.scalar_tensor_tensor(out=rv[:, c, 512 * h:512 * h + 512], in0=bank[6 + c][:],
                                                  scalar=rstd[:, c:c + 1], in1=silu_g[:, c, :],
                                                  op0=ALU.mult, op1=ALU.mult)
                last.then_inc(og_done, 1)

            for b in range(1, 12):
                split(W_RET_IN + 2 * b)
                if b >= 8:
                    score(b - 8)
                split(W_RET_IN + 2 * b + 1)
                ada(32 + b)
                if b % 2 and b > 1:
                    mod(16 + b // 2 - 1)
                if b - 1 < 4:
                    if b == 1:
                        dve.wait_ge(trig_ready, 1)
                    rotate(b - 1)
                if b - 1 >= 8:
                    head_out(b - 1 - 8)
            split(W_RET_OUT)
            ada(44)
            mod(21)
            split(W_RET_OUT + 1)
            ada(45)
            head_out(3)
            dve.wait_ge(og_done, 4)
            down_lo(T_RET, bank[2])
            for j in range(1, 8):
                if j < 7:
                    split(W_RET_OUT + j + 1)
                if j < 3:
                    ada(45 + j)
                if j == 1:
                    mod(22)
                if j == 4:
                    mod(23)
                down_lo(T_RET + j, bank[(2, 0)[j % 2]])
            residual_norm(3, gate1, W_MOE, None)

            dve.wait_ge(router_done, 1)
            dve.wait_ge(s_wr, 32)
            for c in range(NCH):
                link(V.tensor_tensor(logit[:, c, :], bank[ADA_BANK][:, 8 * c:8 * c + 8], brow[:], ALU.add))
                link(V.max(top[:, c, :], logit[:, c, :]))
                link(V.max_index(topi[:, c, :], top[:, c, :], logit[:, c, :]))
            link(V.tensor_copy(topf[:, :, :], topi[:, :, :]))
            V.tensor_tensor(wts[:, :, 0], top[:, :, 1], top[:, :, 0], ALU.subtract).then_inc(top_ready, 1)
            for c in range(NCH):
                for i in range(2):
                    ins = V.tensor_scalar(oh[:, i, c, :], iota[:, 0:NE], topf[:, c, i:i + 1], None, ALU.is_equal)
            link(ins)
            V.tensor_tensor(m_sel[:, :, :], oh[:, 0, :, :], oh[:, 1, :, :], ALU.add).then_inc(sel_ready, 1)
            dve.wait_ge(exp_done, 1)
            link(V.tensor_scalar(wts[:, :, 2], wts[:, :, 1], 1.0, None, ALU.add))
            link(V.reciprocal(wts[:, :, 2], wts[:, :, 2]))
            link(V.tensor_tensor(wts[:, :, 3], wts[:, :, 1], wts[:, :, 2], ALU.mult))
            for c in range(NCH):
                link(V.tensor_scalar(gates[:, c, 1:], oh[:, 0, c, :], wts[:, c, 2:3], None, ALU.mult))
                link(V.scalar_tensor_tensor(out=gates[:, c, 1:], in0=oh[:, 1, c, :], scalar=wts[:, c, 3:4],
                                            in1=gates[:, c, 1:], op0=ALU.mult, op1=ALU.add))
            dve.wait_ge(pos_done, 1)
            for c in range(NCH):
                link(V.scalar_tensor_tensor(out=slot[:, c, 0:NE], in0=bank[ADA_BANK][:, 8 * c:8 * c + 8], scalar=1.0,
                                            in1=m_sel[:, c, :], op0=ALU.add, op1=ALU.mult))
                link(V.tensor_scalar(slot[:, c, 0:NE], slot[:, c, 0:NE], 1.0, None, ALU.subtract))
            V.memset(slot[:, :, NE:], -1.0)
            link(V.memset(gates[:, :, 0:1], 0.0))
            link(V.reduce_max(most[:], bank[ADA_BANK][:, 16:24], AX.X))
            V.tensor_copy(most_i[:], most[:]).then_inc(slots_ready, 1)
            dve.wait_ge(yacc_zero, 1)

            def moe_split(u, units):
                k, w = SLOT_ORDER[u % MOE_RING], W_MOE + u
                dve.wait_ge(split_hi, units + (w + 1))
                dve.wait_ge(units_pe, units + (w - SPLIT_RING + 1))
                V.tensor_tensor(lo[w % SPLIT_RING][:], raw[k][:], hi[w % SPLIT_RING][:].bitcast(f32),
                                ALU.subtract).then_inc(units_dve, 1)

            def pick_tokens(e):
                for c in range(NCH):
                    last = V.tensor_scalar(pick[:, c, :], iota, slot[:, c, bass.ds(e, 1)], None, ALU.is_equal)
                last.then_inc(pick_ready, 1)

            def gathered_values(n):
                dve.wait_ge(gathered, n)
                for kt in range(KT):
                    last = V.tensor_scalar(gval[:, kt, :], bank[6 + kt // 4][:, P * (kt % 4):P * (kt % 4) + P],
                                           mulv[:, kt:kt + 1], mods[:, 1, 2, kt:kt + 1], ALU.mult, ALU.add)
                last.then_inc(gval_ready, 1)

            def gathered_lo(n):
                dve.wait_ge(g_hi_ready, n)
                V.tensor_tensor(h_lo[:, :, 0:P], gval[:, :, :], h_hi[:, :, 0:P].bitcast(f32),
                                ALU.subtract).then_inc(g_ready, 1)

            def scatter_add(n, c, col, b):
                dve.wait_ge(scattered, n)
                for half in range(2):
                    cols = slice(512 * half, 512 * half + 512)
                    last = V.scalar_tensor_tensor(out=yacc[:, c, cols], in0=bank[b + half][:],
                                                  scalar=gates[:, c, bass.ds(col, 1)], in1=yacc[:, c, cols],
                                                  op0=ALU.mult, op1=ALU.add)
                last.then_inc(yacc_done, 1)
                dve.wait_ge(yacc_done, n)

            def expert(e, units, steps, one, turn):
                for u, kind, s in FFN_ORDER:
                    moe_split(u, units)
                    if u in (3, 5):
                        c = (u - 3) // 2
                        scatter_add(turn * NCH + (c + 1), c, e, 6)
                    if u == 25:
                        dve.wait_ge(pick_tr, one + 1)
                        pick_tokens(e + 1)
                    if u == 30:
                        dve.wait_ge(g_ready, turn + 1)
                        gathered_values(turn + 2)
                    for s2 in range(STEPS):
                        if u == ffn_unit("B", s2) + 2:
                            ffn_act(s2, steps + NCH * STEPS, mact, 1)
                            if s2 >= 1:
                                ffn_lo(s2 - 1, steps + T_DENSE, (s2 - 1) % 2, 1)
                    if u == ffn_unit("B", STEPS - 1) + 2:
                        gathered_lo(turn + 2)
                ffn_lo(STEPS - 1, steps + T_DENSE, (STEPS - 1) % 2, 1)

            def last_scatter(n):
                scatter_add(n + 1, 0, NE, 6)
                scatter_add(n + 2, 1, NE, 4)

            pick_tokens(0)
            gathered_values(1)
            gathered_lo(1)
            with dve.Fori(0, NE) as e:
                expert(e, e * FU, e * STEPS, e, e)
            last_scatter(NCH * NE)
            n_most = dve.value_load(most_i[0:1, 0:1], min_val=0, max_val=SEQ)
            with dve.If(n_most > P):
                V.tensor_scalar(slot[:, :, :], slot[:, :, :], float(P), None, ALU.subtract).then_inc(slots_ready, 1)
                dve.wait_ge(slots_ready, 2)
                pick_tokens(0)
                gathered_values(NE + 2)
                gathered_lo(NE + 2)
                with dve.Fori(0, NE) as e:
                    expert(e, e * FU + NE * FU, e * STEPS + NE * STEPS, e + NE, e + NE + 1)
                last_scatter(NCH * (2 * NE + 1))

            for c in range(NCH):
                link(V.tensor_tensor(yacc[:, c, :], yacc[:, c, :], gate2[:], ALU.mult))
                V.tensor_tensor(x_sb[:, c, :], x_sb[:, c, :], yacc[:, c, :], ALU.add).then_inc(x_ready, 1)
            dve.wait_ge(s_fing, 16)
            for c in range(NCH):
                dve.wait_ge(ss_ready, 8 + c + 1)
                rsqrt(ssq[:, c:c + 1], c, c + 1, 1.0 / D_MODEL)
                V.scalar_tensor_tensor(out=yacc[:, c, :], in0=x_sb[:, c, :], scalar=rstd[:, c:c + 1], in1=y_ev[:],
                                       op0=ALU.mult, op1=ALU.mult).then_inc(fin_ready, 1)

        @block.tensor
        def _(pe):
            mm, tr = nc.tensor.matmul, nc.tensor.transpose

            def in_part(w, half, b, c):
                wh, wl = hi[w % SPLIT_RING], lo[w % SPLIT_RING]
                for kk in range(4):
                    kt = 4 * half + kk
                    ah, al = h_hi[:, kt, P * c:P * c + P], h_lo[:, kt, P * c:P * c + P]
                    cols = slice(512 * kk, 512 * kk + 512)
                    mm(bank[b][:], ah, wh[:, cols], start=kt == 0, stop=False)
                    mm(bank[b][:], ah, wl[:, cols], start=False, stop=False)
                    last = mm(bank[b][:], al, wh[:, cols], start=False, stop=kt == KT - 1)
                return last

            def in_unit(w, half, banks, chunks):
                for c in range(chunks):
                    last = in_part(w, half, banks[c], c)
                last.then_inc(units_pe, 1)

            def down_part(w, parity, first, final, c):
                wh, wl = hi[w % SPLIT_RING], lo[w % SPLIT_RING]
                for kk in range(2):
                    ah, al = (a[:, parity, kk, P * c:P * c + P] for a in (a_hi, a_lo))
                    for half in range(2):
                        o = bank[4 + 2 * c + half][:]
                        cols = slice(1024 * kk + 512 * half, 1024 * kk + 512 * half + 512)
                        mm(o, ah, wh[:, cols], start=first and kk == 0, stop=False)
                        mm(o, ah, wl[:, cols], start=False, stop=False)
                        last = mm(o, al, wh[:, cols], start=False, stop=final and kk == 1)
                return last

            def down_unit(w, parity, first, final, chunks):
                for c in range(chunks):
                    last = down_part(w, parity, first, final, c)
                last.then_inc(units_pe, 1)

            def last_downs(w, i):
                down_part(w, i % 2, False, False, 0)
                unit_here(w + 1)
                pe.wait_ge(at_ready, i + 2)
                down_part(w + 1, (i + 1) % 2, False, True, 0).then_inc(first_chunk, 1)
                down_part(w, i % 2, False, False, 1).then_inc(units_pe, 1)
                down_part(w + 1, (i + 1) % 2, False, True, 1).then_inc(units_pe, 1)

            def first_block(k, w, banks):
                for c in range(NCH):
                    norm_transposes(k, c)
                    pe.wait_ge(h_ready, 4 * k + 2 * c + 2)
                    for half in range(2):
                        if c == 0:
                            unit_here(w + half)
                        last = in_part(w + half, half, banks[c], c)
                        if c == 1:
                            last.then_inc(units_pe, 1)

            def unit_here(w):
                pe.wait_ge(units_dve, W_AT[w] + 1)

            def tile_of(a, c, kt):
                return a[:, c, :].rearrange("p (q k) -> p k q", k=KT)[:, kt, :]

            def norm_transposes(k, c):
                for j in (2 * c, 2 * c + 1):
                    half = j % 2
                    pe.wait_ge(xn_ready, 2 * k + c + 1)
                    for q in range(4):
                        kt = 4 * half + q
                        last = tr(bank[4 + j][:, P * q:P * q + P], tile_of(xn, c, kt), ident)
                    last.then_inc(tr_ready, 1)

            def ada_sum(k):
                pe.wait_ge(units_dve, A_AT[2 * k + 1] + 1)
                if k:
                    pe.wait_ge(mod_ready, k)
                a = acc[:, k % 2, :]
                if (k % 12) // 2 in (2, 5):
                    mm(bank[ADA_BANK][:], ones, a, start=True, stop=True).then_inc(acc_summed, 1)
                else:
                    rows = slice(64 * (k % 2), 64 * (k % 2) + 64)
                    cols = a.rearrange("p (q k) -> p k q", k=KT)
                    for kt in range(KT):
                        last = mm(bank[ADA_BANK][rows, kt:kt + 1], cols[:, kt, :], ones[:, 0:1], start=True, stop=True)
                    last.then_inc(acc_summed, 1)

            pe.wait_ge(s_cst, 16)
            for k in range(4):
                ada_sum(k)

            def weights_transposed():
                pe.wait_ge(ws_masked, 1)
                tr(bank[7][:, 0:8], bs_rows[0:8, :], ident[0:8, 0:8])
                for g in range(8):
                    last = tr(bank[5 + g // 4][:, P * (g % 4):P * (g % 4) + P], ws_raw[:, g, :], ident)
                last.then_inc(ws_tr, 1)

            def spatial(j):
                pe.wait_ge(v_ready, j + 1)
                pe.wait_ge(ws_ready, 2)
                if j:
                    pe.wait_ge(y_blk, j)
                for c in range(NCH):
                    for g in range(2):
                        last = mm(bank[5 + c][:, 256 * g:256 * g + 256], ws_t[:, 2 * j + g, :],
                                  v_sb[:, c, 512 * j + 256 * g:512 * j + 256 * g + 256], start=True, stop=True)
                last.then_inc(fv_done, 1)

            first_block(0, W_SGU_IN, BLOCK_BANKS[0])
            weights_transposed()
            for b in range(1, 8):
                if b >= 2:
                    pe.wait_ge(gelu_done, 2 * (b - 1))
                for half in range(2):
                    w = W_SGU_IN + 2 * b + half
                    unit_here(w)
                    in_unit(w, half, BLOCK_BANKS[b % 2], NCH)
                    if half == 0 and b % 2 == 0 and b:
                        ada_sum(4 + b // 2 - 1)
                if b == 7:
                    ada_sum(7)
                if b >= 6:
                    spatial(b - 6)
            spatial(2)
            spatial(3)

            def down_transposes(j, src, b):
                for kk in range(2):
                    for c in range(NCH):
                        n = SEQ * kk + P * c
                        last = tr(bank[b][:, n:n + P], src[:, c, 256 * j + P * kk:256 * j + P * kk + P], ident)
                last.then_inc(t_done, 1)

            def down_phase(w0, t0, src, ready, sums):
                for j in range(8):
                    if j % 2 == 0:
                        pe.wait_ge(ready, j // 2 + 1)
                    if j >= 2:
                        pe.wait_ge(at_ready, t0 + j - 1)
                    down_transposes(j, src, (2, 0)[j % 2])
                    if j >= 1:
                        w, i = w0 + j - 1, t0 + j - 1
                        unit_here(w)
                        pe.wait_ge(at_ready, i + 1)
                        if j == 1:
                            pe.wait_ge(ready, 4)
                        if j == 7:
                            last_downs(w, i)
                        else:
                            down_unit(w, i % 2, j == 1, False, NCH)
                        if j in sums:
                            ada_sum(sums[j])

            pe.wait_ge(gelu_done, 16)
            down_phase(W_SGU_OUT, T_SGU, u_sb, y_blk, {1: 8, 3: 9, 5: 10, 7: 11})


            def ffn_transposes(s, tile, chunks):
                for kk in range(2):
                    for c in range(chunks):
                        n = P * (chunks * kk + c)
                        last = tr(bank[2][:, n:n + P], tile[:, s % 2, c, P * kk:P * kk + P], ident)
                last.then_inc(t_done, 1)

            first_block(1, W_FFN, (0, 1))
            for u, kind, s in FFN_ORDER[2:-1]:
                w = W_FFN + u
                if kind == "A":
                    pe.wait_ge(act_ready, s)
                if kind == "D":
                    pe.wait_ge(at_ready, T_FFN + s + 1)
                    if s == STEPS - 2:
                        pe.wait_ge(act_ready, STEPS)
                        ffn_transposes(s + 1, fact, NCH)
                unit_here(w)
                if kind == "D" and s == STEPS - 2:
                    last_downs(w, T_FFN + s)
                elif kind == "D":
                    down_unit(w, s % 2, s == 0, False, NCH)
                else:
                    in_unit(w, int(kind == "B"), (0, 1), NCH)
                if kind == "B" and s:
                    pe.wait_ge(act_ready, s)
                    pe.wait_ge(at_ready, T_FFN + s - 1)
                    ffn_transposes(s - 1, fact, NCH)
                if kind == "A" and s >= 2 and s % 2 == 0 and s <= 8:
                    ada_sum(12 + s // 2 - 1)

            def qk_transposes(b):
                for c in range(NCH):
                    pe.wait_ge(rope_done, 2 * b + c + 1)
                    if b:
                        pe.wait_ge(qk_ready, 2 * (b - 1) + c + 1)
                    for i in range(4):
                        last = tr(bank[5 + c][:, P * i:P * i + P], rope[:, c, P * i:P * i + P], ident)
                    last.then_inc(qk_tr, 1)

            def scores(h):
                pe.wait_ge(qk_ready, 8)
                if h:
                    pe.wait_ge(sct_ready, h)
                for o, keys, queries in (((0, 256), (0, P), (0, SEQ)), ((256, 384), (P, SEQ), (P, SEQ))):
                    for kk in range(2):
                        last = mm(bank[5][:, o[0]:o[1]], k_t[:, 2 * h + kk, keys[0]:keys[1]],
                                  q_t[:, 2 * h + kk, queries[0]:queries[1]], start=kk == 0, stop=kk == 1)
                last.then_inc(scores_done, 1)

            def head_outputs(h):
                pe.wait_ge(sct_ready, h + 1)
                pe.wait_ge(ret_act, 8)
                if h:
                    pe.wait_ge(og_done, h)
                v0, v1 = (rv[:, c, 512 * h:512 * h + 512] for c in range(NCH))
                mm(bank[6][:], sc_t[:, 0:P], v0, start=True, stop=True)
                mm(bank[7][:], sc_t[:, P:256], v0, start=True, stop=False)
                mm(bank[7][:], sc_t[:, 256:384], v1, start=False, stop=True).then_inc(o_done, 1)

            first_block(2, W_RET_IN, BLOCK_BANKS[0])
            for b in range(1, 12):
                if 2 <= b < 6:
                    pe.wait_ge(rope_done, 2 * (b - 1))
                elif b >= 6:
                    pe.wait_ge(ret_act, 2 * (b - 5))
                if b >= 8:
                    scores(b - 8)
                for half in range(2):
                    w = W_RET_IN + 2 * b + half
                    unit_here(w)
                    in_unit(w, half, BLOCK_BANKS[b % 2], NCH)
                    if half == 0 and b % 2 == 0 and b:
                        ada_sum(16 + b // 2 - 1)
                if 1 <= b <= 4:
                    qk_transposes(b - 1)
                if b >= 8:
                    head_outputs(b - 8)
            ada_sum(21)
            pe.wait_ge(ret_act, 16)
            down_phase(W_RET_OUT, T_RET, rv, og_done, {1: 22, 3: 23})

            for c in range(NCH):
                norm_transposes(3, c)
            pe.wait_ge(val_ready, 16)
            pe.wait_ge(s_wr, 32)
            pe.wait_ge(mod_ready, 24)
            for c in range(NCH):
                for kt in range(KT):
                    last = mm(bank[ADA_BANK][:, 8 * c:8 * c + 8], val_t[:, kt, P * c:P * c + P], wr[:, kt, :],
                              start=kt == 0, stop=kt == KT - 1)
            last.then_inc(router_done, 1)
            pe.wait_ge(sel_ready, 1)
            b3 = bank[ADA_BANK]
            mm(b3[:, 0:8], utri, m_sel[:, 0, :], start=True, stop=True)
            mm(b3[:, 8:16], utri, m_sel[:, 1, :], start=True, stop=False)
            mm(b3[:, 8:16], ones, m_sel[:, 0, :], start=False, stop=True)
            mm(b3[:, 16:24], ones, m_sel[:, 0, :], start=True, stop=False)
            mm(b3[:, 16:24], ones, m_sel[:, 1, :], start=False, stop=True).then_inc(pos_done, 1)
            pe.wait_ge(slots_ready, 1)

            def gather(n):
                pe.wait_ge(pick_ready, n)
                for kt in range(KT):
                    for c in range(NCH):
                        last = mm(bank[6 + kt // 4][:, P * (kt % 4):P * (kt % 4) + P], tile_of(xn, c, kt),
                                  pick[:, c, :], start=c == 0, stop=c == NCH - 1)
                last.then_inc(gathered, 1)

            def scatter(c, b):
                for half in range(2):
                    last = mm(bank[b + half][:], pick_t[:, c, :], y_ev[:, 512 * half:512 * half + 512],
                              start=True, stop=True)
                last.then_inc(scattered, 1)

            def expert(units, steps, one, turn):
                pe.wait_ge(g_ready, turn + 1)
                for u, kind, s in FFN_ORDER:
                    w = W_MOE + u
                    if kind == "A":
                        pe.wait_ge(act_ready, steps + (STEPS + max(0, s - 1)))
                    if kind == "D":
                        if s == STEPS - 1:
                            pe.wait_ge(act_ready, steps + (STEPS + STEPS))
                            pe.wait_ge(at_ready, steps + (T_DENSE + s))
                            ffn_transposes(s, mact, 1)
                        pe.wait_ge(at_ready, steps + (T_DENSE + s + 1))
                    pe.wait_ge(units_dve, units + (N_DENSE + u + 1))
                    if kind == "D":
                        down_unit(w, s % 2, s == 0, s == STEPS - 1, 1)
                    else:
                        in_unit(w, int(kind == "B"), (s % 2,), 1)
                    if kind == "B" and s:
                        pe.wait_ge(act_ready, steps + (STEPS + s))
                        pe.wait_ge(at_ready, steps + (T_DENSE + s - 1))
                        ffn_transposes(s - 1, mact, 1)
                    if u == 1:
                        pe.wait_ge(y_out, turn * 2 + 2)
                        pe.wait_ge(pick_t_ready, one + 1)
                        scatter(0, 6)
                    if u == 3:
                        pe.wait_ge(yacc_done, turn * NCH + 1)
                        scatter(1, 6)
                    if u == 5:
                        for c in range(NCH):
                            last = tr(bank[3][:, P * c:P * c + P], pick[:, c, :], ident)
                        last.then_inc(pick_tr, 1)
                    if u == 27:
                        pe.wait_ge(yacc_done, turn * NCH + 2)
                        gather(turn + 2)

            def last_scatter(n, picks):
                pe.wait_ge(y_out, 2 * n)
                pe.wait_ge(pick_t_ready, picks)
                pe.wait_ge(gval_ready, n)
                scatter(0, 6)
                scatter(1, 4)

            gather(1)
            with pe.Fori(0, NE) as e:
                expert(e * FU, e * STEPS, e, e)
            last_scatter(NE + 1, NE + 1)
            n_most = pe.value_load(most_i[0:1, 0:1], min_val=0, max_val=SEQ)
            with pe.If(n_most > P):
                pe.wait_ge(yacc_done, NCH * (NE + 1))
                gather(NE + 2)
                with pe.Fori(0, NE) as e:
                    expert(e * FU + NE * FU, e * STEPS + NE * STEPS, e + NE, e + NE + 1)
                last_scatter(2 * NE + 2, 2 * NE + 1)


def constants():
    i = np.arange(P)
    cst = np.stack([np.eye(P), np.ones((P, P)), np.tile(i, (P, 1)), i[:, None] < i[None, :]], axis=1)
    log_gamma = np.log1p(-np.exp2(-5.0 - np.arange(HEADS)))
    rel = (i[None, :] - i[:, None])[:, None, :]
    lg = log_gamma[None, :, None]
    intra = np.where(rel >= 0, np.exp(lg * np.maximum(rel, 0)), 0.0)
    cross = np.exp(lg * (P + rel))
    decay = np.concatenate([intra, cross], axis=2) * DK ** -0.5
    inv_freq = 1.0 / (np.float32(10000.0) ** (np.arange(0, DK, 2, dtype=np.float32) / np.float32(DK)))
    return {"consts": cst.reshape(P, 4 * P).astype(np.float32), "decay": decay.reshape(P, -1).astype(np.float32),
            "inv_freq": inv_freq.reshape(1, P).astype(np.float32)}


_INS = ["x", "c", "positions", "ada_w", "ada_b", "mix_norm_g", "ffn_norm_g", "sgu_w_in", "sgu_ln_g", "sgu_ln_b",
        "sgu_w_s", "sgu_b_s", "sgu_w_out", "ffn_w_gate_up", "ffn_w_down", "ret_w_in", "ret_w_out", "moe_w_router",
        "moe_b_router", "moe_w_gate_up", "moe_w_down", "final_norm_g"]


def kernel(**inputs):
    import concourse.bacc as _bacc
    from concourse.bass_utils import run_bass_kernel_spmd as _run

    nc = _bacc.Bacc("TRN2", target_bir_lowering=False, num_devices=1)
    arrays, t = {}, {}
    for name, a in [*((n, inputs[n]) for n in _INS), *constants().items()]:
        a = np.ascontiguousarray(a)
        arrays[f"in_{name}"] = a
        t[name] = nc.dram_tensor(f"in_{name}", a.shape, mybir.dt.from_np(a.dtype), kind="ExternalInput").ap()
    out = nc.dram_tensor("out", (1, SEQ, D_MODEL), mybir.dt.float32, kind="ExternalOutput").ap()
    trunk(nc, t, out)
    return _run(nc, [arrays], core_ids=[0]).results[0]["out"]
```

```python
import concourse.bass as bass
from concourse import mybir
from contextlib import ExitStack
import numpy as np

P = 128
D_MODEL = 1024
SEQ = 256
NCH = SEQ // P
KT = D_MODEL // P
SGU = 2 * D_MODEL
HEADS, DK, DV = 4, 256, 512
RET_IN = 2 * HEADS * DK + 2 * HEADS * DV
FFN = ((8 * D_MODEL // 3 + 127) // 128) * 128
NE = 8
EPS = 1e-6
UNIT = 2048
STEPS = FFN // 256
FU = 3 * STEPS
DENSE_RING, MOE_RING, SPLIT_RING = 9, 11, 3
MAGIC = 1.5 * 2.0 ** 23
TWO_PI_HI, TWO_PI_MID = 6.28125, 0.0019350051879882812
TWO_PI_LO = 2 * np.pi - TWO_PI_HI - TWO_PI_MID
SIN_MAX = 3.1415925


def ffn_unit(kind, s):
    if kind == "D":
        return 3 * s + 6 if s <= STEPS - 3 else FU - STEPS + s
    return 2 * s + max(0, s - 2) + (kind == "B")


FFN_ORDER = sorted([(ffn_unit(k, s), k, s) for k in "ABD" for s in range(STEPS)])

FFN_ADA = {("A", 1): 20, ("B", 1): 21, ("A", 2): 22, **{("B", s): 21 + s for s in range(2, STEPS)}}

W_SGU_IN = 0
W_SGU_OUT = W_SGU_IN + 16
W_FFN = W_SGU_OUT + 8
W_RET_IN = W_FFN + FU
W_RET_OUT = W_RET_IN + 24
W_MOE = W_RET_OUT + 8


def dense_stream():
    out, a, w = [], 0, 0

    def ada(n):
        nonlocal a
        for _ in range(n):
            out.append(("A", a // 2, a % 2))
            a += 1

    def split(n):
        nonlocal w
        for _ in range(n):
            out.append(("W", w))
            w += 1
    ada(8)
    for _ in range(8):
        split(2)
        ada(1)
    for j in range(8):
        split(1)
        ada(int(j % 2 == 0))
    for _, k, s in FFN_ORDER:
        split(1)
        ada(int((k, s) in FFN_ADA))
    split(2)
    for b in range(1, 12):
        split(1)
        ada(int(b == 1))
        split(1)
        ada(1)
    for j in range(8):
        split(1)
        ada(int(j < 4))
    return out


STREAM = dense_stream()
N_DENSE = len(STREAM)
W_AT = {u[1]: n for n, u in enumerate(STREAM) if u[0] == "W"}
W_AT.update({W_MOE + u: N_DENSE + u for u in range(3)})
A_AT = {2 * u[1] + u[2]: n for n, u in enumerate(STREAM) if u[0] == "A"}
SLOT_ORDER = [(N_DENSE + i) % DENSE_RING for i in range(DENSE_RING)] + [9, 10]
BLOCK_BANKS = [(0, 1), (2, 4)]
ADA_BANK = 3


def trunk(nc, t, out):
    f32, f32r, i32, u32 = mybir.dt.float32, mybir.dt.float32r, mybir.dt.int32, mybir.dt.uint32
    ALU, ACT, AX = mybir.AluOpType, mybir.ActivationFunctionType, mybir.AxisListType
    ctx = ExitStack()
    with ctx:
        base = nc.sbuf_base if not callable(nc.sbuf_base) else nc.sbuf_base()
        base = (base + 63) // 64 * 64

        def at(name, shape, dt, off):
            return nc.alloc_sbuf_tensor_at(name, [P, *shape], dt, offset=base + off)

        def sem(name):
            return ctx.enter_context(nc.semaphore(name))

        KB = 1024
        RAW0, HI0, LO0 = 0, 88 * KB, 112 * KB
        X0, HTH0, HTL0, BIG0 = 136 * KB, 144 * KB, 152 * KB, 160 * KB
        ATH0, ATL0, F0 = 192 * KB, 196 * KB, 200 * KB
        E0 = RAW0 + 9 * 8 * KB
        raw = [at(f"raw{i}", [UNIT], f32, RAW0 + 8 * KB * i) for i in range(MOE_RING)]
        hi = [at(f"hi{i}", [UNIT], f32r, HI0 + 8 * KB * i) for i in range(SPLIT_RING)]
        lo = [at(f"lo{i}", [UNIT], f32r, LO0 + 8 * KB * i) for i in range(SPLIT_RING)]
        x_sb = at("x_sb", [NCH, D_MODEL], f32, X0)
        h_hi = at("h_hi", [KT, SEQ], f32r, HTH0)
        h_lo = at("h_lo", [KT, SEQ], f32r, HTL0)
        a_hi = at("a_hi", [2, 2, SEQ], f32r, ATH0)
        a_lo = at("a_lo", [2, 2, SEQ], f32r, ATL0)
        acc = at("acc", [2, 512], f32, E0)
        acc0 = at("acc0", [2, 512], f32, E0 + 4 * KB)
        gate1 = at("gate1", [D_MODEL], f32, E0 + 8 * KB)
        rows1 = at("rows1", [2, 512], f32, E0 + 8 * KB)
        ws_t = at("ws_t", [8, P], f32, E0 + 12 * KB)
        trig = at("trig", [2, NCH, P], f32, E0 + 12 * KB)
        squares_o = at("squares_o", [512], f32, E0 + 12 * KB)
        sc_t = at("sc_t", [384], f32, E0 + 14 * KB)
        rope_tmp = at("rope_tmp", [2, P], f32, E0 + 14 * KB)
        xn = at("xn", [NCH, D_MODEL], f32, BIG0)
        u_sb = at("u_sb", [NCH, SGU], f32, BIG0)
        v_sb = at("v_sb", [NCH, SGU], f32, BIG0 + 16 * KB)
        bs_rows = at("bs_rows", [P], f32, BIG0 + 12 * KB)
        ws_raw = at("ws_raw", [8, P], f32, BIG0 + 8 * KB)
        fact = at("fact", [2, NCH, 256], f32, BIG0 + 8 * KB)
        rv = at("rv", [NCH, SGU], f32, BIG0)
        q_t = at("q_t", [8, SEQ], f32, BIG0 + 16 * KB)
        k_t = at("k_t", [8, SEQ], f32, BIG0 + 24 * KB)
        yacc = at("yacc", [NCH, D_MODEL], f32, BIG0 + 8 * KB)
        y_hi = at("y_hi", [D_MODEL], f32r, BIG0 + 16 * KB)
        pick = at("pick", [NCH, P], f32, BIG0 + 20 * KB)
        pick_t = at("pick_t", [NCH, P], f32r, BIG0 + 21 * KB)
        mact = at("mact", [2, 1, 256], f32, BIG0 + 22 * KB)
        gval = at("gval", [KT, P], f32, BIG0 + 24 * KB)
        y_lo = at("y_lo", [D_MODEL], f32r, BIG0 + 28 * KB)
        fin_g = at("fin_g", [D_MODEL], f32, BIG0 + 28 * KB)
        out_tmp = at("out_tmp", [4, 512], f32, BIG0 + 16 * KB)
        fin = at("fin", [D_MODEL], f32, HTH0)
        val_t = at("val_t", [KT, SEQ], f32, ATH0)
        ln_rows = at("ln_rows", [2, 2, 512], f32, ATH0)
        decay = at("decay", [HEADS, 256], f32, ATH0)
        rope = at("rope", [NCH, 512], f32, ATL0)
        silu_g = at("silu_g", [NCH, 512], f32, ATL0)
        gate2 = at("gate2", [D_MODEL], f32, F0)
        cst = at("cst", [4, P], f32, F0 + 4 * KB)
        small = [F0 + 6 * KB]

        def little(name, shape, dt=f32):
            n = int(np.prod(shape)) * 4
            small[0] += (-small[0]) % 32
            r = at(name, shape, dt, small[0])
            small[0] += n
            return r
        ident, ones, iota, utri = (cst[:, i, :] for i in range(4))
        vecs = little("vecs", [40])
        sc = little("sc", [KT])
        mods = little("mods", [2, 4, KT])
        mulv = little("mulv", [KT])
        ssq = little("ssq", [NCH])
        rstd = little("rstd", [NCH])
        bs_t = little("bs_t", [8])
        stats = little("stats", [NCH, 4, 6])
        mv = little("mv", [NCH, 2])
        oss = little("oss", [NCH])
        root = little("root", [NCH])
        step_t = little("step_t", [NCH])
        warm = little("warm", [8])
        pos_i = little("pos_i", [NCH], i32)
        pos_f = little("pos_f", [NCH])
        wr = little("wr", [KT, NE])
        brow = little("brow", [NE])
        logit = at("logit", [NCH, NE], f32, BIG0 + 30 * KB)
        top = at("top", [NCH, 8], f32, BIG0 + 30 * KB + 64)
        topi = at("topi", [NCH, 8], u32, BIG0 + 30 * KB + 128)
        topf = at("topf", [NCH, 8], f32, BIG0 + 30 * KB + 192)
        oh = at("oh", [2, NCH, NE], f32, BIG0 + 30 * KB + 256)
        wts = at("wts", [NCH, 4], f32, BIG0 + 30 * KB + 384)
        m_sel = little("m_sel", [NCH, NE])
        gates = little("gates", [NCH, NE + 1])
        slot = little("slot", [NCH, NE + 1])
        most = little("most", [1])
        most_i = little("most_i", [1], i32)
        assert base + small[0] <= nc.sbuf_usable_end, (base, small[0], nc.sbuf_usable_end)

        bank = [ctx.enter_context(nc.psum_tensor(f"bank{i}", [P, 512], f32)) for i in range(8)]

        raw_full = [sem(f"raw_full{i}") for i in range(MOE_RING)]
        split_hi, units_dve, units_pe, first_chunk = (
            sem(n) for n in ("split_hi", "units_dve", "units_pe", "first_chunk"))
        acc0_full = [sem(f"acc0_full{i}") for i in range(2)]
        acc0_zero, acc0_used, acc_summed, mod_ready, row_summed, row_copied = (
            sem(n) for n in ("acc0_zero", "acc0_used", "acc_summed", "mod_ready", "row_summed", "row_copied"))
        s_cst, s_x, s_vec, s_ws, s_pos, s_invf, s_decay, s_wr, s_fing, s_out = (
            sem(n) for n in ("s_cst", "s_x", "s_vec", "s_ws", "s_pos", "s_invf", "s_decay", "s_wr", "s_fing", "s_out"))
        ln_full = [sem(f"ln_full{i}") for i in range(2)]
        sc_ready, var_ready, root_ready = sem("sc_ready"), sem("var_ready"), sem("root_ready")
        ws_masked, ws_tr, ws_ready = sem("ws_masked"), sem("ws_tr"), sem("ws_ready")
        x_ready, ss_ready, xn_ready, tr_ready, val_ready, h_hi_ready, h_ready = (
            sem(n) for n in ("x_ready", "ss_ready", "xn_ready", "tr_ready", "val_ready", "h_hi_ready", "h_ready"))
        gelu_done, v_norm, v_ready, fv_done, y_blk = (
            sem(n) for n in ("gelu_done", "v_norm", "v_ready", "fv_done", "y_blk"))
        t_done, at_hi, at_ready, silu_done, act_ready = (
            sem(n) for n in ("t_done", "at_hi", "at_ready", "silu_done", "act_ready"))
        ang_ready, trig_ready, rope_done, qk_tr, qk_ready, ret_act, scores_done, sct_ready, o_done, o_ss, onorm_done, og_done = (
            sem(n) for n in ("ang_ready", "trig_ready", "rope_done", "qk_tr", "qk_ready", "ret_act", "scores_done",
                             "sct_ready", "o_done", "o_ss", "onorm_done", "og_done"))
        router_done, top_ready, exp_done, sel_ready, pos_done, slots_ready = (
            sem(n) for n in ("router_done", "top_ready", "exp_done", "sel_ready", "pos_done", "slots_ready"))
        pick_ready, pick_tr, pick_t_ready, gathered, gval_ready, g_hi_ready, g_ready, y_out, y_split, scattered, yacc_done = (
            sem(n) for n in ("pick_ready", "pick_tr", "pick_t_ready", "gathered", "gval_ready", "g_hi_ready",
                             "g_ready", "y_out", "y_split", "scattered", "yacc_done"))
        dve_seq, fin_ready, yacc_zero, v_scaled = (
            sem(n) for n in ("dve_seq", "fin_ready", "yacc_zero", "v_scaled"))

        T_DENSE = 8 + STEPS + 8
        T_SGU, T_FFN, T_RET = 0, 8, 8 + STEPS

        def rhs(tile, kk, n0, n1, width):
            return tile[:, kk * width + n0:kk * width + n1]

        block = ctx.enter_context(nc.Block())

        @block.sync
        def _(sp):
            def ada_source(k, half):
                layer, b = divmod(k, 12)
                return columns(t["ada_w"][layer], b, half)

            def columns(w, b, half):
                return w.rearrange("(p k) n -> p k n", p=P)[:, 4 * half:4 * half + 4, 512 * b:512 * b + 512]

            def rows(w, j):
                return w[256 * j:256 * j + 256, :].rearrange("(k p) n -> p k n", p=P)

            def ffn_load(dst, gate_up, down, kind, s, full):
                if kind == "D":
                    sp.dma_start(dst[:].rearrange("p (k n) -> p k n", k=2), rows(down, s)).then_inc(full, 16)
                    return
                half = int(kind == "B")
                src = gate_up.rearrange("(p k) (g n) -> p (k g) n", p=P, g=2)
                sp.dma_start(dst[:].rearrange("p (k n) -> p k n", k=8),
                             src[:, 8 * half:8 * half + 8, 256 * s:256 * s + 256]).then_inc(full, 16)

            for k in range(4):
                g = t[("mix_norm_g", "ffn_norm_g")[k % 2]][k // 2]
                sp.dma_start(vecs[:, 8 * k:8 * k + 8], g.rearrange("(p k) -> p k", p=P)).then_inc(s_vec, 16)
            sp.dma_start(vecs[:, 32:40], t["c"].rearrange("a (p k) -> p (a k)", p=P)).then_inc(s_vec, 16)
            sp.dma_start(cst[:], t["consts"].rearrange("p (k n) -> p k n", k=4)).then_inc(s_cst, 16)
            for n, unit in enumerate(STREAM):
                slot_n, full = raw[n % DENSE_RING], raw_full[n % DENSE_RING]
                if DENSE_RING <= n < DENSE_RING + 8:
                    sp.wait_ge(acc_summed, (n - DENSE_RING) // 2 + 1)
                elif n >= DENSE_RING:
                    sp.wait_ge(units_dve, n - DENSE_RING + 1)
                if unit[0] == "A":
                    _, k, half = unit
                    if half == 0:
                        if k < 2:
                            sp.wait_ge(acc0_zero, 1)
                        else:
                            sp.wait_ge(acc0_used, k - 1)
                        layer, b = divmod(k, 12)
                        sp.dma_start(acc0[0:1, k % 2, :], t["ada_b"][layer:layer + 1, 512 * b:512 * b + 512]) \
                            .then_inc(acc0_full[k % 2], 16)
                    sp.dma_start(slot_n[:].rearrange("p (k n) -> p k n", k=4), ada_source(k, half)).then_inc(full, 16)
                else:
                    w = unit[1]
                    if w < W_SGU_OUT:
                        b, half = divmod(w - W_SGU_IN, 2)
                        col = (b + 4) % 8
                        sp.dma_start(slot_n[:].rearrange("p (k n) -> p k n", k=4),
                                     columns(t["sgu_w_in"][0], col, half)).then_inc(full, 16)
                    elif w < W_FFN:
                        sp.dma_start(slot_n[:].rearrange("p (k n) -> p k n", k=2),
                                     rows(t["sgu_w_out"][0], w - W_SGU_OUT)).then_inc(full, 16)
                    elif w < W_RET_IN:
                        _, kind, s = FFN_ORDER[w - W_FFN]
                        ffn_load(slot_n, t["ffn_w_gate_up"][0], t["ffn_w_down"][0], kind, s, full)
                    elif w < W_RET_OUT:
                        b, half = divmod(w - W_RET_IN, 2)
                        sp.dma_start(slot_n[:].rearrange("p (k n) -> p k n", k=4),
                                     columns(t["ret_w_in"][0], b, half)).then_inc(full, 16)
                    else:
                        sp.dma_start(slot_n[:].rearrange("p (k n) -> p k n", k=2),
                                     rows(t["ret_w_out"][0], w - W_RET_OUT)).then_inc(full, 16)
                if n == 1:
                    sp.dma_start(x_sb[:], t["x"].rearrange("a (c p) n -> p (a c) n", p=P)).then_inc(s_x, 16)
                    sp.dma_start(bs_rows[0:8, :], t["sgu_b_s"][0]).then_inc(s_ws, 16)
                    sp.dma_start(ws_raw[:], t["sgu_w_s"][0].rearrange("g p s -> p g s")).then_inc(s_ws, 16)
                    sp.dma_start(pos_i[:], t["positions"].rearrange("a (c p) -> p (a c)", p=P),
                                 allow_slow_non_contiguous=True).then_inc(s_pos, 16)
                    sp.dma_start(wr[:], t["moe_w_router"][0].rearrange("(p k) n -> p k n", p=P)).then_inc(s_wr, 16)
                    sp.dma_start(brow[:], t["moe_b_router"][0:1, :].to_broadcast([P, NE])).then_inc(s_wr, 16)

            def expert_load(e, u, kind, s):
                gu = t["moe_w_gate_up"][0][bass.ds(e, 1)].rearrange("a k n -> (a k) n")
                dn = t["moe_w_down"][0][bass.ds(e, 1)].rearrange("a k n -> (a k) n")
                k = SLOT_ORDER[u % MOE_RING]
                ffn_load(raw[k], gu, dn, kind, s, raw_full[k])

            for u, kind, s in FFN_ORDER[:MOE_RING]:
                if u < DENSE_RING:
                    sp.wait_ge(units_dve, N_DENSE + u - DENSE_RING + 1)
                elif u == DENSE_RING:
                    sp.wait_ge(mod_ready, 24)
                    sp.wait_ge(x_ready, 6)
                expert_load(0, u, kind, s)
            with sp.Fori(0, NE - 1) as e:
                for u, kind, s in FFN_ORDER[MOE_RING:]:
                    sp.wait_ge(units_dve, e * FU + (N_DENSE + u - MOE_RING + 1))
                    expert_load(e, u, kind, s)
                for u, kind, s in FFN_ORDER[:MOE_RING]:
                    sp.wait_ge(units_dve, e * FU + (N_DENSE + FU + u - MOE_RING + 1))
                    expert_load(e + 1, u, kind, s)
            for u, kind, s in FFN_ORDER[MOE_RING:]:
                sp.wait_ge(units_dve, (NE - 1) * FU + N_DENSE + u - MOE_RING + 1)
                expert_load(NE - 1, u, kind, s)
            sp.wait_ge(slots_ready, 1)
            n_most = sp.value_load(most_i[0:1, 0:1], min_val=0, max_val=SEQ)
            with sp.If(n_most > P):
                with sp.Fori(0, NE) as e:
                    for u, kind, s in FFN_ORDER:
                        sp.wait_ge(units_dve, e * FU + (NE * FU + N_DENSE + u - MOE_RING + 1))
                        expert_load(e, u, kind, s)
            sp.wait_ge(x_ready, 7)
            sp.dma_start(fin_g[:], t["final_norm_g"].rearrange("(a n) -> a n", a=1).to_broadcast([P, D_MODEL])) \
                .then_inc(s_fing, 16)
            for c in range(NCH):
                sp.wait_ge(fin_ready, c + 1)
                sp.dma_start(out[0, P * c:P * c + P, :], yacc[:, c, :]).then_inc(s_out, 16)
            sp.wait_ge(s_out, 16 * NCH)

        def raw_times(n):
            return 16 * (n // DENSE_RING + 1)

        def moe_raw_times(k, u, experts):
            before = sum(1 for n in range(N_DENSE) if n % DENSE_RING == k) if k < DENSE_RING else 0
            return experts * (16 * FU // MOE_RING) + 16 * (before + u // MOE_RING + 1)

        @block.scalar
        def _(act):
            copy = ACT.Copy
            roots = [0]

            def take_root(c0, c1):
                act.wait_ge(var_ready, roots[0] + 1)
                nc.scalar.activation(root[:, c0:c1], rstd[:, c0:c1], ACT.Sqrt).then_inc(root_ready, 1)
                roots[0] += 1

            def split(w):
                n = W_AT[w]
                act.wait_ge(raw_full[n % DENSE_RING], raw_times(n))
                if w >= SPLIT_RING:
                    act.wait_ge(units_pe, w - SPLIT_RING + 1)
                nc.scalar.activation(hi[w % SPLIT_RING][:], raw[n % DENSE_RING][:], copy).then_inc(split_hi, 1)

            def moe_split(u, e_units, experts):
                k, w = SLOT_ORDER[u % MOE_RING], W_MOE + u
                act.wait_ge(raw_full[k], moe_raw_times(k, u, experts))
                act.wait_ge(units_pe, e_units + (w - SPLIT_RING + 1))
                nc.scalar.activation(hi[w % SPLIT_RING][:], raw[k][:], copy).then_inc(split_hi, 1)

            def squares(k, c):
                if k == 0:
                    act.wait_ge(s_x, 16)
                else:
                    act.wait_ge(x_ready, 2 * (k - 1) + c + 1)
                nc.scalar.activation(xn[:, c, :], x_sb[:, c, :], ACT.Square, accum_out=ssq[:, c:c + 1]) \
                    .then_inc(ss_ready, 1)

            def norm_hi(k, c):
                for half in range(2):
                    act.wait_ge(val_ready, 4 * k + 2 * c + half + 1)
                    nc.scalar.activation(h_hi[:, 4 * half:4 * half + 4, P * c:P * c + P],
                                         val_t[:, 4 * half:4 * half + 4, P * c:P * c + P], copy).then_inc(h_hi_ready, 1)

            tables = [0]

            def root_table():
                nc.scalar.activation(warm[:, tables[0]:tables[0] + 1], ones[:, 0:1], ACT.Sqrt)
                tables[0] += 1

            def norm(k, w):
                root_table()
                squares(k, 0)
                take_root(0, 1)
                squares(k, 1)
                norm_hi(k, 0)
                split(w)
                take_root(1, 2)
                split(w + 1)
                norm_hi(k, 1)

            def down_hi(i, psum, free):
                act.wait_ge(t_done, i + 1)
                if free is not None:
                    act.wait_ge(units_pe, free)
                nc.scalar.activation(a_hi[:, (i - T_SGU) % 2, :, :], psum[:].rearrange("p (k n) -> p k n", k=2),
                                     copy).then_inc(at_hi, 1)

            act.wait_ge(s_vec, 80)
            nc.scalar.activation(sc[:], vecs[:, 32:40], ACT.Silu).then_inc(sc_ready, 1)

            def copy_row(k):
                act.wait_ge(row_summed, k + 1)
                if k >= 2:
                    act.wait_ge(acc_summed, k - 1)
                nc.scalar.activation(rows1[0:1, k % 2, :], bank[k % 3][0:1, :], copy).then_inc(row_copied, 1)

            copy_row(0)
            act.wait_ge(s_cst, 16)
            root_table()
            squares(0, 0)
            take_root(0, 1)
            copy_row(1)
            squares(0, 1)
            take_root(1, 2)
            copy_row(2)
            copy_row(3)

            def gating_gelu(b):
                act.wait_ge(units_pe, W_SGU_IN + 2 * b + 2)
                for c in range(NCH):
                    dst = (v_sb if b < 4 else u_sb)[:, c, 512 * (b % 4):512 * (b % 4) + 512]
                    nc.scalar.activation(dst, bank[BLOCK_BANKS[b % 2][c]][:], ACT.Gelu_apprx_tanh).then_inc(gelu_done, 1)

            split(W_SGU_IN)
            norm_hi(0, 0)
            split(W_SGU_IN + 1)
            norm_hi(0, 1)
            for b in range(1, 8):
                split(W_SGU_IN + 2 * b)
                split(W_SGU_IN + 2 * b + 1)
                gating_gelu(b - 1)
                if b == 4:
                    take_root(0, NCH)
            split(W_SGU_OUT)
            split(W_SGU_OUT + 1)
            gating_gelu(7)

            def down_phase(w0, t0, wnext):
                for j in range(1, 8):
                    if j + 1 < 8:
                        split(w0 + j + 1)
                    down_hi(t0 + j, bank[(2, 0)[j % 2]], w0 + j - 1 if j >= 2 else None)
                if wnext is not None:
                    split(wnext)

            down_hi(T_SGU, bank[2], None)
            down_phase(W_SGU_OUT, T_SGU, W_FFN)
            norm(1, W_FFN + 1)

            def ffn_silu(s, units, a0, tile, chunks, done):
                act.wait_ge(units_pe, units + (ffn_unit("B", s) + 1))
                if s >= 2:
                    act.wait_ge(t_done, a0 + (s - 1))
                for c in range(chunks):
                    b = c if chunks == 2 else s % 2
                    nc.scalar.activation(tile[:, s % 2, c, :], bank[b][:, 0:256], ACT.Silu).then_inc(silu_done, 1)

            def ffn_hi(s, units, t0, parity, chunks):
                act.wait_ge(t_done, t0 + (s + 1))
                act.wait_ge(units_pe, units + (ffn_unit("D", s - 2) + 1 if s >= 2 else 0))
                n = P * chunks
                nc.scalar.activation(a_hi[:, parity, :, 0:n], bank[2][:, 0:2 * n].rearrange("p (k n) -> p k n", k=2),
                                     copy).then_inc(at_hi, 1)

            for u, kind, s in FFN_ORDER:
                if u >= 3:
                    split(W_FFN + u)
                for s2 in range(STEPS):
                    if u == ffn_unit("B", s2) + 2:
                        ffn_silu(s2, W_FFN, T_FFN, fact, NCH, None)
                        if s2 >= 1:
                            ffn_hi(s2 - 1, W_FFN, T_FFN, (s2 - 1) % 2, NCH)
            ffn_hi(STEPS - 1, W_FFN, T_FFN, (STEPS - 1) % 2, NCH)

            split(W_RET_IN)
            act.wait_ge(ang_ready, 1)
            nc.scalar.activation(trig[:, :, :, :], trig[:, :, :, :], ACT.Sin).then_inc(trig_ready, 1)
            norm(2, W_RET_IN + 1)

            def qk_copy(b):
                for c in range(NCH):
                    act.wait_ge(qk_tr, 2 * b + c + 1)
                    dst = (q_t if b < 2 else k_t)[:, 4 * (b % 2):4 * (b % 2) + 4, P * c:P * c + P]
                    nc.scalar.activation(dst, bank[5 + c][:].rearrange("p (k n) -> p k n", k=4),
                                         copy).then_inc(qk_ready, 1)

            def ret_v(b):
                act.wait_ge(units_pe, W_RET_IN + 2 * b + 2)
                for c in range(NCH):
                    nc.scalar.activation(rv[:, c, 512 * (b - 4):512 * (b - 4) + 512], bank[BLOCK_BANKS[b % 2][c]][:],
                                         copy).then_inc(ret_act, 1)

            def ret_squares(h):
                act.wait_ge(o_done, h + 1)
                for c in range(NCH):
                    nc.scalar.activation(squares_o[:], bank[6 + c][:], ACT.Square, accum_out=oss[:, c:c + 1]) \
                        .then_inc(o_ss, 1)
                    act.wait_ge(o_ss, 2 * h + c + 1)
                take_root(0, NCH)

            def ret_gate(h):
                b = 8 + h
                act.wait_ge(units_pe, W_RET_IN + 2 * b + 2)
                if h >= 1:
                    act.wait_ge(og_done, h)
                for c in range(NCH):
                    nc.scalar.activation(silu_g[:, c, :], bank[BLOCK_BANKS[b % 2][c]][:], ACT.Silu).then_inc(ret_act, 1)

            for b in range(1, 12):
                if b > 1:
                    split(W_RET_IN + 2 * b)
                split(W_RET_IN + 2 * b + 1)
                if 4 <= b - 1 < 8:
                    ret_v(b - 1)
                if 2 <= b < 6:
                    qk_copy(b - 2)
                if b >= 8:
                    ret_squares(b - 8)
                if b >= 9:
                    ret_gate(b - 9)
            split(W_RET_OUT)
            ret_gate(3)
            down_hi(T_RET, bank[2], None)
            split(W_RET_OUT + 1)
            down_phase(W_RET_OUT, T_RET, W_MOE)
            root_table()
            squares(3, 0)
            take_root(0, 1)
            squares(3, 1)
            take_root(1, 2)
            split(W_MOE + 1)
            split(W_MOE + 2)

            nc.scalar.activation(warm[:, 6:7], ones[:, 0:1], ACT.Exp)
            act.wait_ge(top_ready, 1)
            nc.scalar.activation(wts[:, :, 1], wts[:, :, 0], ACT.Exp).then_inc(exp_done, 1)
            nc.scalar.activation(warm[:, 7:8], ones[:, 0:1], ACT.Silu)

            def gathered_hi(n):
                for half in range(2):
                    kts = slice(4 * half, 4 * half + 4)
                    act.wait_ge(gval_ready, n * 2 + (half - 1))
                    nc.scalar.activation(h_hi[:, kts, 0:P], gval[:, kts, :], copy).then_inc(g_hi_ready, 1)

            def take_output(units):
                act.wait_ge(units_pe, units + W_MOE)
                for half in range(2):
                    nc.scalar.activation(y_hi[:, 512 * half:512 * half + 512], bank[4 + half][:], copy).then_inc(y_out, 1)

            def expert(units, experts, steps, one, turn, last):
                for u, kind, s in FFN_ORDER:
                    if u >= 3:
                        moe_split(u, units, experts)
                    if u == 7:
                        act.wait_ge(pick_tr, one + 1)
                        nc.scalar.activation(pick_t[:, :, :], bank[3][:, 0:SEQ].rearrange("p (c n) -> p c n", c=NCH),
                                             copy).then_inc(pick_t_ready, 1)
                    for s2 in range(STEPS):
                        if u == ffn_unit("B", s2) + 2:
                            ffn_silu(s2, units + W_MOE, steps + T_DENSE, mact, 1, None)
                            if s2 >= 1:
                                ffn_hi(s2 - 1, units + W_MOE, steps + T_DENSE, (s2 - 1) % 2, 1)
                    if u == ffn_unit("B", STEPS - 1) + 2:
                        gathered_hi(turn + 2)
                ffn_hi(STEPS - 1, units + W_MOE, steps + T_DENSE, (STEPS - 1) % 2, 1)
                if not last:
                    moe_split(0, units + FU, experts + 1)
                    moe_split(1, units + FU, experts + 1)
                take_output(units + FU)
                if not last:
                    moe_split(2, units + FU, experts + 1)

            gathered_hi(1)
            take_output(0)
            with act.Fori(0, NE - 1) as e:
                expert(e * FU, e, e * STEPS, e, e, False)
            expert((NE - 1) * FU, NE - 1, (NE - 1) * STEPS, NE - 1, NE - 1, True)
            act.wait_ge(slots_ready, 1)
            n_most = act.value_load(most_i[0:1, 0:1], min_val=0, max_val=SEQ)
            with act.If(n_most > P):
                gathered_hi(NE + 2)
                for u in range(3):
                    moe_split(u, NE * FU, NE)
                take_output(NE * FU)
                with act.Fori(0, NE - 1) as e:
                    expert(e * FU + NE * FU, e + NE, e * STEPS + NE * STEPS, e + NE, e + NE + 1, False)
                expert((2 * NE - 1) * FU, 2 * NE - 1, (2 * NE - 1) * STEPS, 2 * NE - 1, 2 * NE, True)
            root_table()
            act.wait_ge(x_ready, 7)
            nc.scalar.activation(fin[:], x_sb[:, 0, :], ACT.Square, accum_out=ssq[:, 0:1]).then_inc(ss_ready, 1)
            take_root(0, 1)
            act.wait_ge(x_ready, 8)
            nc.scalar.activation(gval[:, :, :], x_sb[:, 1, :].rearrange("p (k n) -> p k n", k=KT), ACT.Square,
                                 accum_out=ssq[:, 1:2]).then_inc(ss_ready, 1)
            take_root(1, 2)

        @block.gpsimd
        def _(pool):
            nc.gpsimd.memset(acc0[:, :, :], 0.0).then_inc(acc0_zero, 1)

            def load_ln_rows(j):
                for i, name in enumerate(("sgu_ln_g", "sgu_ln_b")):
                    pool.dma_start(ln_rows[:, j % 2, i, :], t[name][0:1, 512 * j:512 * j + 512]
                                   .to_broadcast([P, 512])).then_inc(ln_full[j % 2], 16)

            pool.wait_ge(s_ws, 32)
            nc.gpsimd.affine_select(out=ws_raw[:, :, :], in_=ws_raw[:, :, :], compare_op=ALU.is_ge, fill=0.0, base=0,
                                    pattern=[[0, 8], [-1, P]], channel_multiplier=1).then_inc(ws_masked, 1)
            pool.wait_ge(h_ready, 4)
            load_ln_rows(0)
            load_ln_rows(1)
            for j in range(4):
                pool.wait_ge(v_norm, 2)
                pool.wait_ge(ln_full[j % 2], 32 * (j // 2 + 1))
                for c in range(NCH):
                    v = v_sb[:, c, 512 * j:512 * j + 512]
                    nc.gpsimd.tensor_tensor(v, v, ln_rows[:, j % 2, 0, :], ALU.mult).then_inc(v_scaled, 1)
                    pool.wait_ge(v_scaled, 2 * j + c + 1)
                    last = nc.gpsimd.tensor_tensor(v, v, ln_rows[:, j % 2, 1, :], ALU.add)
                last.then_inc(v_ready, 1)
                if j < 2:
                    pool.wait_ge(v_ready, j + 1)
                    load_ln_rows(j + 2)
            pool.wait_ge(y_blk, 4)
            pool.dma_start(trig[:, 0, 0, :], t["inv_freq"].to_broadcast([P, P])).then_inc(s_invf, 16)
            pool.wait_ge(h_ready, 12)
            pool.dma_start(decay[:], t["decay"].rearrange("p (h n) -> p h n", h=HEADS)).then_inc(s_decay, 16)
            pool.wait_ge(x_ready, 6)
            nc.gpsimd.memset(yacc[:, :, :], 0.0).then_inc(yacc_zero, 1)
            nc.gpsimd.memset(pick_t[:, :, :].bitcast(f32), 0.0).then_inc(pick_t_ready, 1)

        @block.vector
        def _(dve):
            seq = [0]

            def link(ins):
                seq[0] += 1
                ins.then_inc(dve_seq, 1)
                dve.wait_ge(dve_seq, seq[0])

            V = nc.vector
            roots = [0]

            def rsqrt(src, c0, c1, scale):
                var, r, s = rstd[:, c0:c1], root[:, c0:c1], step_t[:, c0:c1]
                V.tensor_scalar(var, src, scale, EPS, ALU.mult, ALU.add).then_inc(var_ready, 1)
                roots[0] += 1
                dve.wait_ge(root_ready, roots[0])
                link(V.reciprocal(r, r))
                link(V.tensor_tensor(s, r, r, ALU.mult))
                link(V.tensor_tensor(s, s, var, ALU.mult))
                link(V.tensor_scalar(s, s, -0.5, 1.5, ALU.mult, ALU.add))
                link(V.tensor_tensor(var, r, s, ALU.mult))

            def split(w):
                n = W_AT[w]
                dve.wait_ge(split_hi, w + 1)
                if w >= SPLIT_RING:
                    dve.wait_ge(units_pe, w - SPLIT_RING + 1)
                V.tensor_tensor(lo[w % SPLIT_RING][:], raw[n % DENSE_RING][:], hi[w % SPLIT_RING][:].bitcast(f32),
                                ALU.subtract).then_inc(units_dve, 1)

            chain = [None, None]

            def ada(i):
                n = A_AT[i]
                k, half = divmod(i, 2)
                dve.wait_ge(raw_full[n % DENSE_RING], raw_times(n))
                if half == 0:
                    dve.wait_ge(acc0_full[k % 2], 16 * (k // 2 + 1))
                    if k >= 2:
                        dve.wait_ge(acc_summed, k - 1)
                for kk in range(4):
                    for side in range(2):
                        cols = slice(256 * side, 256 * side + 256)
                        a, first = acc[:, k % 2, cols], half == 0 and kk == 0
                        if not first:
                            dve.wait_ge(*chain[side])
                        ins = V.scalar_tensor_tensor(
                            out=a, in0=raw[n % DENSE_RING][:, 512 * kk + 256 * side:512 * kk + 256 * side + 256],
                            scalar=sc[:, 4 * half + kk:4 * half + kk + 1],
                            in1=acc0[:, k % 2, cols] if first else a, op0=ALU.mult, op1=ALU.add)
                        if side == 1 and first:
                            ins.then_inc(acc0_used, 1)
                            chain[side] = (acc0_used, k + 1)
                        elif side == 1 and kk == 3:
                            both = k < 4
                            ins.then_inc(units_dve, 2 if both else 1)
                            chain[side] = (units_dve, n + 2 if both else n + 1)
                        else:
                            seq[0] += 1
                            ins.then_inc(dve_seq, 1)
                            chain[side] = (dve_seq, seq[0])

            def mod(k):
                dve.wait_ge(acc_summed, k + 1)
                layer, b = divmod(k, 12)
                part, half = divmod(b, 2)
                if part in (2, 5):
                    dst, src = (gate1 if part == 2 else gate2)[:, 512 * half:512 * half + 512], bank[ADA_BANK][:]
                else:
                    i = {0: 0, 1: 1, 3: 2, 4: 3}[part]
                    rows = slice(64 * half, 64 * half + 64)
                    dst, src = mods[rows, layer, i, :], bank[ADA_BANK][rows, 0:KT]
                V.tensor_copy(dst, src).then_inc(mod_ready, 1)

            def normalize(k, c):
                dve.wait_ge(ss_ready, 2 * k + c + 1)
                rsqrt(ssq[:, c:c + 1], c, c + 1, 1.0 / D_MODEL)
                V.tensor_scalar(xn[:, c, :], x_sb[:, c, :], rstd[:, c:c + 1], None, ALU.mult).then_inc(xn_ready, 1)

            def norm_scale(k):
                layer, second = divmod(k, 2)
                dve.wait_ge(mod_ready, 12 * layer + (4 if not second else 10))
                dve.wait_ge(s_vec, 80)
                link(V.tensor_scalar(mulv[:], mods[:, layer, 2 * second + 1, :], 1.0, None, ALU.add))
                link(V.tensor_tensor(mulv[:], mulv[:], vecs[:, 8 * k:8 * k + 8], ALU.mult))

            def norm_values(k, c):
                layer, second = divmod(k, 2)
                for half in range(2):
                    j = 2 * c + half
                    dve.wait_ge(tr_ready, 4 * k + j + 1)
                    for q in range(4):
                        kt = 4 * half + q
                        last = V.tensor_scalar(val_t[:, kt, P * c:P * c + P], bank[4 + j][:, P * q:P * q + P],
                                               mulv[:, kt:kt + 1], mods[:, layer, 2 * second, kt:kt + 1],
                                               ALU.mult, ALU.add)
                    last.then_inc(val_ready, 1)
                if k < 3:
                    for half in range(2):
                        dve.wait_ge(h_hi_ready, 4 * k + 2 * c + half + 1)
                        at4 = (slice(None), slice(4 * half, 4 * half + 4), slice(P * c, P * c + P))
                        V.tensor_tensor(h_lo[at4], val_t[at4], h_hi[at4].bitcast(f32), ALU.subtract).then_inc(h_ready, 1)

            def residual_norm(k, gate, units, w):
                norm_scale(k)
                dve.wait_ge(first_chunk, k)
                add_output(gate, 0)
                normalize(k, 0)
                dve.wait_ge(units_pe, units)
                add_output(gate, 1)
                norm_values(k, 0)
                if w is not None:
                    split(w)
                normalize(k, 1)
                if w is not None:
                    split(w + 1)
                norm_values(k, 1)

            def down_lo(i, psum):
                dve.wait_ge(at_hi, i + 1)
                V.tensor_tensor(a_lo[:, i % 2, :, :], psum[:].rearrange("p (k n) -> p k n", k=2),
                                a_hi[:, i % 2, :, :].bitcast(f32), ALU.subtract).then_inc(at_ready, 1)

            def add_output(gate, c):
                for half in range(2):
                    cols = slice(512 * half, 512 * half + 512)
                    y = out_tmp[:, 2 * c + half, :]
                    link(V.tensor_tensor(y, bank[4 + 2 * c + half][:], gate[:, cols], ALU.mult))
                    last = V.tensor_tensor(x_sb[:, c, cols], x_sb[:, c, cols], y, ALU.add)
                last.then_inc(x_ready, 1)

            dve.wait_ge(sc_ready, 1)
            for k in range(4):
                ada(2 * k)
                if k:
                    mod(k - 1)
                    if k < 3:
                        normalize(0, k - 1)
            mod(3)
            norm_scale(0)
            split(W_SGU_IN)
            norm_values(0, 0)
            split(W_SGU_IN + 1)
            norm_values(0, 1)

            ada(8)
            dve.wait_ge(ws_tr, 1)
            V.tensor_copy(bs_t[:], bank[7][:, 0:8])
            V.tensor_copy(ws_t[:, 0:4, :], bank[5][:].rearrange("p (g n) -> p g n", g=4)).then_inc(ws_ready, 1)
            V.tensor_copy(ws_t[:, 4:8, :], bank[6][:].rearrange("p (g n) -> p g n", g=4)).then_inc(ws_ready, 1)

            def gating_out(j):
                dve.wait_ge(fv_done, j + 1)
                dve.wait_ge(gelu_done, 8 + 2 * (j + 1))
                for c in range(NCH):
                    for g in range(2):
                        u = u_sb[:, c, 512 * j + 256 * g:512 * j + 256 * g + 256]
                        last = V.scalar_tensor_tensor(out=u, in0=bank[5 + c][:, 256 * g:256 * g + 256],
                                                      scalar=bs_t[:, 2 * j + g:2 * j + g + 1], in1=u,
                                                      op0=ALU.add, op1=ALU.mult)
                last.then_inc(y_blk, 1)

            for b in range(1, 8):
                split(W_SGU_IN + 2 * b)
                split(W_SGU_IN + 2 * b + 1)
                ada(8 + b)
                if b % 2 and b > 1:
                    mod(4 + b // 2 - 1)
                if b - 1 < 4:
                    for c in range(NCH):
                        dve.wait_ge(gelu_done, 2 * (b - 1) + c + 1)
                        ins = V.bn_stats(stats[:, c, b - 1, :], v_sb[:, c, 512 * (b - 1):512 * b])
                        if b == 4:
                            link(ins)
                if b == 4:
                    for c in range(NCH):
                        link(V.bn_aggr(mv[:, c, :], stats[:, c, :, :]))
                    rsqrt(mv[:, :, 1], 0, NCH, 1.0)
                    for c in range(NCH):
                        V.tensor_scalar(v_sb[:, c, :], v_sb[:, c, :], mv[:, c, 0:1], rstd[:, c:c + 1],
                                        ALU.subtract, ALU.mult).then_inc(v_norm, 1)
            gating_out(0)

            split(W_SGU_OUT)
            ada(16)
            mod(7)
            split(W_SGU_OUT + 1)
            for j in range(1, 4):
                gating_out(j)
            down_lo(T_SGU, bank[2])
            for j in range(1, 8):
                if j < 7:
                    split(W_SGU_OUT + j + 1)
                    if j % 2 == 1 and j < 6:
                        ada(17 + j // 2)
                    if j == 4:
                        mod(8)
                down_lo(T_SGU + j, bank[(2, 0)[j % 2]])
            mod(9)
            split(W_FFN)
            residual_norm(1, gate1, W_FFN, W_FFN + 1)

            def ffn_act(s, silu0, tile, chunks):
                for c in range(chunks):
                    dve.wait_ge(silu_done, silu0 + (chunks * s + c + 1))
                    b = c if chunks == 2 else s % 2
                    last = V.tensor_tensor(tile[:, s % 2, c, :], tile[:, s % 2, c, :], bank[b][:, 256:512], ALU.mult)
                last.then_inc(act_ready, 1)

            def ffn_lo(s, t0, parity, chunks):
                dve.wait_ge(at_hi, t0 + (s + 1))
                n = P * chunks
                V.tensor_tensor(a_lo[:, parity, :, 0:n], bank[2][:, 0:2 * n].rearrange("p (k n) -> p k n", k=2),
                                a_hi[:, parity, :, 0:n].bitcast(f32), ALU.subtract).then_inc(at_ready, 1)

            for u, kind, s in FFN_ORDER:
                if u >= 3:
                    split(W_FFN + u)
                if (kind, s) in FFN_ADA:
                    ada(FFN_ADA[kind, s])
                if kind == "D" and s in (0, 1, 3, 5, 7):
                    mod(10 + (s + 1) // 2)
                for s2 in range(STEPS):
                    if u == ffn_unit("B", s2) + 2:
                        ffn_act(s2, 0, fact, NCH)
                        if s2 >= 1:
                            ffn_lo(s2 - 1, T_FFN, (s2 - 1) % 2, NCH)
            ffn_lo(STEPS - 1, T_FFN, (STEPS - 1) % 2, NCH)
            mod(15)

            split(W_RET_IN)
            dve.wait_ge(s_invf, 16)
            dve.wait_ge(s_pos, 16)
            link(V.tensor_copy(pos_f[:], pos_i[:]))
            for c in range(NCH):
                link(V.tensor_scalar(trig[:, 1, c, :], trig[:, 0, 0, :], pos_f[:, c:c + 1], None, ALU.mult))
            for fn in range(2):
                a, turn, dst = trig[:, 1, :, :], rope_tmp[:, :, :], trig[:, fn, :, :]
                link(V.tensor_scalar(turn, a, 1.0 / (2 * np.pi), 0.25 if fn == 0 else 0.0, ALU.mult, ALU.add))
                link(V.tensor_scalar(turn, turn, MAGIC, MAGIC, ALU.add, ALU.subtract))
                link(V.scalar_tensor_tensor(out=dst, in0=turn, scalar=-TWO_PI_HI, in1=a, op0=ALU.mult, op1=ALU.add))
                link(V.scalar_tensor_tensor(out=dst, in0=turn, scalar=-TWO_PI_MID, in1=dst, op0=ALU.mult, op1=ALU.add))
                link(V.scalar_tensor_tensor(out=dst, in0=turn, scalar=-TWO_PI_LO, in1=dst, op0=ALU.mult, op1=ALU.add))
                if fn == 0:
                    link(V.tensor_scalar(dst, dst, np.pi / 2, None, ALU.add))
                last = V.tensor_scalar(dst, dst, SIN_MAX, -SIN_MAX, ALU.min, ALU.max)
                if fn == 0:
                    link(last)
            last.then_inc(ang_ready, 1)
            residual_norm(2, gate2, W_RET_IN, W_RET_IN + 1)

            def rotate(b):
                dve.wait_ge(units_pe, W_RET_IN + 2 * b + 2)
                for c in range(NCH):
                    if b:
                        dve.wait_ge(qk_tr, 2 * (b - 1) + c + 1)
                    ps = bank[BLOCK_BANKS[b % 2][c]][:].rearrange("p (h s f) -> p h s f", h=2, s=2)
                    r = rope[:, c, :].rearrange("p (h s f) -> p h s f", h=2, s=2)
                    t1, t2, r1, r2 = ps[:, :, 0, :], ps[:, :, 1, :], r[:, :, 0, :], r[:, :, 1, :]
                    cos, sin = (trig[:, i, c:c + 1, :].broadcast_to([P, 2, P]) for i in range(2))
                    link(V.tensor_tensor(rope_tmp[:, :, :], t2, sin, ALU.mult))
                    link(V.tensor_tensor(r1, t1, cos, ALU.mult))
                    link(V.tensor_tensor(r1, r1, rope_tmp[:, :, :], ALU.subtract))
                    link(V.tensor_tensor(rope_tmp[:, :, :], t1, sin, ALU.mult))
                    link(V.tensor_tensor(r2, t2, cos, ALU.mult))
                    V.tensor_tensor(r2, r2, rope_tmp[:, :, :], ALU.add).then_inc(rope_done, 1)
                    dve.wait_ge(rope_done, 2 * b + c + 1)

            def score(h):
                dve.wait_ge(scores_done, h + 1)
                dve.wait_ge(s_decay, 16)
                if h:
                    dve.wait_ge(o_done, h)
                V.tensor_tensor(sc_t[:, 0:256], bank[5][:, 0:256], decay[:, h, :], ALU.mult)
                V.tensor_tensor(sc_t[:, 256:384], bank[5][:, 256:384], decay[:, h, 0:P], ALU.mult) \
                    .then_inc(sct_ready, 1)

            def o_norm(h):
                dve.wait_ge(o_ss, 2 * h + 2)
                rsqrt(oss[:, :], 0, NCH, 1.0 / DV)
                for c in range(NCH):
                    last = V.tensor_scalar(rv[:, c, 512 * h:512 * h + 512], bank[6 + c][:], rstd[:, c:c + 1], None,
                                           ALU.mult)
                last.then_inc(onorm_done, 1)

            def gate_out(h):
                dve.wait_ge(onorm_done, h + 1)
                dve.wait_ge(ret_act, 8 + 2 * h + 2)
                for c in range(NCH):
                    o = rv[:, c, 512 * h:512 * h + 512]
                    last = V.tensor_tensor(o, o, silu_g[:, c, :], ALU.mult)
                last.then_inc(og_done, 1)

            for b in range(1, 12):
                if b > 1:
                    split(W_RET_IN + 2 * b)
                else:
                    ada(32)
                if 7 <= b <= 10:
                    score(b - 7)
                split(W_RET_IN + 2 * b + 1)
                ada(32 + b)
                if b % 2 and b > 1:
                    mod(16 + b // 2 - 1)
                if b - 1 < 4:
                    if b == 1:
                        dve.wait_ge(trig_ready, 1)
                    rotate(b - 1)
                if b >= 8:
                    o_norm(b - 8)
                if b >= 9:
                    gate_out(b - 9)
            split(W_RET_OUT)
            gate_out(3)
            dve.wait_ge(og_done, 4)
            down_lo(T_RET, bank[2])
            ada(44)
            mod(21)
            split(W_RET_OUT + 1)
            ada(45)
            for j in range(1, 8):
                if j < 7:
                    split(W_RET_OUT + j + 1)
                if j < 3:
                    ada(45 + j)
                if j == 1:
                    mod(22)
                if j == 4:
                    mod(23)
                down_lo(T_RET + j, bank[(2, 0)[j % 2]])
            split(W_MOE)
            residual_norm(3, gate1, W_MOE, None)

            split(W_MOE + 1)
            dve.wait_ge(s_wr, 32)
            for c in range(NCH):
                dve.wait_ge(router_done, c + 1)
                link(V.tensor_tensor(logit[:, c, :], bank[c][:, 0:NE], brow[:], ALU.add))
                link(V.max(top[:, c, :], logit[:, c, :]))
                link(V.max_index(topi[:, c, :], top[:, c, :], logit[:, c, :]))
            link(V.tensor_copy(topf[:, :, :], topi[:, :, :]))
            V.tensor_tensor(wts[:, :, 0], top[:, :, 1], top[:, :, 0], ALU.subtract).then_inc(top_ready, 1)
            for c in range(NCH):
                for i in range(2):
                    ins = V.tensor_scalar(oh[:, i, c, :], iota[:, 0:NE], topf[:, c, i:i + 1], None, ALU.is_equal)
            link(ins)
            V.tensor_tensor(m_sel[:, :, :], oh[:, 0, :, :], oh[:, 1, :, :], ALU.add).then_inc(sel_ready, 1)
            dve.wait_ge(exp_done, 1)
            link(V.tensor_scalar(wts[:, :, 2], wts[:, :, 1], 1.0, None, ALU.add))
            link(V.reciprocal(wts[:, :, 2], wts[:, :, 2]))
            link(V.tensor_tensor(wts[:, :, 3], wts[:, :, 1], wts[:, :, 2], ALU.mult))
            for c in range(NCH):
                link(V.tensor_scalar(gates[:, c, 1:], oh[:, 0, c, :], wts[:, c, 2:3], None, ALU.mult))
                link(V.scalar_tensor_tensor(out=gates[:, c, 1:], in0=oh[:, 1, c, :], scalar=wts[:, c, 3:4],
                                            in1=gates[:, c, 1:], op0=ALU.mult, op1=ALU.add))
            dve.wait_ge(pos_done, 1)
            for c in range(NCH):
                link(V.scalar_tensor_tensor(out=slot[:, c, 0:NE], in0=bank[ADA_BANK][:, 8 * c:8 * c + 8], scalar=1.0,
                                            in1=m_sel[:, c, :], op0=ALU.add, op1=ALU.mult))
                link(V.tensor_scalar(slot[:, c, 0:NE], slot[:, c, 0:NE], 1.0, None, ALU.subtract))
            V.memset(slot[:, :, NE:], -1.0)
            link(V.memset(gates[:, :, 0:1], 0.0))
            link(V.reduce_max(most[:], bank[ADA_BANK][:, 16:24], AX.X))
            V.tensor_copy(most_i[:], most[:]).then_inc(slots_ready, 1)
            dve.wait_ge(yacc_zero, 1)

            def moe_split(u, units):
                k, w = SLOT_ORDER[u % MOE_RING], W_MOE + u
                dve.wait_ge(split_hi, units + (w + 1))
                dve.wait_ge(units_pe, units + (w - SPLIT_RING + 1))
                V.tensor_tensor(lo[w % SPLIT_RING][:], raw[k][:], hi[w % SPLIT_RING][:].bitcast(f32),
                                ALU.subtract).then_inc(units_dve, 1)

            def pick_tokens(e):
                for c in range(NCH):
                    last = V.tensor_scalar(pick[:, c, :], iota, slot[:, c, bass.ds(e, 1)], None, ALU.is_equal)
                last.then_inc(pick_ready, 1)

            def gathered_values(n):
                for half in range(2):
                    dve.wait_ge(gathered, n * 2 + (half - 1))
                    for kt in range(4 * half, 4 * half + 4):
                        last = V.tensor_scalar(gval[:, kt, :], bank[6 + half][:, P * (kt % 4):P * (kt % 4) + P],
                                               mulv[:, kt:kt + 1], mods[:, 1, 2, kt:kt + 1], ALU.mult, ALU.add)
                    last.then_inc(gval_ready, 1)

            def gathered_lo(n):
                for half in range(2):
                    kts = slice(4 * half, 4 * half + 4)
                    dve.wait_ge(g_hi_ready, n * 2 + (half - 1))
                    V.tensor_tensor(h_lo[:, kts, 0:P], gval[:, kts, :], h_hi[:, kts, 0:P].bitcast(f32),
                                    ALU.subtract).then_inc(g_ready, 1)

            def scatter_add(n, c, col, b):
                dve.wait_ge(scattered, n)
                for half in range(2):
                    cols = slice(512 * half, 512 * half + 512)
                    last = V.scalar_tensor_tensor(out=yacc[:, c, cols], in0=bank[b + half][:],
                                                  scalar=gates[:, c, bass.ds(col, 1)], in1=yacc[:, c, cols],
                                                  op0=ALU.mult, op1=ALU.add)
                last.then_inc(yacc_done, 1)
                dve.wait_ge(yacc_done, n)

            def output_lo(n):
                dve.wait_ge(y_out, n * 2)
                for half in range(2):
                    cols = slice(512 * half, 512 * half + 512)
                    last = V.tensor_tensor(y_lo[:, cols], bank[4 + half][:], y_hi[:, cols].bitcast(f32), ALU.subtract)
                last.then_inc(y_split, 1)

            def expert(e, units, steps, one, turn, final):
                for u, kind, s in FFN_ORDER:
                    if u >= 3:
                        moe_split(u, units)
                    if u in (3, 5):
                        c = (u - 3) // 2
                        scatter_add(turn * NCH + (c + 1), c, e, 6)
                    if u == 25:
                        dve.wait_ge(pick_tr, one + 1)
                        pick_tokens(e + 1)
                    if u == 30:
                        dve.wait_ge(g_ready, turn * 2 + 2)
                        gathered_values(turn + 2)
                    for s2 in range(STEPS):
                        if u == ffn_unit("B", s2) + 2:
                            ffn_act(s2, steps + NCH * STEPS, mact, 1)
                            if s2 >= 1:
                                ffn_lo(s2 - 1, steps + T_DENSE, (s2 - 1) % 2, 1)
                    if u == ffn_unit("B", STEPS - 1) + 2:
                        gathered_lo(turn + 2)
                ffn_lo(STEPS - 1, steps + T_DENSE, (STEPS - 1) % 2, 1)
                if not final:
                    moe_split(0, units + FU)
                    moe_split(1, units + FU)
                output_lo(turn + 2)
                if not final:
                    moe_split(2, units + FU)

            def last_scatter(n):
                scatter_add(n + 1, 0, NE, 6)
                scatter_add(n + 2, 1, NE, 4)

            pick_tokens(0)
            split(W_MOE + 2)
            gathered_values(1)
            gathered_lo(1)
            output_lo(1)
            with dve.Fori(0, NE - 1) as e:
                expert(e, e * FU, e * STEPS, e, e, False)
            expert(NE - 1, (NE - 1) * FU, (NE - 1) * STEPS, NE - 1, NE - 1, True)
            last_scatter(NCH * NE)
            n_most = dve.value_load(most_i[0:1, 0:1], min_val=0, max_val=SEQ)
            with dve.If(n_most > P):
                V.tensor_scalar(slot[:, :, :], slot[:, :, :], float(P), None, ALU.subtract).then_inc(slots_ready, 1)
                dve.wait_ge(slots_ready, 2)
                pick_tokens(0)
                gathered_values(NE + 2)
                gathered_lo(NE + 2)
                for u in range(3):
                    moe_split(u, NE * FU)
                output_lo(NE + 2)
                with dve.Fori(0, NE - 1) as e:
                    expert(e, e * FU + NE * FU, e * STEPS + NE * STEPS, e + NE, e + NE + 1, False)
                expert(NE - 1, (2 * NE - 1) * FU, (2 * NE - 1) * STEPS, 2 * NE - 1, 2 * NE, True)
                last_scatter(NCH * (2 * NE + 1))

            for c in range(NCH):
                link(V.tensor_tensor(yacc[:, c, :], yacc[:, c, :], gate2[:], ALU.mult))
                V.tensor_tensor(x_sb[:, c, :], x_sb[:, c, :], yacc[:, c, :], ALU.add).then_inc(x_ready, 1)
            dve.wait_ge(s_fing, 16)
            for c in range(NCH):
                dve.wait_ge(ss_ready, 8 + c + 1)
                rsqrt(ssq[:, c:c + 1], c, c + 1, 1.0 / D_MODEL)
                V.scalar_tensor_tensor(out=yacc[:, c, :], in0=x_sb[:, c, :], scalar=rstd[:, c:c + 1], in1=fin_g[:],
                                       op0=ALU.mult, op1=ALU.mult).then_inc(fin_ready, 1)

        @block.tensor
        def _(pe):
            mm, tr = nc.tensor.matmul, nc.tensor.transpose

            def in_part(w, half, b, c):
                wh, wl = hi[w % SPLIT_RING], lo[w % SPLIT_RING]
                for kk in range(4):
                    kt = 4 * half + kk
                    ah, al = h_hi[:, kt, P * c:P * c + P], h_lo[:, kt, P * c:P * c + P]
                    cols = slice(512 * kk, 512 * kk + 512)
                    mm(bank[b][:], ah, wh[:, cols], start=kt == 0, stop=False)
                    mm(bank[b][:], ah, wl[:, cols], start=False, stop=False)
                    last = mm(bank[b][:], al, wh[:, cols], start=False, stop=kt == KT - 1)
                return last

            def in_unit(w, half, banks, chunks):
                for c in range(chunks):
                    last = in_part(w, half, banks[c], c)
                last.then_inc(units_pe, 1)

            def down_part(w, parity, first, final, c):
                wh, wl = hi[w % SPLIT_RING], lo[w % SPLIT_RING]
                for kk in range(2):
                    ah, al = (a[:, parity, kk, P * c:P * c + P] for a in (a_hi, a_lo))
                    for half in range(2):
                        o = bank[4 + 2 * c + half][:]
                        cols = slice(1024 * kk + 512 * half, 1024 * kk + 512 * half + 512)
                        mm(o, ah, wh[:, cols], start=first and kk == 0, stop=False)
                        mm(o, ah, wl[:, cols], start=False, stop=False)
                        last = mm(o, al, wh[:, cols], start=False, stop=final and kk == 1)
                return last

            def down_unit(w, parity, first, final, chunks):
                for c in range(chunks):
                    last = down_part(w, parity, first, final, c)
                last.then_inc(units_pe, 1)

            def last_downs(w, i):
                down_part(w, i % 2, False, False, 0)
                unit_here(w + 1)
                pe.wait_ge(at_ready, i + 2)
                down_part(w + 1, (i + 1) % 2, False, True, 0).then_inc(first_chunk, 1)
                down_part(w, i % 2, False, False, 1).then_inc(units_pe, 1)
                down_part(w + 1, (i + 1) % 2, False, True, 1).then_inc(units_pe, 1)

            def first_block(k, w, banks):
                if k:
                    norm_transposes(k, 0)
                for c in range(NCH):
                    pe.wait_ge(h_ready, 4 * k + 2 * c + 2)
                    for half in range(2):
                        if c == 0:
                            unit_here(w + half)
                        last = in_part(w + half, half, banks[c], c)
                        if c == 1:
                            last.then_inc(units_pe, 1)
                        elif half == 0 and k:
                            norm_transposes(k, 1)

            def unit_here(w):
                pe.wait_ge(units_dve, W_AT[w] + 1)

            def tile_of(a, c, kt):
                return a[:, c, :].rearrange("p (q k) -> p k q", k=KT)[:, kt, :]

            def norm_transposes(k, c):
                for j in (2 * c, 2 * c + 1):
                    half = j % 2
                    pe.wait_ge(xn_ready, 2 * k + c + 1)
                    for q in range(4):
                        kt = 4 * half + q
                        last = tr(bank[4 + j][:, P * q:P * q + P], tile_of(xn, c, kt), ident)
                    last.then_inc(tr_ready, 1)

            def ada_sum(k):
                pe.wait_ge(units_dve, A_AT[2 * k + 1] + 1)
                if k:
                    pe.wait_ge(mod_ready, k)
                a = acc[:, k % 2, :]
                if (k % 12) // 2 in (2, 5):
                    mm(bank[ADA_BANK][:], ones, a, start=True, stop=True).then_inc(acc_summed, 1)
                else:
                    rows = slice(64 * (k % 2), 64 * (k % 2) + 64)
                    cols = a.rearrange("p (q k) -> p k q", k=KT)
                    row = rows1[:, k % 2, :].rearrange("p (q k) -> p k q", k=KT)
                    if k < 4:
                        pe.wait_ge(row_copied, k + 1)
                    for kt in range(KT):
                        o = bank[ADA_BANK][rows, kt:kt + 1]
                        last = mm(o, cols[:, kt, :], ones[:, 0:1], start=True, stop=k >= 4)
                        if k < 4:
                            last = mm(o, row[0:1, kt, :], ones[0:1, 0:1], start=False, stop=True)
                    last.then_inc(acc_summed, 1)

            def row_sum(k):
                n = A_AT[2 * k + 1]
                pe.wait_ge(raw_full[n % DENSE_RING], raw_times(n))
                b = bank[k % 3]
                if k == 3:
                    pe.wait_ge(row_copied, 1)
                for kk in range(4):
                    last = mm(b[0:1, :], sc[:, 4 + kk:5 + kk], raw[n % DENSE_RING][:, 512 * kk:512 * kk + 512],
                              start=kk == 0, stop=kk == 3)
                last.then_inc(row_summed, 1)

            pe.wait_ge(sc_ready, 1)
            for k in range(4):
                row_sum(k)
                if k == 0:
                    pe.wait_ge(s_cst, 16)
                else:
                    ada_sum(k - 1)
                if k == 3:
                    norm_transposes(0, 0)
                    norm_transposes(0, 1)
            ada_sum(3)

            def weights_transposed():
                pe.wait_ge(ws_masked, 1)
                tr(bank[7][:, 0:8], bs_rows[0:8, :], ident[0:8, 0:8])
                for g in range(8):
                    last = tr(bank[5 + g // 4][:, P * (g % 4):P * (g % 4) + P], ws_raw[:, g, :], ident)
                last.then_inc(ws_tr, 1)

            def spatial(j):
                pe.wait_ge(v_ready, j + 1)
                pe.wait_ge(ws_ready, 2)
                if j:
                    pe.wait_ge(y_blk, j)
                for c in range(NCH):
                    for g in range(2):
                        last = mm(bank[5 + c][:, 256 * g:256 * g + 256], ws_t[:, 2 * j + g, :],
                                  v_sb[:, c, 512 * j + 256 * g:512 * j + 256 * g + 256], start=True, stop=True)
                last.then_inc(fv_done, 1)

            first_block(0, W_SGU_IN, BLOCK_BANKS[0])
            weights_transposed()
            for b in range(1, 8):
                if b >= 2:
                    pe.wait_ge(gelu_done, 2 * (b - 1))
                for half in range(2):
                    w = W_SGU_IN + 2 * b + half
                    unit_here(w)
                    in_unit(w, half, BLOCK_BANKS[b % 2], NCH)
                    if half == 0 and b % 2 == 0 and b:
                        ada_sum(4 + b // 2 - 1)
                if b == 7:
                    ada_sum(7)
                if b >= 6:
                    spatial(b - 6)
            spatial(2)
            spatial(3)

            def down_transposes(j, src, b):
                for kk in range(2):
                    for c in range(NCH):
                        n = SEQ * kk + P * c
                        last = tr(bank[b][:, n:n + P], src[:, c, 256 * j + P * kk:256 * j + P * kk + P], ident)
                last.then_inc(t_done, 1)

            def down_phase(w0, t0, src, ready, banks_read, sums):
                for j in range(8):
                    if j % 2 == 0:
                        pe.wait_ge(ready, j // 2 + 1)
                    if j >= 2:
                        pe.wait_ge(at_ready, t0 + j - 1)
                    down_transposes(j, src, (2, 0)[j % 2])
                    if j >= 1:
                        w, i = w0 + j - 1, t0 + j - 1
                        unit_here(w)
                        pe.wait_ge(at_ready, i + 1)
                        if j == 1:
                            pe.wait_ge(banks_read, 4)
                        if j == 7:
                            last_downs(w, i)
                        else:
                            down_unit(w, i % 2, j == 1, False, NCH)
                        if j in sums:
                            ada_sum(sums[j])

            pe.wait_ge(gelu_done, 16)
            down_phase(W_SGU_OUT, T_SGU, u_sb, y_blk, y_blk, {2: 8, 6: 9})


            def ffn_transposes(s, tile, chunks):
                for kk in range(2):
                    for c in range(chunks):
                        n = P * (chunks * kk + c)
                        last = tr(bank[2][:, n:n + P], tile[:, s % 2, c, P * kk:P * kk + P], ident)
                last.then_inc(t_done, 1)

            first_block(1, W_FFN, (0, 1))
            for u, kind, s in FFN_ORDER[2:-1]:
                w = W_FFN + u
                if kind == "A":
                    pe.wait_ge(act_ready, s)
                if kind == "D":
                    pe.wait_ge(at_ready, T_FFN + s + 1)
                    if s == STEPS - 2:
                        pe.wait_ge(act_ready, STEPS)
                        ffn_transposes(s + 1, fact, NCH)
                unit_here(w)
                if kind == "D" and s == STEPS - 2:
                    last_downs(w, T_FFN + s)
                elif kind == "D":
                    down_unit(w, s % 2, s == 0, False, NCH)
                else:
                    in_unit(w, int(kind == "B"), (0, 1), NCH)
                if kind == "B" and s:
                    pe.wait_ge(act_ready, s)
                    pe.wait_ge(at_ready, T_FFN + s - 1)
                    ffn_transposes(s - 1, fact, NCH)
                if kind == "A" and s in (2, 3, 5, 7, 9):
                    ada_sum(10 + (s - 1) // 2)
                if kind == "D" and s == STEPS - 3:
                    ada_sum(15)

            def qk_transposes(b):
                for c in range(NCH):
                    pe.wait_ge(rope_done, 2 * b + c + 1)
                    if b:
                        pe.wait_ge(qk_ready, 2 * (b - 1) + c + 1)
                    for i in range(4):
                        last = tr(bank[5 + c][:, P * i:P * i + P], rope[:, c, P * i:P * i + P], ident)
                    last.then_inc(qk_tr, 1)

            def scores(h):
                pe.wait_ge(qk_ready, 8)
                if h:
                    pe.wait_ge(sct_ready, h)
                for o, keys, queries in (((0, 256), (0, P), (0, SEQ)), ((256, 384), (P, SEQ), (P, SEQ))):
                    for kk in range(2):
                        last = mm(bank[5][:, o[0]:o[1]], k_t[:, 2 * h + kk, keys[0]:keys[1]],
                                  q_t[:, 2 * h + kk, queries[0]:queries[1]], start=kk == 0, stop=kk == 1)
                last.then_inc(scores_done, 1)

            def head_outputs(h):
                pe.wait_ge(sct_ready, h + 1)
                pe.wait_ge(ret_act, 2 * (h + 1))
                if h:
                    pe.wait_ge(onorm_done, h)
                v0, v1 = (rv[:, c, 512 * h:512 * h + 512] for c in range(NCH))
                mm(bank[6][:], sc_t[:, 0:P], v0, start=True, stop=True)
                mm(bank[7][:], sc_t[:, P:256], v0, start=True, stop=False)
                mm(bank[7][:], sc_t[:, 256:384], v1, start=False, stop=True).then_inc(o_done, 1)

            first_block(2, W_RET_IN, BLOCK_BANKS[0])
            for b in range(1, 12):
                if 2 <= b < 6:
                    pe.wait_ge(rope_done, 2 * (b - 1))
                elif b >= 6:
                    pe.wait_ge(ret_act, 2 * (b - 5))
                if 7 <= b <= 10:
                    scores(b - 7)
                for half in range(2):
                    w = W_RET_IN + 2 * b + half
                    unit_here(w)
                    in_unit(w, half, BLOCK_BANKS[b % 2], NCH)
                    if half == 0 and b % 2 == 0 and b:
                        ada_sum(16 + b // 2 - 1)
                if 1 <= b <= 4:
                    qk_transposes(b - 1)
                if 7 <= b <= 10:
                    head_outputs(b - 7)
            ada_sum(21)
            pe.wait_ge(ret_act, 16)
            down_phase(W_RET_OUT, T_RET, rv, og_done, onorm_done, {1: 22, 3: 23})

            for c in range(NCH):
                norm_transposes(3, c)
                pe.wait_ge(val_ready, 12 + 2 * c + 2)
                pe.wait_ge(s_wr, 32)
                for kt in range(KT):
                    last = mm(bank[c][:, 0:NE], val_t[:, kt, P * c:P * c + P], wr[:, kt, :],
                              start=kt == 0, stop=kt == KT - 1)
                last.then_inc(router_done, 1)
            pe.wait_ge(mod_ready, 24)
            pe.wait_ge(sel_ready, 1)
            b3 = bank[ADA_BANK]
            mm(b3[:, 0:8], utri, m_sel[:, 0, :], start=True, stop=True)
            mm(b3[:, 8:16], utri, m_sel[:, 1, :], start=True, stop=False)
            mm(b3[:, 8:16], ones, m_sel[:, 0, :], start=False, stop=True)
            mm(b3[:, 16:24], ones, m_sel[:, 0, :], start=True, stop=False)
            mm(b3[:, 16:24], ones, m_sel[:, 1, :], start=False, stop=True).then_inc(pos_done, 1)
            pe.wait_ge(slots_ready, 1)

            def gather(n):
                pe.wait_ge(pick_ready, n)
                for kt in range(KT):
                    for c in range(NCH):
                        last = mm(bank[6 + kt // 4][:, P * (kt % 4):P * (kt % 4) + P], tile_of(xn, c, kt),
                                  pick[:, c, :], start=c == 0, stop=c == NCH - 1)
                    if kt % 4 == 3:
                        last.then_inc(gathered, 1)

            def scatter(c, b):
                for half in range(2):
                    cols = slice(512 * half, 512 * half + 512)
                    mm(bank[b + half][:], pick_t[:, c, :], y_hi[:, cols], start=True, stop=False)
                    last = mm(bank[b + half][:], pick_t[:, c, :], y_lo[:, cols], start=False, stop=True)
                last.then_inc(scattered, 1)

            def expert(units, steps, one, turn):
                for u, kind, s in FFN_ORDER:
                    w = W_MOE + u
                    if u < 2:
                        pe.wait_ge(g_ready, turn * 2 + (u + 1))
                    if kind == "A":
                        pe.wait_ge(act_ready, steps + (STEPS + max(0, s - 1)))
                    if kind == "D":
                        pe.wait_ge(at_ready, steps + (T_DENSE + s + 1))
                        if s == STEPS - 2:
                            pe.wait_ge(act_ready, steps + (STEPS + STEPS))
                            ffn_transposes(s + 1, mact, 1)
                    pe.wait_ge(units_dve, units + (N_DENSE + u + 1))
                    if kind == "D":
                        down_unit(w, s % 2, s == 0, s == STEPS - 1, 1)
                    else:
                        in_unit(w, int(kind == "B"), (s % 2,), 1)
                    if kind == "B" and s:
                        pe.wait_ge(act_ready, steps + (STEPS + s))
                        pe.wait_ge(at_ready, steps + (T_DENSE + s - 1))
                        ffn_transposes(s - 1, mact, 1)
                    if u == 1:
                        pe.wait_ge(y_split, turn + 1)
                        pe.wait_ge(pick_t_ready, one + 1)
                        scatter(0, 6)
                    if u == 3:
                        pe.wait_ge(yacc_done, turn * NCH + 1)
                        scatter(1, 6)
                    if u == 5:
                        for c in range(NCH):
                            last = tr(bank[3][:, P * c:P * c + P], pick[:, c, :], ident)
                        last.then_inc(pick_tr, 1)
                    if u == 27:
                        pe.wait_ge(yacc_done, turn * NCH + 2)
                        gather(turn + 2)

            def last_scatter(n, picks):
                pe.wait_ge(y_split, n)
                pe.wait_ge(pick_t_ready, picks)
                pe.wait_ge(gval_ready, 2 * n)
                scatter(0, 6)
                scatter(1, 4)

            gather(1)
            with pe.Fori(0, NE) as e:
                expert(e * FU, e * STEPS, e, e)
            last_scatter(NE + 1, NE + 1)
            n_most = pe.value_load(most_i[0:1, 0:1], min_val=0, max_val=SEQ)
            with pe.If(n_most > P):
                pe.wait_ge(yacc_done, NCH * (NE + 1))
                gather(NE + 2)
                with pe.Fori(0, NE) as e:
                    expert(e * FU + NE * FU, e * STEPS + NE * STEPS, e + NE, e + NE + 1)
                last_scatter(2 * NE + 2, 2 * NE + 1)


def constants():
    i = np.arange(P)
    cst = np.stack([np.eye(P), np.ones((P, P)), np.tile(i, (P, 1)), i[:, None] < i[None, :]], axis=1)
    log_gamma = np.log1p(-np.exp2(-5.0 - np.arange(HEADS)))
    rel = (i[None, :] - i[:, None])[:, None, :]
    lg = log_gamma[None, :, None]
    intra = np.where(rel >= 0, np.exp(lg * np.maximum(rel, 0)), 0.0)
    cross = np.exp(lg * (P + rel))
    decay = np.concatenate([intra, cross], axis=2) * DK ** -0.5
    inv_freq = 1.0 / (np.float32(10000.0) ** (np.arange(0, DK, 2, dtype=np.float32) / np.float32(DK)))
    return {"consts": cst.reshape(P, 4 * P).astype(np.float32), "decay": decay.reshape(P, -1).astype(np.float32),
            "inv_freq": inv_freq.reshape(1, P).astype(np.float32)}


_INS = ["x", "c", "positions", "ada_w", "ada_b", "mix_norm_g", "ffn_norm_g", "sgu_w_in", "sgu_ln_g", "sgu_ln_b",
        "sgu_w_s", "sgu_b_s", "sgu_w_out", "ffn_w_gate_up", "ffn_w_down", "ret_w_in", "ret_w_out", "moe_w_router",
        "moe_b_router", "moe_w_gate_up", "moe_w_down", "final_norm_g"]


def kernel(**inputs):
    import concourse.bacc as _bacc
    from concourse.bass_utils import run_bass_kernel_spmd as _run

    nc = _bacc.Bacc("TRN2", target_bir_lowering=False, num_devices=1)
    arrays, t = {}, {}
    for name, a in [*((n, inputs[n]) for n in _INS), *constants().items()]:
        a = np.ascontiguousarray(a)
        arrays[f"in_{name}"] = a
        t[name] = nc.dram_tensor(f"in_{name}", a.shape, mybir.dt.from_np(a.dtype), kind="ExternalInput").ap()
    out = nc.dram_tensor("out", (1, SEQ, D_MODEL), mybir.dt.float32, kind="ExternalOutput").ap()
    trunk(nc, t, out)
    return _run(nc, [arrays], core_ids=[0]).results[0]["out"]
```
